# Optimizing a Trainium2 kernel written in Bass

```python
import jax, jax.numpy as jnp
from jax import lax
import numpy as np

D_MODEL = 1024
BATCH = 1
SEQ = 256
DEPTH = 2

CHUNK = 64
Q_BLOCK = 2 * CHUNK
N_META = 16

HEAD_DIM = 64
ATT_W = D_MODEL // 2
ATT_HEADS = ATT_W // HEAD_DIM

CONV_W = D_MODEL // 4
CONV_K = 31

POOL_W = D_MODEL // 4
POOL_WINDOWS = (2, 4, 8, 16)
POOL_GROUPS = len(POOL_WINDOWS)
POOL_GROUP_W = POOL_W // POOL_GROUPS

N_BRANCH = 3
IN_W = 3 * ATT_W + ATT_HEADS + 2 * CONV_W + POOL_W + N_BRANCH * D_MODEL

D_FF = ((8 * D_MODEL // 3 + 127) // 128) * 128
N_EXPERTS = 8
TOP_K = 2
D_FF_EXPERT = 7 * D_MODEL // 2
N_DENSE = (DEPTH + 1) // 2
N_MOE = DEPTH // 2

NEG_INF = -1e30

kernel_name = "hybrid_fox_conformer_pool_moe_trunk"

def rms_norm(x, g, eps=1e-6):
    xf = x.astype(jnp.float32)
    y = xf * lax.rsqrt(jnp.mean(xf * xf, axis=-1, keepdims=True) + eps)
    return (y * g.astype(jnp.float32)).astype(x.dtype)

def layer_norm(x, g, b, eps=1e-5):
    xf = x.astype(jnp.float32)
    mu = jnp.mean(xf, axis=-1, keepdims=True)
    var = jnp.mean(jnp.square(xf - mu), axis=-1, keepdims=True)
    y = (xf - mu) * lax.rsqrt(var + eps)
    return (y * g.astype(jnp.float32) + b.astype(jnp.float32)).astype(x.dtype)

def swiglu(h, wg, wu, wd):
    return (jax.nn.silu(h @ wg) * (h @ wu)) @ wd

def forgetting_attention(q, k, v, F):
    B, H, L, hd = q.shape
    nb = -(-L // Q_BLOCK)
    Lp = nb * Q_BLOCK
    pad = Lp - L
    pad4 = ((0, 0), (0, 0), (0, pad), (0, 0))
    q, k, v = jnp.pad(q, pad4), jnp.pad(k, pad4), jnp.pad(v, pad4)
    F = jnp.pad(F, ((0, 0), (0, 0), (0, pad)))
    qb = q.reshape(B, H, nb, Q_BLOCK, hd).transpose(2, 0, 1, 3, 4)
    Fb = F.reshape(B, H, nb, Q_BLOCK).transpose(2, 0, 1, 3)
    kpos = jnp.arange(Lp)
    scale = HEAD_DIM ** -0.5

    def block(args):
        qi, Fi, i = args
        s = jnp.einsum('bhqd,bhkd->bhqk', qi, k, preferred_element_type=jnp.float32) * scale
        s = s + Fi[..., None] - F[:, :, None, :]
        qpos = i * Q_BLOCK + jnp.arange(Q_BLOCK)
        s = jnp.where(kpos[None, :] <= qpos[:, None], s, NEG_INF)
        p = jax.nn.softmax(s, axis=-1)
        return jnp.einsum('bhqk,bhkd->bhqd', p.astype(v.dtype), v)

    out = lax.map(block, (qb, Fb, jnp.arange(nb)))
    return out.transpose(1, 2, 0, 3, 4).reshape(B, H, Lp, hd)[:, :, :L]

def causal_depthwise_conv(u, w, b):
    y = lax.conv_general_dilated(
        u, w[:, None, :].astype(u.dtype), window_strides=(1,), padding=[(CONV_K - 1, 0)],
        dimension_numbers=('NWC', 'WIO', 'NWC'), feature_group_count=u.shape[-1])
    return y + b

def causal_multiscale_pool(p):
    B, L, C = p.shape
    cs = lax.cumsum(p.astype(jnp.float32), axis=1)
    cs0 = jnp.pad(cs, ((0, 0), (1, 0), (0, 0)))
    t = jnp.arange(L)
    outs = []
    for g, w in enumerate(POOL_WINDOWS):
        c = cs0[:, :, g * POOL_GROUP_W:(g + 1) * POOL_GROUP_W]
        upper = c[:, 1:]
        lower = jnp.pad(c[:, :L + 1 - w], ((0, 0), (w - 1, 0), (0, 0)))
        cnt = jnp.minimum(t + 1, w).astype(jnp.float32)
        outs.append((upper - lower) / cnt[None, :, None])
    return jnp.concatenate(outs, axis=-1).astype(p.dtype)

def mixer_block(hn, w_in, b_in, q_norm, k_norm, w_attn_o, conv_w, conv_b, conv_ln_g, conv_ln_b,
                w_conv_o, pool_w, pool_scale, w_pool_o, w_out):
    B, L, _ = hn.shape
    z = hn @ w_in + b_in
    sizes = [ATT_W, ATT_W, ATT_W, ATT_HEADS, 2 * CONV_W, POOL_W, N_BRANCH * D_MODEL]
    q, k, v, fgl, conv_in, pool_in, gate = jnp.split(z, np.cumsum(sizes)[:-1].tolist(), axis=-1)

    q = rms_norm(q.reshape(B, L, ATT_HEADS, HEAD_DIM), q_norm).transpose(0, 2, 1, 3)
    k = rms_norm(k.reshape(B, L, ATT_HEADS, HEAD_DIM), k_norm).transpose(0, 2, 1, 3)
    v = v.reshape(B, L, ATT_HEADS, HEAD_DIM).transpose(0, 2, 1, 3)
    F = lax.cumsum(jax.nn.log_sigmoid(fgl.astype(jnp.float32)), axis=1).transpose(0, 2, 1)
    att = forgetting_attention(q, k, v, F).transpose(0, 2, 1, 3).reshape(B, L, ATT_W)
    y_att = att @ w_attn_o

    a, g = jnp.split(conv_in, 2, axis=-1)
    u = a * jax.nn.sigmoid(g)
    u = causal_depthwise_conv(u, conv_w, conv_b)
    u = jax.nn.silu(layer_norm(u, conv_ln_g, conv_ln_b))
    y_conv = u @ w_conv_o

    pm = causal_multiscale_pool(pool_in) - pool_in
    pm = jnp.einsum('blgc,gcd->blgd', pm.reshape(B, L, POOL_GROUPS, POOL_GROUP_W), pool_w)
    pm = pm.reshape(B, L, POOL_W) * pool_scale
    y_pool = pm @ w_pool_o

    gts = jax.nn.sigmoid(gate).reshape(B, L, N_BRANCH, D_MODEL)
    m = gts[:, :, 0] * y_att + gts[:, :, 1] * y_conv + gts[:, :, 2] * y_pool
    return m @ w_out

def moe_swiglu(h, w_router, b_router, w_e_gate, w_e_up, w_e_down):
    B, L, D = h.shape
    hf = h.reshape(B * L, D)
    logits = (hf @ w_router).astype(jnp.float32) + b_router.astype(jnp.float32)
    top_v, top_i = lax.top_k(logits, TOP_K)
    gates = jax.nn.softmax(top_v, axis=-1)
    combine = jnp.sum(jax.nn.one_hot(top_i, N_EXPERTS, dtype=jnp.float32) * gates[..., None], axis=1)
    out = jnp.zeros((B * L, D), jnp.float32)
    for e in range(N_EXPERTS):
        y = swiglu(hf, w_e_gate[e], w_e_up[e], w_e_down[e])
        out = out + combine[:, e:e + 1] * y.astype(jnp.float32)
    return out.astype(h.dtype).reshape(B, L, D)

def setup_inputs(seed: int = 0) -> dict:
    key = jax.random.key(seed)
    ks = iter(jax.random.split(key, 32))
    nrm = lambda shape, s: jax.random.normal(next(ks), shape, jnp.float32) * s
    gain = lambda shape: 1.0 + nrm(shape, 0.02)
    return {
        "x": nrm((BATCH, SEQ, D_MODEL), 1.0),
        "meta": nrm((N_META, D_MODEL), 1.0),
        "norm_mix": gain((DEPTH, D_MODEL)),
        "w_in": nrm((DEPTH, D_MODEL, IN_W), D_MODEL ** -0.5),
        "b_in": nrm((DEPTH, IN_W), 0.02),
        "q_norm": gain((DEPTH, HEAD_DIM)),
        "k_norm": gain((DEPTH, HEAD_DIM)),
        "w_attn_o": nrm((DEPTH, ATT_W, D_MODEL), ATT_W ** -0.5),
        "conv_w": nrm((DEPTH, CONV_K, CONV_W), CONV_K ** -0.5),
        "conv_b": nrm((DEPTH, CONV_W), 0.02),
        "conv_ln_g": gain((DEPTH, CONV_W)),
        "conv_ln_b": nrm((DEPTH, CONV_W), 0.02),
        "w_conv_o": nrm((DEPTH, CONV_W, D_MODEL), CONV_W ** -0.5),
        "pool_w": nrm((DEPTH, POOL_GROUPS, POOL_GROUP_W, POOL_GROUP_W), POOL_GROUP_W ** -0.5),
        "pool_scale": gain((DEPTH, POOL_W)),
        "w_pool_o": nrm((DEPTH, POOL_W, D_MODEL), POOL_W ** -0.5),
        "w_out": nrm((DEPTH, D_MODEL, D_MODEL), D_MODEL ** -0.5),
        "norm_ffn": gain((DEPTH, D_MODEL)),
        "w_ff_gate": nrm((N_DENSE, D_MODEL, D_FF), D_MODEL ** -0.5),
        "w_ff_up": nrm((N_DENSE, D_MODEL, D_FF), D_MODEL ** -0.5),
        "w_ff_down": nrm((N_DENSE, D_FF, D_MODEL), D_FF ** -0.5),
        "w_router": nrm((N_MOE, D_MODEL, N_EXPERTS), D_MODEL ** -0.5),
        "b_router": nrm((N_MOE, N_EXPERTS), 0.01),
        "w_e_gate": nrm((N_MOE, N_EXPERTS, D_MODEL, D_FF_EXPERT), D_MODEL ** -0.5),
        "w_e_up": nrm((N_MOE, N_EXPERTS, D_MODEL, D_FF_EXPERT), D_MODEL ** -0.5),
        "w_e_down": nrm((N_MOE, N_EXPERTS, D_FF_EXPERT, D_MODEL), D_FF_EXPERT ** -0.5),
    }

def reference(x, meta, norm_mix, w_in, b_in, q_norm, k_norm, w_attn_o, conv_w, conv_b, conv_ln_g,
              conv_ln_b, w_conv_o, pool_w, pool_scale, w_pool_o, w_out, norm_ffn, w_ff_gate, w_ff_up,
              w_ff_down, w_router, b_router, w_e_gate, w_e_up, w_e_down):
    B = x.shape[0]
    h = jnp.concatenate([jnp.broadcast_to(meta[None].astype(x.dtype), (B, N_META, D_MODEL)), x], axis=1)
    for l in range(DEPTH):
        hn = rms_norm(h, norm_mix[l])
        h = h + mixer_block(hn, w_in[l], b_in[l], q_norm[l], k_norm[l], w_attn_o[l], conv_w[l], conv_b[l],
                            conv_ln_g[l], conv_ln_b[l], w_conv_o[l], pool_w[l], pool_scale[l], w_pool_o[l],
                            w_out[l])
        hn = rms_norm(h, norm_ffn[l])
        if l % 2 == 0:
            i = l // 2
            h = h + swiglu(hn, w_ff_gate[i], w_ff_up[i], w_ff_down[i])
        else:
            i = l // 2
            h = h + moe_swiglu(hn, w_router[i], b_router[i], w_e_gate[i], w_e_up[i], w_e_down[i])
    return h[:, N_META:]


_drawn_inputs = setup_inputs


def setup_inputs(seed=0):
    import zlib

    import numpy as np

    out = dict(_drawn_inputs(seed))
    spreads = {}
    factors = {'q_norm': 4.259,
     'k_norm': 3.847,
     'pool_scale': 2.718,
     'conv_b': 3.209,
     'conv_ln_g': 3.131,
     'conv_ln_b': 4.129,
     'b_router': 2.857}
    for name, (base, spread) in spreads.items():
        noise = np.random.default_rng([zlib.crc32(name.encode()), seed]).standard_normal(out[name].shape)
        drawn = base * np.exp(spread * noise) if base else spread * noise
        out[name] = __import__('jax').numpy.asarray(drawn.astype(out[name].dtype))
    for name, factor in factors.items():
        out[name] = (out[name] * factor).astype(out[name].dtype)
    return out
```

```python
from contextlib import ExitStack

import numpy as np

import concourse.bass as bass
from concourse import mybir

ALU = mybir.AluOpType
ACT = mybir.ActivationFunctionType
F32 = mybir.dt.float32
I32 = mybir.dt.int32
U32 = mybir.dt.uint32
AX_X = mybir.AxisListType.X

P = 128
BANK = 512
BANKS = 8


def trunk_program(nc, x, meta, norm_mix, w_in, b_in, q_norm, k_norm, w_attn_o, conv_w, conv_b, conv_ln_g,
                  conv_ln_b, w_conv_o, pool_w, pool_scale, w_pool_o, w_out, norm_ffn, w_ff_gate, w_ff_up,
                  w_ff_down, w_router, b_router, w_e_gate, w_e_up, w_e_down, out):
    _, SEQ, D = x.shape
    META = meta.shape[0]
    DEPTH, _, IN_W = w_in.shape
    HD = q_norm.shape[1]
    ATT_W = w_attn_o.shape[1]
    HEADS = ATT_W // HD
    TAPS, CONV_W = conv_w.shape[1:]
    GROUPS, GW = pool_w.shape[1:3]
    POOL_W = GROUPS * GW
    D_FF = w_ff_gate.shape[2]
    EXPERTS, D_FE = w_e_gate.shape[1], w_e_gate.shape[3]
    L = META + SEQ
    assert DEPTH == 2 and SEQ == 2 * P and META == 16 and 2 * HD == P and 2 * GW == P

    KD = D // P
    QT = ATT_W // P
    CT = CONV_W // P
    PT_ = POOL_W // P
    GT = 3 * KD
    FT = D_FF // P
    ET = D_FE // P
    COL_F = 3 * ATT_W
    COL_CONV = COL_F + HEADS
    COL_POOL = COL_CONV + 2 * CONV_W
    COL_GATE = COL_POOL + POOL_W
    PAD_C = TAPS - 1
    PAD_P = 16
    EPS_RMS, EPS_LN = 1e-6, 1e-5
    NEG = -1e30
    TOK = [(0, META), (META, P), (META + P, P)]
    S_COL = {2: (0, L), 1: (L, META + P), 0: (L + META + P, META)}
    SW = L + META + P + META
    WIDTHS = (128, 144, 160, 256)
    SLOTS = SEQ
    assert WIDTHS[-1] == SLOTS

    BW = 4096
    blocks = []
    for l in range(DEPTH):
        def cols(w, c0, n):
            return w[:, c0:c0 + n].rearrange("(k p) n -> p k n", p=P), w.shape[0] // P, n
        blocks.append((("conv", l), *cols(w_in[l], COL_CONV, 2 * CONV_W)))
        blocks.append((("pool", l), *cols(w_in[l], COL_POOL, POOL_W)))
        for i, part in enumerate("qkv"):
            blocks.append(((part, l), *cols(w_in[l], i * ATT_W, ATT_W)))
        for i in range(GT // 4):
            blocks.append((("gate", l, i), *cols(w_in[l], COL_GATE + i * 4 * P, 4 * P)))
        blocks.append((("attn_o", l), *cols(w_attn_o[l], 0, D)))
        blocks.append((("conv_o", l), *cols(w_conv_o[l], 0, D)))
        blocks.append((("pool_o", l), *cols(w_pool_o[l], 0, D)))
        for i in range(2):
            blocks.append((("out", l, i), *cols(w_out[l], i * D // 2, D // 2)))
        if l == 0:
            for i in range(0, FT, 4):
                n = min(4, FT - i) * P
                blocks.append((("ff_gate", i // 4), *cols(w_ff_gate[0], i * P, n)))
                blocks.append((("ff_up", i // 4), *cols(w_ff_up[0], i * P, n)))
            for half in range(2):
                for k in range(0, FT, 8):
                    n = min(8, FT - k)
                    blocks.append((("ff_down", half, k // 8), *cols(w_ff_down[0][k * P:(k + n) * P, :], half * D // 2, D // 2)))
    RING = 5
    ERING = 7
    index = {b[0]: n for n, b in enumerate(blocks)}
    NB = len(blocks)
    FB = ET // 4
    EB = 3 * FB
    assert EB % ERING == 0
    ESEQ = [("g", 0), ("u", 0)]
    for i in range(1, FB):
        ESEQ += [("g", i), ("u", i), ("d", i - 1)]
    ESEQ.append(("d", FB - 1))
    epos = {b: n for n, b in enumerate(ESEQ)}

    order = []
    GATES_F, GATES_H = 5, GT - 2 * HEADS
    for kt in range(KD):
        order.append(("x", kt))
    for l in range(DEPTH):
        order += [("norm", l)] + ([("param", 0), ("param", 1)] if l == 0 else [])
        order += [("conv", l, i) for i in range(2 * CT)] + [("pool", l, i) for i in range(PT_)]
        order += [("q", l, i) for i in range(QT)] + [("k", l, i) for i in range(QT)]
        order += [("mean", l)] + ([("param", 2), ("param", 3)] if l == 0 else [])
        order += [("v", l, i) for i in range(QT)]
        order += [("var", l)] + [("mix", l, i) for i in range(PT_)]
        order += [("qk_ms", l, i) for i in range(2 * QT)]
        order += [("fg", l)] + [("vtok", l, j) for j in range(3)]
        order += [("gate", l, g) for g in range(GATES_F)]
        order += [("ftok", l), ("frow", l)] + [("gate", l, GATES_F)]
        order += [("fbc", l, h) for h in range(HEADS)]
        order += [("gate", l, g) for g in range(GATES_F + 1, GATES_H)]
        for h in range(HEADS):
            order += [("s", l, h), ("gate", l, GATES_H + 2 * h)]
            order += [("pv", l, h - 1)] if h else []
            order += [("gate", l, GATES_H + 2 * h + 1), ("pt", l, h), ("ptm", l, h)]
        order += [("pv", l, HEADS - 1)]
        for d in range(KD):
            order += [("ya", l, d), ("yc", l, d), ("yp", l, d)]
        order += [("out", l, d) for d in range(KD)]
        if l == 0:
            order += [("norm", "ffn")]
            for f in range(FT):
                order += [("ffg", f), ("ffu", f)]
            order += [("ffd", d) for d in range(KD)]
    order += [("htok", n) for n in range(4)] + [("logit",), ("pos",)]
    unit = {name: n for n, name in enumerate(order)}
    NU = len(order)
    U_PG, U_H, U_Y, U_O = 4, 5, 5 + ET, 9 + ET
    EU = U_O + 4

    ctx = ExitStack()
    with ctx:
        def sb(name, shape, dt=F32):
            return ctx.enter_context(nc.sbuf_tensor(name, shape, dt))

        def sem(name):
            return ctx.enter_context(nc.semaphore(name))

        psum = [ctx.enter_context(nc.psum_tensor(f"bank{i}", [P, BANK], F32)) for i in range(BANKS)]

        ring = sb("ring", [P, RING, BW])
        spare = sb("spare", [P, 2 * BW])
        gates = spare[:, 0:GT * L].rearrange("p (b d t) -> p b d t", b=3, d=KD)
        hidden = spare[:, 0:FT * L].rearrange("p (f t) -> p f t", f=FT)
        xload = spare[:, 0:2 * D].rearrange("p (j n) -> p j n", j=2)
        mload = spare[0:META, 2 * D:3 * D]
        hT = sb("hT", [P, KD, L])
        hn = sb("hn", [P, KD, L])
        qkT = sb("qkT", [P, 2 * QT, L])
        mT = qkT
        vT = sb("vT", [P, QT, L])
        fbm = sb("fbm", [P, HEADS, SW])
        sq = fbm[:, :, 0:L]
        conv_buf = sb("conv_buf", [P, 4 * CT, L])
        conv_in = conv_buf[:, 0:2 * CT, :]
        cy = conv_buf[:, 2 * CT:3 * CT, :]
        csq = conv_buf[:, 3 * CT:4 * CT, :]
        upad = sb("upad", [P, CT, PAD_C + L])
        ppad = sb("ppad", [P, PT_, PAD_P + L])
        poolo = sb("poolo", [P, PT_, L])
        att_buf = sb("att_buf", [P, QT * L + 3 * ATT_W])
        attT = att_buf[:, 0:QT * L].rearrange("p (i t) -> p i t", i=QT)
        vtok_flat = att_buf[:, QT * L:QT * L + 3 * ATT_W]
        vtok = vtok_flat.rearrange("p (j n) -> p j n", j=3)
        WP = PT_ * (PAD_P + L)
        psa = vtok_flat[:, 0:WP].rearrange("p (c t) -> p c t", c=PT_)
        psb = vtok_flat[:, WP:2 * WP].rearrange("p (c t) -> p c t", c=PT_)
        sc = sb("sc", [P, 2, SW])
        pt = sb("pt", [P, 3 * P])
        ptm = sb("ptm", [META, L])
        rms = sb("rms", [P, 2, L])
        rstd = sb("rstd", [P, 2, L])
        silu = sb("silu", [P, 2, L])
        silu_flat = silu[:, :, :].rearrange("p a t -> p (a t)")
        ident = sb("ident", [P, P])
        ones = sb("ones", [P, P])
        mean_ones = sb("mean_ones", [P, P])
        head_ones = sb("head_ones", [P, P])
        tri = sb("tri", [P, 3, L])
        strict = tri[:, 1, META - 1:META - 1 + P]
        iota_i = rms[:, :, :].rearrange("p a t -> p (a t)")[:, 0:SLOTS].bitcast(I32)
        iota_f = sb("iota_f", [P, SLOTS])
        rcnt = sb("rcnt", [P, PT_, PAD_P])
        NA = 2 * KD + 3 * QT + 2 * CT + PT_ + GT + 3 * CT + PT_ + 2
        NT = TAPS * CT
        rows = silu_flat[:, 0:2 * DEPTH * P].rearrange("p (r n) -> p r n", n=P)
        par = sb("par", [P, 2 * DEPTH, P])
        bf_bc = sb("bf_bc", [P, DEPTH, HEADS])
        wf = sb("wf", [P, DEPTH, KD, HEADS])
        pw = sb("pw", [P, DEPTH, PT_, P])
        wr = sb("wr", [P, KD, EXPERTS])
        wrg = sb("wrg", [P, KD, EXPERTS])
        br_bc = sb("br_bc", [P, EXPERTS])
        fg = sb("fg", [P, 3 * HEADS])
        fga = sb("fga", [P, 3 * HEADS])
        fge = sb("fge", [P, 3 * HEADS])
        fgl = sb("fgl", [P, 3 * HEADS])
        ls = sb("ls", [P, 3 * HEADS])
        ftok = sb("ftok", [P, 3 * HEADS])
        frow = sb("frow", [HEADS, L])
        qgain = sb("qgain", [P, 2])
        nmax = sb("nmax", [P, 2, 3])
        rsum = sb("rsum", [P, 2, 3])
        rinv = sb("rinv", [P, 2, 3])

        def flat(t):
            return t[:, :, :].rearrange("p a t -> p (a t)")

        hacc = att_buf[:, 0:2 * D].rearrange("p (j n) -> p j n", j=2)
        xs = flat(qkT)[:, 0:2 * D].rearrange("p (j n) -> p j n", j=2)
        gbc = flat(vT)[:, 0:D]
        xg = hn[:, :, 0:SLOTS]
        fbm_flat = flat(fbm)
        yT = fbm_flat[:, 0:KD * SLOTS].rearrange("p (d s) -> p d s", d=KD)
        psel = fbm_flat[:, KD * SLOTS:(KD + 2) * SLOTS].rearrange("p (j s) -> p j s", j=2)
        pgat = fbm_flat[:, (KD + 2) * SLOTS:(KD + 4) * SLOTS].rearrange("p (j s) -> p j s", j=2)
        ytok = flat(hT)[:, 0:2 * D].rearrange("p (s n) -> p s n", s=2)
        act = flat(conv_buf)[:, 0:8 * SLOTS].rearrange("p (b f s) -> p b f s", b=2, f=4)
        pgT = flat(tri)[:, 0:2 * SEQ].rearrange("p (s t) -> p s t", s=2)
        esilu = silu_flat[:, 0:2 * SLOTS].rearrange("p (b s) -> p b s", b=2)
        tok_sq = fbm_flat[:, 0:D]
        small = {n: sb(n, [P, 2]) for n in ("ss", "sms", "srt", "srs", "gap", "pexp", "pden", "pr0", "pr1")}
        ss, sms, srt, srs, gap, pexp, pden, pr0, pr1 = (small[n] for n in small)
        lg = sb("lg", [P, 2, 8])
        mx = sb("mx", [P, 2, 8])
        mi = sb("mi", [P, 2, 8], U32)
        mif = sb("mif", [P, 2, 8])
        oh0 = sb("oh0", [P, 2, EXPERTS])
        oh1 = sb("oh1", [P, 2, EXPERTS])
        comb = sb("comb", [P, 2, 2 * EXPERTS])
        mask = sb("mask", [P, 2, 2 * EXPERTS])
        pos = sb("pos", [P, 2, 2 * EXPERTS])
        count = sb("count", [P, EXPERTS], I32)

        s_x = sem("x_loaded")
        s_par = [sem(f"params_loaded{l}") for l in range(DEPTH)]
        s_out = sem("out_written")
        s_gbc = sem("ffn_gain_loaded")
        slot_full = [sem(f"slot_full{i}") for i in range(ERING)]
        psum_ready = sem("psum_ready")
        taken = sem("units_taken")
        down_used = sem("down_block_used")
        zeroed = sem("psum_zeroed")
        pw_zeroed = sem("pool_blocks_zeroed")
        rcnt_ready = sem("window_counts_ready")
        consts = sem("consts_built")
        pool_step = sem("pool_step")
        dve_step = sem("dve_step")
        act_step = sem("act_step")
        sq_ready = sem("squares_ready")
        root_ready = sem("root_ready")
        hn_ready = sem("normed_ready")
        glu_gate = sem("glu_gate")
        conv_done = sem("conv_done")
        centred_sq = sem("centred_sq")
        ln_root = sem("ln_root")
        ln_scaled = sem("ln_scaled")
        conv_act = sem("conv_act")
        pool_mix = sem("pool_mix")
        qk_sq = sem("qk_sq")
        qk_root = sem("qk_root")
        qk_ready = sem("qk_ready")
        fg_log = sem("forget_log")
        ls_ready = sem("log_sigmoid_ready")
        fbm_ready = sem("decay_masked")
        max_ready = sem("max_ready")
        exp_ready = sem("exp_ready")
        rinv_ready = sem("rinv_ready")
        probs_ready = sem("probs_ready")
        gate_ready = sem("gate_ready")
        m_ready = sem("mixed_ready")
        silu_ready = sem("silu_ready")
        ss_ready = sem("token_square_ready")
        sms_ready = sem("token_ms_ready")
        srt_ready = sem("token_root_ready")
        xs_ready = sem("tokens_normed")
        wrg_ready = sem("router_ready")
        gap_ready = sem("top_gap_ready")
        pexp_ready = sem("top_exp_ready")
        mask_ready = sem("mask_ready")
        routed = sem("routed")
        comb_ready = sem("combine_ready")
        sel_ready = sem("selection_ready")
        e_full = sem("expert_unit_ready")
        e_taken = sem("expert_units_taken")
        e_down_used = sem("expert_down_used")
        e_silu = sem("expert_silu_ready")
        y_ready = sem("expert_out_ready")
        yT_ready = sem("expert_out_copied")

        N_PAR = [15 + 4, 15 + 4 + 2]

        def tokens_of(l):
            return 0 if l == 0 else META

        def eslot(b, k):
            i = b % ERING
            flat_slot = ring[:, i, :] if i < RING else spare[:, (i - RING) * BW:(i - RING + 1) * BW]
            return flat_slot.rearrange("p (k n) -> p k n", k=k)

        def block_ap(name):
            _, _, k, n = blocks[index[name]]
            return ring[:, index[name] % RING, 0:k * n].rearrange("p (k n) -> p k n", k=k)

        C_MIX, C_FFN = 0, KD
        C_Q = 2 * KD
        C_K = C_Q + QT
        C_V = C_K + QT
        C_CONV = C_V + QT
        C_POOL = C_CONV + 2 * CT
        C_GATE = C_POOL + PT_
        C_CB = C_GATE + GT
        C_LG = C_CB + CT
        C_LB = C_LG + CT
        C_PS = C_LB + CT
        C_QN = C_PS + PT_
        C_KN = C_QN + 1
        assert C_KN + 1 == NA <= P and NT <= P

        def pcol(l, c):
            return par[:, 2 * l, c:c + 1]

        def tap(l, t, c):
            return par[:, 2 * l + 1, CT * t + c:CT * t + c + 1]



        last_unit = {}
        down_used_at = {}
        for l in range(DEPTH):
            last_unit["conv", l] = ("conv", l, 2 * CT - 1)
            last_unit["pool", l] = ("pool", l, PT_ - 1)
            for part in "qkv":
                last_unit[part, l] = (part, l, QT - 1)
            for i in range(GT // 4):
                last_unit["gate", l, i] = ("gate", l, 4 * i + 3)
            last_unit["attn_o", l] = ("ya", l, KD - 1)
            last_unit["conv_o", l] = ("yc", l, KD - 1)
            last_unit["pool_o", l] = ("yp", l, KD - 1)
            for i in range(2):
                last_unit["out", l, i] = ("out", l, 4 * i + 3)
        for i in range(0, FT, 4):
            last_unit["ff_gate", i // 4] = ("ffg", min(i + 3, FT - 1))
            last_unit["ff_up", i // 4] = ("ffu", min(i + 3, FT - 1))
        KB = (FT + 7) // 8
        for half in range(2):
            last_unit["ff_down", half, KB - 1] = ("ffd", 4 * half + 3)
            for k in range(KB - 1):
                down_used_at["ff_down", half, k] = half * (KB - 1) + k + 1

        def wait_used(eng, n):
            name = blocks[n][0]
            if name in down_used_at:
                eng.wait_ge(down_used, down_used_at[name])
            else:
                eng.wait_ge(psum_ready, unit[last_unit[name]] + 1)

        last_in_slot = {s: max(n for n in range(NB) if n % RING == s) for s in range(RING)}
        used_before = {s: sum(n % RING == s for n in range(NB)) for s in range(RING)}
        used_before.update({s: 0 for s in range(RING, ERING)})

        def free_unit(eng, name):
            n = unit[name]
            if n >= BANKS:
                eng.wait_ge(taken, n - BANKS + 1)
            return psum[n % BANKS]

        def ready_unit(eng, name):
            eng.wait_ge(psum_ready, unit[name] + 1)
            return psum[unit[name] % BANKS]

        def wait_taken(eng, name):
            eng.wait_ge(taken, unit[name] + 1)

        def wait_etaken(eng, e, u):
            eng.wait_ge(e_taken, e * EU + (u + 2))

        def residual(n, kt):
            return (("x", kt), ("out", 0, kt), ("ffd", kt), ("out", 1, kt))[n]

        def score_tiles(l):
            return (2, 1, 0) if l == 0 else (2, 1)

        def scored(l, h, n):
            return sum(len(score_tiles(i)) * HEADS for i in range(l)) + len(score_tiles(l)) * h + n

        class Steps:

            def __init__(self, eng, semaphore):
                self.eng, self.semaphore, self.n = eng, semaphore, 0

            def did(self, instruction):
                self.n += 1
                instruction.then_inc(self.semaphore, 1)
                return self.n

            def settle(self, n=None):
                self.eng.wait_ge(self.semaphore, self.n if n is None else n)

        def load_params(eng, l):
            r = rows[:, 2 * l, :]
            for at, src in ((C_MIX, norm_mix[l]), (C_FFN, norm_ffn[l]), (C_Q, b_in[l, 0:COL_F]),
                            (C_CONV, b_in[l, COL_CONV:IN_W]), (C_CB, conv_b[l]), (C_LG, conv_ln_g[l]),
                            (C_LB, conv_ln_b[l]), (C_PS, pool_scale[l])):
                v = src.rearrange("(r p) -> r p", p=P)
                eng.dma_start(r[at:at + v.shape[0], :], v).then_inc(s_par[l], 16)
            for at, src in ((C_QN, q_norm), (C_KN, k_norm)):
                for b in range(2):
                    eng.dma_start(r[at:at + 1, b * HD:(b + 1) * HD], src[l:l + 1, :]).then_inc(s_par[l], 16)
            eng.dma_start(rows[0:NT, 2 * l + 1, :], conv_w[l].rearrange("k (c p) -> (k c) p", p=P)).then_inc(s_par[l], 16)
            eng.dma_start(bf_bc[:, l, :], b_in[l:l + 1, COL_F:COL_CONV].broadcast_to([P, HEADS])).then_inc(s_par[l], 16)
            eng.dma_start(wf[:, l], w_in[l][:, COL_F:COL_CONV].rearrange("(k p) n -> p k n", p=P)).then_inc(s_par[l], 16)
            eng.wait_ge(pw_zeroed, 1)
            for g in range(GROUPS):
                b = GW * (g % 2)
                eng.dma_start(pw[b:b + GW, l, g // 2, b:b + GW], pool_w[l, g]).then_inc(s_par[l], 16)

        block = ctx.enter_context(nc.Block())

        @block.sync
        def _(sp):
            sp.dma_start(xload, x[0].rearrange("(j p) n -> p j n", p=P)).then_inc(s_x, 16)
            sp.dma_start(mload, meta).then_inc(s_x, 16)
            for n, (name, src, k, cols_) in enumerate(blocks):
                if n >= RING:
                    wait_used(sp, n - RING)
                dst = ring[:, n % RING, 0:k * cols_].rearrange("p (k n) -> p k n", k=k)
                sp.dma_start(dst, src).then_inc(slot_full[n % RING], 16)

            def expert_block(e, b):
                kind, i = ESEQ[b]
                if kind == "d":
                    src = w_e_down[0][bass.ds(e, 1), i * BANK:(i + 1) * BANK, :].rearrange("a (k p) n -> p (a k) n", p=P)
                else:
                    w = w_e_gate if kind == "g" else w_e_up
                    src = w[0][bass.ds(e, 1), :, i * BANK:(i + 1) * BANK].rearrange("a (k p) n -> p (a k) n", p=P)
                sp.dma_start(eslot(b, 4 if kind == "d" else KD), src).then_inc(slot_full[b % ERING], 16)

            def wait_expert_block(e, b):
                kind, i = ESEQ[b]
                if kind == "d" and i == FB - 1:
                    sp.wait_ge(y_ready, e * 4 + 4)
                elif kind == "d":
                    sp.wait_ge(e_down_used, e * (FB - 1) + (i + 1))
                else:
                    sp.wait_ge(e_full, e * EU + (U_H + 4 * i + 4))

            for b in range(ERING):
                if b < RING:
                    wait_used(sp, last_in_slot[b])
                else:
                    sp.wait_ge(m_ready, DEPTH * KD)
                expert_block(0, b)
            with sp.Fori(0, EXPERTS - 1) as e:
                for b in range(ERING, EB):
                    wait_expert_block(e, b - ERING)
                    expert_block(e, b)
                for b in range(ERING):
                    wait_expert_block(e, b + EB - ERING)
                    expert_block(e + 1, b)
            for b in range(ERING, EB):
                wait_expert_block(EXPERTS - 1, b - ERING)
                expert_block(EXPERTS - 1, b)
            for n, (j, half) in enumerate((j, half) for j in range(2) for half in range(2)):
                wait_etaken(sp, EXPERTS - 1, U_O + n)
                sp.dma_start(out[0, j * P:(j + 1) * P, half * BANK:(half + 1) * BANK],
                             hacc[:, j, half * BANK:(half + 1) * BANK]).then_inc(s_out, 16)
            sp.wait_ge(s_out, 4 * 16)

        @block.gpsimd
        def _(pool):
            steps = Steps(pool, pool_step)
            pool.memset(ident[:, :], 0.0).then_inc(consts, 1)
            pool.memset(ones[:, :], 1.0).then_inc(consts, 1)
            pool.memset(mean_ones[:, :], 1.0 / CONV_W).then_inc(consts, 1)
            pool.memset(tri[:, :, :], 1.0).then_inc(consts, 1)
            pool.memset(upad[:, :, 0:PAD_C], 0.0).then_inc(consts, 1)
            pool.memset(ppad[:, :, 0:PAD_P], 0.0).then_inc(consts, 1)
            pool.iota(iota_i, pattern=[[1, SLOTS]], base=0, channel_multiplier=0).then_inc(consts, 1)
            pool.wait_ge(consts, 7)
            pool.affine_select(out=ident[:, :], in_=ident[:, :], compare_op=ALU.not_equal, fill=1.0, base=0,
                               pattern=[[-1, P]], channel_multiplier=1).then_inc(consts, 1)
            for i, (t0, _) in enumerate(TOK):
                pool.affine_select(out=tri[:, i, :], in_=tri[:, i, :], compare_op=ALU.is_ge, fill=0.0, base=-t0,
                                   pattern=[[1, L]], channel_multiplier=-1).then_inc(consts, 1)
            pool.tensor_copy(iota_f[:, :], iota_i).then_inc(consts, 1)

            for l in range(1, DEPTH):
                load_params(pool, l)
            pool.dma_start(wr[:, :, :], w_router[0].rearrange("(k p) n -> p k n", p=P)).then_inc(s_par[1], 16)
            pool.dma_start(br_bc[:, :], b_router.broadcast_to([P, EXPERTS])).then_inc(s_par[1], 16)

            for l in range(DEPTH):
                if l > 0:
                    pool.wait_ge(psum_ready, unit["pv", l - 1, HEADS - 1] + 1)
                steps.did(pool.memset(psa[:, :, 0:PAD_P], 0.0))
                steps.did(pool.memset(psb[:, :, 0:PAD_P], 0.0))
                wait_taken(pool, ("pool", l, PT_ - 1))

                def shifted(dst, src, n, tiles):
                    steps.settle()
                    steps.did(pool.tensor_tensor(dst[:, tiles, PAD_P:], src[:, tiles, PAD_P:],
                                                 src[:, tiles, PAD_P - n:PAD_P + L - n], ALU.add))

                shifted(psa, ppad, 1, slice(0, 2))
                shifted(psb, psa, 2, slice(0, 2))
                shifted(psa, psb, 4, slice(1, 2))
                shifted(psb, psa, 8, slice(1, 2))
                for g in range(GROUPS):
                    b, c, w = GW * (g % 2), g // 2, 2 ** (g + 1)
                    total = (psa, psb)[g % 2]
                    steps.settle()
                    steps.did(pool.tensor_scalar(poolo[b:b + GW, c, PAD_P:], total[b:b + GW, c, 2 * PAD_P:], 1.0 / w, None, ALU.mult))
                    if l == 0 and g == 0:
                        pool.wait_ge(rcnt_ready, 1)
                    steps.did(pool.tensor_tensor(poolo[b:b + GW, c, 0:PAD_P], total[b:b + GW, c, PAD_P:2 * PAD_P],
                                                 rcnt[b:b + GW, c, :], ALU.mult))
                steps.settle()
                for c in range(PT_):
                    pool.tensor_tensor(poolo[:, c, :], poolo[:, c, :], ppad[:, c, PAD_P:], ALU.subtract).then_inc(pool_mix, 1)

                wait_taken(pool, ("fbc", l, HEADS - 1))
                steps.did(pool.tensor_copy(fbm[:, :, S_COL[1][0]:S_COL[1][0] + S_COL[1][1]], fbm[:, :, 0:S_COL[1][1]]))
                steps.settle()
                steps.did(pool.tensor_copy(fbm[0:META, :, S_COL[0][0]:S_COL[0][0] + META], fbm[0:META, :, 0:META]))
                steps.settle()
                for j, n in ((0, META), (1, P), (2, P)):
                    c0 = S_COL[j][0] + S_COL[j][1] - n
                    v = fbm[0:n, :, c0:c0 + n]
                    if j > 0:
                        pool.wait_ge(fbm_ready, 3 * l + j)
                    pool.affine_select(out=v, in_=v, compare_op=ALU.is_ge, fill=-NEG, base=0,
                                       pattern=[[0, HEADS], [-1, n]], channel_multiplier=1).then_inc(fbm_ready, 1)

                t0 = tokens_of(l)
                for d in range(KD):
                    wait_taken(pool, ("yp", l, d))
                    steps.did(pool.tensor_tensor(mT[:, d, t0:], gates[:, 0, d, t0:], gates[:, 1, d, t0:], ALU.add))
                    steps.settle()
                    pool.tensor_tensor(mT[:, d, t0:], mT[:, d, t0:], gates[:, 2, d, t0:], ALU.add).then_inc(m_ready, 1)

            pool.wait_ge(psum_ready, unit["pv", DEPTH - 1, HEADS - 1] + 1)
            pool.dma_start(gbc, norm_ffn[DEPTH - 1:DEPTH, :].broadcast_to([P, D])).then_inc(s_gbc, 16)

        @block.tensor
        def _(pe):
            def need(name):
                n = index[name]
                pe.wait_ge(slot_full[n % RING], 16 * (n // RING + 1))

            def project(name, w, c0, rhs, kts, t0=0, out_rows=P):
                bank = free_unit(pe, name)
                for kt in range(kts):
                    mm = nc.tensor.matmul(bank[0:out_rows, t0:L], w[:, kt, c0:c0 + P], rhs(kt), start=(kt == 0), stop=(kt == kts - 1))
                mm.then_inc(psum_ready, 1)

            def norm_sum(name, k):
                bank = free_unit(pe, name)
                for kt in range(KD):
                    pe.wait_ge(sq_ready, k * KD + kt + 1)
                    mm = nc.tensor.matmul(bank[:, 0:L], ones[:, :], sq[:, kt, :], start=(kt == 0), stop=(kt == KD - 1))
                mm.then_inc(psum_ready, 1)

            pe.wait_ge(consts, 12)
            pe.wait_ge(zeroed, BANKS + 3)
            pe.wait_ge(s_x, 32)
            for kt in range(KD):
                bank = free_unit(pe, ("x", kt))
                c = slice(kt * P, (kt + 1) * P)
                nc.tensor.transpose(bank[:, 0:META], mload[:, c], ident[0:META, 0:META])
                for j in range(2):
                    tr = nc.tensor.transpose(bank[:, TOK[j + 1][0]:TOK[j + 1][0] + P], xload[:, j, c], ident[:, :])
                tr.then_inc(psum_ready, 1)
            def turn_params(l):
                pe.wait_ge(s_par[l], 16 * N_PAR[l])
                for n, height in ((2 * l, NA), (2 * l + 1, NT)):
                    bank = free_unit(pe, ("param", n))
                    nc.tensor.transpose(bank[:, 0:height], rows[0:height, n, :], ident[0:height, 0:height]).then_inc(psum_ready, 1)


            for l in range(DEPTH):
                t0 = tokens_of(l)
                norm_sum(("norm", l), 2 * l)
                if l == 0:
                    turn_params(0)

                def normed(kt, c0=0):
                    return hn[:, kt, c0:]

                def wait_normed(kt):
                    pe.wait_ge(hn_ready, 2 * l * KD + kt + 1)
                    return hn[:, kt, :]

                need(("conv", l))
                w = block_ap(("conv", l))
                for i in range(2 * CT):
                    project(("conv", l, i), w, i * P, wait_normed if i == 0 else normed, KD)
                need(("pool", l))
                w = block_ap(("pool", l))
                for i in range(PT_):
                    project(("pool", l, i), w, i * P, normed, KD)
                for part in "qk":
                    need((part, l))
                    w = block_ap((part, l))
                    for i in range(QT):
                        project((part, l, i), w, i * P, normed, KD)
                bank = free_unit(pe, ("mean", l))
                for c in range(CT):
                    pe.wait_ge(conv_done, l * CT + c + 1)
                    mm = nc.tensor.matmul(bank[:, 0:L], mean_ones[:, :], cy[:, c, :], start=(c == 0), stop=(c == CT - 1))
                mm.then_inc(psum_ready, 1)
                if l == 0:
                    turn_params(1)
                need(("v", l))
                w = block_ap(("v", l))
                for i in range(QT):
                    project(("v", l, i), w, i * P, normed, KD)
                bank = free_unit(pe, ("var", l))
                for c in range(CT):
                    pe.wait_ge(centred_sq, l * CT + c + 1)
                    mm = nc.tensor.matmul(bank[:, 0:L], mean_ones[:, :], csq[:, c, :], start=(c == 0), stop=(c == CT - 1))
                mm.then_inc(psum_ready, 1)
                for c in range(PT_):
                    bank = free_unit(pe, ("mix", l, c))
                    pe.wait_ge(pool_mix, l * PT_ + c + 1)
                    nc.tensor.matmul(bank[:, 0:L], pw[:, l, c, :], poolo[:, c, :], start=True, stop=True).then_inc(psum_ready, 1)
                for i in range(2 * QT):
                    bank = free_unit(pe, ("qk_ms", l, i))
                    pe.wait_ge(qk_sq, l * 2 * QT + i + 1)
                    nc.tensor.matmul(bank[:, 0:L], head_ones[:, :], fbm[:, i, 0:L], start=True, stop=True).then_inc(psum_ready, 1)
                bank = free_unit(pe, ("fg", l))
                for j, (a, n) in enumerate(TOK):
                    for kt in range(KD):
                        mm = nc.tensor.matmul(bank[0:n, j * HEADS:(j + 1) * HEADS], hn[:, kt, a:a + n], wf[:, l, kt, :],
                                              start=(kt == 0), stop=(kt == KD - 1))
                mm.then_inc(psum_ready, 1)
                for j, (a, n) in enumerate(TOK):
                    bank = free_unit(pe, ("vtok", l, j))
                    wait_taken(pe, ("v", l, QT - 1))
                    for i in range(QT):
                        tr = nc.tensor.transpose(bank[0:n, i * P:(i + 1) * P], vT[:, i, a:a + n], ident[:, :])
                    tr.then_inc(psum_ready, 1)
                def gate_tile(g):
                    if g % 4 == 0:
                        need(("gate", l, g // 4))
                    project(("gate", l, g), block_ap(("gate", l, g // 4)), g % 4 * P, lambda kt: hn[:, kt, t0:], KD, t0)

                for g in range(GATES_F):
                    gate_tile(g)
                pe.wait_ge(ls_ready, l + 1)
                bank = free_unit(pe, ("ftok", l))
                for j, (a, n) in enumerate(TOK):
                    for i in range(j + 1):
                        m = TOK[i][1]
                        mm = nc.tensor.matmul(bank[0:n, j * HEADS:(j + 1) * HEADS], tri[0:m, i, a:a + n],
                                              ls[0:m, i * HEADS:(i + 1) * HEADS], start=(i == 0), stop=(i == j))
                mm.then_inc(psum_ready, 1)
                bank = free_unit(pe, ("frow", l))
                for i, (a, n) in enumerate(TOK):
                    mm = nc.tensor.matmul(bank[0:HEADS, 0:L], ls[0:n, i * HEADS:(i + 1) * HEADS], tri[0:n, i, :],
                                          start=(i == 0), stop=(i == 2))
                mm.then_inc(psum_ready, 1)
                gate_tile(GATES_F)
                for h in range(HEADS):
                    bank = free_unit(pe, ("fbc", l, h))
                    if h == 0:
                        wait_taken(pe, ("frow", l))
                    nc.tensor.matmul(bank[:, 0:L], ident[0:HEADS, h:h + 1].broadcast_to([HEADS, P]), frow[:, :],
                                     start=True, stop=True).then_inc(psum_ready, 1)

                for g in range(GATES_F + 1, GATES_H):
                    gate_tile(g)

                def scores(h):
                    b, i = HD * (h % 2), h // 2
                    bank = free_unit(pe, ("s", l, h))
                    if h == 0:
                        pe.wait_ge(qk_ready, (l + 1) * 2 * QT)
                    for j in score_tiles(l):
                        a, n = TOK[j]
                        c0, keys = S_COL[j]
                        mm = nc.tensor.matmul(bank[0:n, c0:c0 + keys], qkT[b:b + HD, i, a:a + n], qkT[b:b + HD, QT + i, 0:keys],
                                              start=True, stop=True)
                    mm.then_inc(psum_ready, 1)

                def turn_probs(h):
                    s = sc[:, h % 2, :]
                    c2, c1, c0 = S_COL[2][0], S_COL[1][0], S_COL[0][0]
                    bank = free_unit(pe, ("pt", l, h))
                    pe.wait_ge(probs_ready, scored(l, h + 1, 0))
                    nc.tensor.transpose(bank[:, 0:P], s[:, c1 + META:c1 + META + P], ident[:, :])
                    nc.tensor.transpose(bank[:, P:2 * P], s[:, c2 + META:c2 + META + P], ident[:, :])
                    nc.tensor.transpose(bank[:, 2 * P:3 * P], s[:, c2 + META + P:c2 + L], ident[:, :]).then_inc(psum_ready, 1)
                    bank = free_unit(pe, ("ptm", l, h))
                    if l == 0:
                        nc.tensor.transpose(bank[0:META, 0:META], s[0:META, c0:c0 + META], ident[0:META, 0:META])
                    nc.tensor.transpose(bank[0:META, META:META + P], s[:, c1:c1 + META], ident[:, :])
                    nc.tensor.transpose(bank[0:META, META + P:L], s[:, c2:c2 + META], ident[:, :]).then_inc(psum_ready, 1)

                def values(h):
                    b, c = HD * (h % 2), slice(h * HD, (h + 1) * HD)
                    bank = free_unit(pe, ("pv", l, h))
                    wait_taken(pe, ("ptm", l, h))
                    nc.tensor.matmul(bank[b:b + HD, t0:L], vtok[0:META, 0, c], ptm[:, t0:L], start=True, stop=False)
                    nc.tensor.matmul(bank[b:b + HD, META:L], vtok[:, 1, c], pt[:, 0:2 * P], start=False, stop=False)
                    nc.tensor.matmul(bank[b:b + HD, META + P:L], vtok[:, 2, c], pt[:, 2 * P:3 * P], start=False,
                                     stop=True).then_inc(psum_ready, 1)

                for h in range(HEADS):
                    scores(h)
                    gate_tile(GATES_H + 2 * h)
                    if h > 0:
                        values(h - 1)
                    gate_tile(GATES_H + 2 * h + 1)
                    turn_probs(h)
                values(HEADS - 1)

                for d in range(KD):
                    if d == 0:
                        need(("attn_o", l))
                        wait_taken(pe, ("pv", l, HEADS - 1))
                    project(("ya", l, d), block_ap(("attn_o", l)), d * P, lambda i: attT[:, i, t0:], QT, t0)
                    if d == 0:
                        need(("conv_o", l))
                        pe.wait_ge(conv_act, (l + 1) * CT)
                    project(("yc", l, d), block_ap(("conv_o", l)), d * P, lambda i: csq[:, i, t0:], CT, t0)
                    if d == 0:
                        need(("pool_o", l))
                    project(("yp", l, d), block_ap(("pool_o", l)), d * P, lambda i: poolo[:, i, t0:], PT_, t0)

                def mixed(kt):
                    pe.wait_ge(m_ready, l * KD + kt + 1)
                    return mT[:, kt, t0:]

                for d in range(KD):
                    if d % 4 == 0:
                        need(("out", l, d // 4))
                    project(("out", l, d), block_ap(("out", l, d // 4)), d % 4 * P,
                            mixed if d == 0 else lambda kt: mT[:, kt, t0:], KD, t0)

                if l == 0:
                    norm_sum(("norm", "ffn"), 1)

                    def ffn_normed(kt):
                        pe.wait_ge(hn_ready, KD + kt + 1)
                        return hn[:, kt, :]

                    for f in range(FT):
                        for part, name in (("ff_gate", "ffg"), ("ff_up", "ffu")):
                            if f % 4 == 0:
                                need((part, f // 4))
                            project((name, f), block_ap((part, f // 4)), f % 4 * P, ffn_normed if f == 0 else normed, KD)
                    for half in range(2):
                        banks = []
                        for k in range(KB):
                            need(("ff_down", half, k))
                            w = block_ap(("ff_down", half, k))
                            ks = min(8, FT - 8 * k)
                            for d in range(4):
                                if k == 0:
                                    banks.append(free_unit(pe, ("ffd", 4 * half + d)))
                                for kt in range(ks):
                                    f = 8 * k + kt
                                    if half == 0 and d == 0:
                                        wait_taken(pe, ("ffu", f))
                                    mm = nc.tensor.matmul(banks[d][:, 0:L], w[:, kt, d * P:(d + 1) * P], hidden[:, f, :],
                                                          start=(f == 0), stop=(f == FT - 1))
                                if k == KB - 1:
                                    mm.then_inc(psum_ready, 1)
                            if k < KB - 1:
                                mm.then_inc(down_used, 1)

            for n in range(4):
                j, half = n // 2, n % 2
                a = TOK[j + 1][0]
                bank = free_unit(pe, ("htok", n))
                for d in range(4):
                    if j == 0:
                        wait_taken(pe, residual(3, 4 * half + d))
                    tr = nc.tensor.transpose(bank[:, d * P:(d + 1) * P], hT[:, 4 * half + d, a:a + P], ident[:, :])
                tr.then_inc(psum_ready, 1)
            bank = free_unit(pe, ("logit",))
            pe.wait_ge(wrg_ready, 1)
            for j in range(2):
                a = TOK[j + 1][0]
                for kt in range(KD):
                    mm = nc.tensor.matmul(bank[:, j * EXPERTS:(j + 1) * EXPERTS], hT[:, kt, a:a + P], wrg[:, kt, :],
                                          start=(kt == 0), stop=(kt == KD - 1))
            mm.then_inc(psum_ready, 1)
            bank = free_unit(pe, ("pos",))
            pe.wait_ge(mask_ready, 2)
            for c, terms in enumerate((((strict, 0),), ((ones[:, :], 0), (strict, 1)), ((ones[:, :], 0), (ones[:, :], 1)))):
                for n, (lhs, j) in enumerate(terms):
                    mm = nc.tensor.matmul(bank[:, c * EXPERTS:(c + 1) * EXPERTS], lhs, mask[:, j, 0:EXPERTS],
                                          start=(n == 0), stop=(n == len(terms) - 1))
            mm.then_inc(psum_ready, 1)

            pe.wait_ge(routed, 2)
            pe.wait_ge(xs_ready, 1)
            pe.wait_ge(taken, NU)

            def expert(e, width):
                def unit_bank(u):
                    if u < 4:
                        if u == 0:
                            wait_etaken(pe, e, -1)
                    else:
                        wait_etaken(pe, e, u - 4)
                    return psum[u % 4]

                def landed(b):
                    pe.wait_ge(slot_full[b % ERING], e * (16 * (EB // ERING)) + 16 * (used_before[b % ERING] + b // ERING + 1))

                pe.wait_ge(sel_ready, e * 4 + 4)
                for u in range(4):
                    bank = unit_bank(u)
                    for d in range(2):
                        kt = 2 * u + d
                        for j in range(2):
                            mm = nc.tensor.matmul(bank[:, d * SLOTS:d * SLOTS + width], xs[:, j, kt * P:(kt + 1) * P],
                                                  psel[:, j, 0:width], start=(j == 0), stop=(j == 1))
                    mm.then_inc(e_full, 1)
                bank = unit_bank(U_PG)
                tiles = [(s, min(P, width - s * P)) for s in range(-(-width // P))]
                for s, n in tiles:
                    for j in range(2):
                        tr = nc.tensor.transpose(bank[0:n, s * SEQ + j * P:s * SEQ + (j + 1) * P], pgat[:, j, s * P:s * P + n], ident[:, :])
                tr.then_inc(e_full, 1)

                def down(i):
                    b = epos["d", i]
                    landed(b)
                    w = eslot(b, 4)
                    for d in range(KD):
                        for f in range(4):
                            if d == 0:
                                wait_etaken(pe, e, U_H + 4 * i + f)
                            mm = nc.tensor.matmul(psum[4 + d // 2][:, d % 2 * SLOTS:d % 2 * SLOTS + width],
                                                  w[:, f, d * P:(d + 1) * P], act[:, i % 2, f, 0:width],
                                                  start=(i == 0 and f == 0 and d % 2 == 0), stop=(i == FB - 1 and f == 3),
                                                  skip_group_check=True)
                        if i == FB - 1 and d % 2 == 1 and d < KD - 1:
                            mm.then_inc(y_ready, 1)
                    mm.then_inc(y_ready if i == FB - 1 else e_down_used, 1)

                for i in range(FB):
                    bg, bu = epos["g", i], epos["u", i]
                    landed(bg)
                    landed(bu)
                    for f in range(4):
                        bank = unit_bank(U_H + 4 * i + f)
                        for col, b in ((0, bg), (SLOTS, bu)):
                            w = eslot(b, KD)
                            for kt in range(KD):
                                if i == 0 and f == 0 and col == 0:
                                    wait_etaken(pe, e, kt // 2)
                                mm = nc.tensor.matmul(bank[:, col:col + width], w[:, kt, f * P:(f + 1) * P], xg[:, kt, 0:width],
                                                      start=(kt == 0), stop=(kt == KD - 1))
                        mm.then_inc(e_full, 1)
                    if i > 0:
                        down(i - 1)
                down(FB - 1)
                units = [(s, half) for s, n in tiles for half in range(2)]
                for u, (s, half) in enumerate(units):
                    n = tiles[s][1]
                    bank = unit_bank(U_Y + u)
                    for d in range(4):
                        if s == 0:
                            pe.wait_ge(yT_ready, e * 4 + (2 * half + d // 2 + 1))
                        tr = nc.tensor.transpose(bank[0:n, d * P:(d + 1) * P], yT[:, 4 * half + d, s * P:s * P + n], ident[:, :])
                    tr.then_inc(e_full, 1 if u < len(units) - 1 else 5 - len(units))
                for u in range(4):
                    j, half = u // 2, u % 2
                    bank = unit_bank(U_O + u)
                    if u < 2:
                        wait_etaken(pe, e, U_Y + 2 * (len(tiles) - 1) + half)
                    for s, n in tiles:
                        mm = nc.tensor.matmul(bank[:, 0:BANK], pgT[0:n, s, j * P:(j + 1) * P], ytok[0:n, s, half * BANK:(half + 1) * BANK],
                                              start=(s == 0), stop=(s == len(tiles) - 1))
                    mm.then_inc(e_full, 1)

            def by_width(e, tokens, widths):
                if len(widths) == 1:
                    expert(e, widths[0])
                    return
                with pe.If(tokens <= widths[0]):
                    expert(e, widths[0])
                with pe.Else():
                    by_width(e, tokens, widths[1:])
                    pe.nop()

            with pe.Fori(0, EXPERTS) as e:
                tokens = pe.value_load(count[0:1, bass.ds(e, 1)], min_val=0, max_val=SLOTS)
                by_width(e, tokens, WIDTHS)

        @block.scalar
        def _(act_e):
            a_ = nc.scalar.activation
            steps = Steps(act_e, act_step)
            load_params(act_e, 0)

            def root(n):
                wait_taken(act_e, (("norm", 0), ("norm", "ffn"), ("norm", 1))[n])
                a_(rms[:, 0, :], rms[:, 0, :], ACT.Sqrt).then_inc(root_ready, 1)

            def squares(n):
                for kt in range(KD):
                    wait_taken(act_e, residual(n, kt))
                    a_(sq[:, kt, :], hT[:, kt, :], ACT.Square).then_inc(sq_ready, 1)

            for l in range(DEPTH):
                t0 = tokens_of(l)
                squares(2 * l)
                root(2 * l)
                for c in range(CT):
                    wait_taken(act_e, ("conv", l, CT + c))
                    a_(conv_in[:, CT + c, :], conv_in[:, CT + c, :], ACT.Sigmoid).then_inc(glu_gate, 1)
                for i in range(2 * QT):
                    wait_taken(act_e, ("qk"[i // QT], l, i % QT))
                    a_(fbm[:, i, 0:L], qkT[:, i, :], ACT.Square).then_inc(qk_sq, 1)
                wait_taken(act_e, ("mean", l))
                for c in range(CT):
                    a_(csq[:, c, :], cy[:, c, :], ACT.Square).then_inc(centred_sq, 1)
                wait_taken(act_e, ("var", l))
                a_(rms[:, 1, :], rms[:, 1, :], ACT.Sqrt).then_inc(ln_root, 1)
                for c in range(CT):
                    act_e.wait_ge(ln_scaled, l * CT + c + 1)
                    a_(csq[:, c, :], cy[:, c, :], ACT.Silu, bias=pcol(l, C_LB + c)).then_inc(conv_act, 1)
                for i in range(2 * QT):
                    wait_taken(act_e, ("qk_ms", l, i))
                    a_(silu[:, i % 2, :], rms[:, i % 2, :], ACT.Sqrt).then_inc(qk_root, 1)
                wait_taken(act_e, ("fg", l))
                steps.did(a_(fga[:, :], fg[:, :], ACT.Abs))
                steps.settle()
                steps.did(a_(fge[:, :], fga[:, :], ACT.Exp, scale=-1.0))
                steps.settle()
                a_(fgl[:, :], fge[:, :], ACT.Ln, bias=ones[:, 0:1]).then_inc(fg_log, 1)
                for h in range(HEADS):
                    s = sc[:, h % 2, :]
                    for n, j in enumerate(score_tiles(l)):
                        m, (c0, keys) = TOK[j][1], S_COL[j]
                        act_e.wait_ge(max_ready, scored(l, h, n) + 1)
                        a_(s[0:m, c0:c0 + keys], s[0:m, c0:c0 + keys], ACT.Exp, bias=nmax[0:m, h % 2, j:j + 1],
                           accum_out=rsum[0:m, h % 2, j:j + 1]).then_inc(exp_ready, 1)
                    act_e.wait_ge(rinv_ready, l * HEADS + h + 1)
                    for j in score_tiles(l):
                        m, (c0, keys) = TOK[j][1], S_COL[j]
                        a_(s[0:m, c0:c0 + keys], s[0:m, c0:c0 + keys], ACT.Copy,
                           scale=rinv[0:m, h % 2, j:j + 1]).then_inc(probs_ready, 1)
                wait_taken(act_e, ("gate", l, GT - 1))
                for d in range(KD):
                    a_(gates[:, :, d, t0:], gates[:, :, d, t0:], ACT.Sigmoid).then_inc(gate_ready, 1)
                if l == 0:
                    squares(1)
                    root(1)
                    for f in range(FT):
                        bank = ready_unit(act_e, ("ffg", f))
                        if f >= 2:
                            wait_taken(act_e, ("ffu", f - 2))
                        a_(silu[:, f % 2, :], bank[:, 0:L], ACT.Silu).then_inc(silu_ready, 1)

            for j in range(2):
                wait_taken(act_e, ("htok", 2 * j + 1))
                if j > 0:
                    act_e.wait_ge(ss_ready, j)
                a_(tok_sq, hacc[:, j, :], ACT.Square, accum_out=ss[:, j:j + 1]).then_inc(ss_ready, 1)
            act_e.wait_ge(sms_ready, 1)
            a_(srt[:, :], sms[:, :], ACT.Sqrt).then_inc(srt_ready, 1)
            act_e.wait_ge(gap_ready, 1)
            a_(pexp[:, :], gap[:, :], ACT.Exp).then_inc(pexp_ready, 1)

            with act_e.Fori(0, EXPERTS) as e:
                for f in range(ET):
                    act_e.wait_ge(e_full, e * EU + (U_H + f + 1))
                    if f >= 2:
                        wait_etaken(act_e, e, U_H + f - 2)
                    a_(esilu[:, f % 2, :], psum[(U_H + f) % 4][:, 0:SLOTS], ACT.Silu).then_inc(e_silu, 1)
                for n in range(4):
                    act_e.wait_ge(y_ready, e * 4 + (n + 1))
                    a_(yT[:, 2 * n:2 * n + 2, :], psum[4 + n][:, :].rearrange("p (d s) -> p d s", d=2), ACT.Copy).then_inc(yT_ready, 1)

        @block.vector
        def _(dve):
            v = nc.vector
            steps = Steps(dve, dve_step)
            freed = [0]

            def frees(name, instruction, count=1):
                assert unit[name] == freed[0], (name, freed[0])
                freed[0] += count
                instruction.then_inc(taken, count)

            v.memset(pw[:, :, :, :].rearrange("p l c n -> p (l c n)"), 0.0).then_inc(pw_zeroed, 1)
            for i in range(BANKS):
                v.memset(psum[i][:, :], 0.0).then_inc(zeroed, 1)
            v.memset(fg[:, :], 0.0).then_inc(zeroed, 1)
            steps.did(v.memset(head_ones[:, :], 0.0))
            steps.settle()
            for b in range(2):
                v.memset(head_ones[b * HD:(b + 1) * HD, b * HD:(b + 1) * HD], 1.0).then_inc(zeroed, 1)
            steps.did(v.memset(rsum[:, :, :], 1.0))
            for t in (pos, mask, comb):
                steps.did(v.memset(t[:, :, :], 0.0))
            dve.wait_ge(consts, 12)
            for g in range(GROUPS):
                b = GW * (g % 2)
                steps.did(v.tensor_scalar(rcnt[b:b + GW, g // 2, :], iota_f[b:b + GW, 0:PAD_P], 1.0, 2.0 ** (g + 1), ALU.add, ALU.min))
            steps.settle()
            v.reciprocal(rcnt[:, :, :], rcnt[:, :, :]).then_inc(rcnt_ready, 1)

            for kt in range(KD):
                bank = ready_unit(dve, ("x", kt))
                frees(("x", kt), v.tensor_copy(hT[:, kt, :], bank[:, 0:L]))
            def take_params(l):
                for n in (2 * l, 2 * l + 1):
                    bank = ready_unit(dve, ("param", n))
                    height = (NA, NT)[n % 2]
                    frees(("param", n), v.tensor_copy(par[:, n, 0:height], bank[:, 0:height]))
                wait_taken(dve, ("param", 2 * l + 1))

            def norm(name, n, l, gain):
                bank = ready_unit(dve, name)
                frees(name, v.tensor_scalar(rms[:, 0, :], bank[:, 0:L], 1.0 / D, EPS_RMS, ALU.mult, ALU.add))
                if n == 0:
                    take_params(0)
                dve.wait_ge(root_ready, n + 1)
                steps.did(v.reciprocal(rstd[:, 0, :], rms[:, 0, :]))
                steps.settle()
                for kt in range(KD):
                    v.scalar_tensor_tensor(hn[:, kt, :], hT[:, kt, :], pcol(l, gain + kt), rstd[:, 0, :], ALU.mult, ALU.mult)\
                     .then_inc(hn_ready, 1)

            for l in range(DEPTH):
                t0 = tokens_of(l)
                norm(("norm", l), 2 * l, l, C_MIX)

                for i in range(2 * CT):
                    bank = ready_unit(dve, ("conv", l, i))
                    frees(("conv", l, i), v.tensor_scalar(conv_in[:, i, :], bank[:, 0:L], pcol(l, C_CONV + i), None, ALU.add))
                for i in range(PT_):
                    bank = ready_unit(dve, ("pool", l, i))
                    frees(("pool", l, i), v.tensor_scalar(ppad[:, i, PAD_P:], bank[:, 0:L], pcol(l, C_POOL + i), None, ALU.add))
                last = [0] * CT
                for c in range(CT):
                    dve.wait_ge(glu_gate, l * CT + c + 1)
                    last[c] = steps.did(v.tensor_tensor(upad[:, c, PAD_C:], conv_in[:, c, :], conv_in[:, CT + c, :], ALU.mult))

                def taps(first, count):
                    for t in range(first, min(first + count, TAPS)):
                        for c in range(CT):
                            steps.settle(last[c])
                            if t == 0:
                                last[c] = steps.did(v.tensor_scalar(cy[:, c, :], upad[:, c, 0:L], tap(l, 0, c), pcol(l, C_CB + c),
                                                                    ALU.mult, ALU.add))
                                continue
                            ins = v.scalar_tensor_tensor(cy[:, c, :], upad[:, c, t:t + L], tap(l, t, c), cy[:, c, :], ALU.mult, ALU.add)
                            if t < TAPS - 1:
                                last[c] = steps.did(ins)
                            else:
                                ins.then_inc(conv_done, 1)

                per = -(-TAPS // (2 * QT - 1))
                for i in range(2 * QT):
                    name = ("qk"[i // QT], l, i % QT)
                    bank = ready_unit(dve, name)
                    frees(name, v.tensor_scalar(qkT[:, i, :], bank[:, 0:L], pcol(l, C_Q + i), None, ALU.add))
                    taps(i * per, per)
                bank = ready_unit(dve, ("mean", l))
                dve.wait_ge(conv_done, (l + 1) * CT)
                v.tensor_tensor(cy[:, 0, :], cy[:, 0, :], bank[:, 0:L], ALU.subtract)
                frees(("mean", l), v.tensor_tensor(cy[:, 1, :], cy[:, 1, :], bank[:, 0:L], ALU.subtract))
                if l == 0:
                    take_params(1)
                for i in range(QT):
                    bank = ready_unit(dve, ("v", l, i))
                    frees(("v", l, i), v.tensor_scalar(vT[:, i, :], bank[:, 0:L], pcol(l, C_V + i), None, ALU.add))
                bank = ready_unit(dve, ("var", l))
                frees(("var", l), v.tensor_scalar(rms[:, 1, :], bank[:, 0:L], EPS_LN, None, ALU.add))
                dve.wait_ge(ln_root, l + 1)
                steps.did(v.reciprocal(rstd[:, 1, :], rms[:, 1, :]))
                steps.settle()
                for c in range(CT):
                    v.scalar_tensor_tensor(cy[:, c, :], cy[:, c, :], pcol(l, C_LG + c), rstd[:, 1, :], ALU.mult, ALU.mult).then_inc(ln_scaled, 1)
                for c in range(PT_):
                    bank = ready_unit(dve, ("mix", l, c))
                    frees(("mix", l, c), v.tensor_scalar(poolo[:, c, :], bank[:, 0:L], pcol(l, C_PS + c), None, ALU.mult))

                steps.did(v.tensor_scalar(qgain[:, 0:1], pcol(l, C_QN), float(HD) ** -0.5, None, ALU.mult))
                steps.did(v.tensor_copy(qgain[:, 1:2], pcol(l, C_KN)))
                for i in range(2 * QT):
                    bank = ready_unit(dve, ("qk_ms", l, i))
                    frees(("qk_ms", l, i), v.tensor_scalar(rms[:, i % 2, :], bank[:, 0:L], 1.0 / HD, EPS_RMS, ALU.mult, ALU.add))
                    dve.wait_ge(qk_root, l * 2 * QT + i + 1)
                    steps.did(v.reciprocal(rstd[:, i % 2, :], silu[:, i % 2, :]))
                    steps.settle()
                    v.scalar_tensor_tensor(qkT[:, i, :], qkT[:, i, :], qgain[:, i // QT:i // QT + 1], rstd[:, i % 2, :],
                                           ALU.mult, ALU.mult).then_inc(qk_ready, 1)

                def take_gate(g):
                    bank = ready_unit(dve, ("gate", l, g))
                    frees(("gate", l, g), v.tensor_scalar(gates[:, g // KD, g % KD, t0:], bank[:, t0:L], pcol(l, C_GATE + g), None, ALU.add))

                bank = ready_unit(dve, ("fg", l))
                v.tensor_tensor(fg[0:META, 0:HEADS], bank[0:META, 0:HEADS], bf_bc[0:META, l, :], ALU.add)
                v.tensor_tensor(fg[:, HEADS:2 * HEADS], bank[:, HEADS:2 * HEADS], bf_bc[:, l, :], ALU.add)
                frees(("fg", l), v.tensor_tensor(fg[:, 2 * HEADS:], bank[:, 2 * HEADS:3 * HEADS], bf_bc[:, l, :], ALU.add))
                for j, (_, n) in enumerate(TOK):
                    bank = ready_unit(dve, ("vtok", l, j))
                    if j == 0:
                        dve.wait_ge(pool_mix, (l + 1) * PT_)
                    frees(("vtok", l, j), v.tensor_copy(vtok[0:n, j, :], bank[0:n, 0:ATT_W]))
                dve.wait_ge(fg_log, l + 1)
                v.scalar_tensor_tensor(ls[:, :], fg[:, :], 0.0, fgl[:, :], ALU.min, ALU.subtract).then_inc(ls_ready, 1)
                for g in range(GATES_F):
                    take_gate(g)
                bank = ready_unit(dve, ("ftok", l))
                v.tensor_copy(ftok[0:META, 0:HEADS], bank[0:META, 0:HEADS])
                frees(("ftok", l), v.tensor_copy(ftok[:, HEADS:], bank[:, HEADS:3 * HEADS]))
                bank = ready_unit(dve, ("frow", l))
                frees(("frow", l), v.tensor_copy(frow[:, :], bank[0:HEADS, 0:L]))
                take_gate(GATES_F)
                for h in range(HEADS):
                    bank = ready_unit(dve, ("fbc", l, h))
                    frees(("fbc", l, h), v.tensor_copy(fbm[:, h, 0:L], bank[:, 0:L]))

                def take_values(h):
                    b = HD * (h % 2)
                    bank = ready_unit(dve, ("pv", l, h))
                    frees(("pv", l, h), v.tensor_copy(attT[b:b + HD, h // 2, t0:], bank[b:b + HD, t0:L]))

                for g in range(GATES_F + 1, GATES_H):
                    take_gate(g)
                dve.wait_ge(fbm_ready, (l + 1) * 3)
                for h in range(HEADS):
                    bank = ready_unit(dve, ("s", l, h))
                    tiles = score_tiles(l)
                    for j in tiles:
                        m, (c0, keys) = TOK[j][1], S_COL[j]
                        ins = v.scalar_tensor_tensor(sc[0:m, h % 2, c0:c0 + keys], bank[0:m, c0:c0 + keys],
                                                     ftok[0:m, j * HEADS + h:j * HEADS + h + 1], fbm[0:m, h, c0:c0 + keys],
                                                     ALU.add, ALU.subtract)
                    frees(("s", l, h), ins)
                    wait_taken(dve, ("s", l, h))
                    for j in tiles:
                        m, (c0, keys) = TOK[j][1], S_COL[j]
                        v.tensor_reduce(nmax[0:m, h % 2, j:j + 1], sc[0:m, h % 2, c0:c0 + keys], AX_X, ALU.max, negate=True).then_inc(max_ready, 1)
                    take_gate(GATES_H + 2 * h)
                    dve.wait_ge(exp_ready, scored(l, h + 1, 0))
                    v.reciprocal(rinv[:, h % 2, :], rsum[:, h % 2, :]).then_inc(rinv_ready, 1)
                    if h > 0:
                        take_values(h - 1)
                    take_gate(GATES_H + 2 * h + 1)
                    bank = ready_unit(dve, ("pt", l, h))
                    frees(("pt", l, h), v.tensor_copy(pt[:, :], bank[:, 0:3 * P]))
                    bank = ready_unit(dve, ("ptm", l, h))
                    frees(("ptm", l, h), v.tensor_copy(ptm[:, t0:], bank[0:META, t0:L]))
                take_values(HEADS - 1)

                for d in range(KD):
                    dve.wait_ge(gate_ready, l * KD + d + 1)
                    for b, name in enumerate(("ya", "yc", "yp")):
                        bank = ready_unit(dve, (name, l, d))
                        g = gates[:, b, d, t0:]
                        frees((name, l, d), v.tensor_tensor(g, bank[:, t0:L], g, ALU.mult))
                for d in range(KD):
                    bank = ready_unit(dve, ("out", l, d))
                    frees(("out", l, d), v.tensor_tensor(hT[:, d, t0:], bank[:, t0:L], hT[:, d, t0:], ALU.add))
                if l == 0:
                    norm(("norm", "ffn"), 1, 0, C_FFN)
                    for f in range(FT):
                        dve.wait_ge(silu_ready, f + 1)
                        bank = ready_unit(dve, ("ffu", f))
                        frees(("ffg", f), v.tensor_tensor(hidden[:, f, :], bank[:, 0:L], silu[:, f % 2, :], ALU.mult), 2)
                    for d in range(KD):
                        bank = ready_unit(dve, ("ffd", d))
                        frees(("ffd", d), v.tensor_tensor(hT[:, d, :], bank[:, 0:L], hT[:, d, :], ALU.add))

            steps.did(v.tensor_tensor(wrg[:, :, :], wr[:, :, :],
                                      par[:, 2 * (DEPTH - 1), C_FFN:C_FFN + KD].unsqueeze(2).broadcast_to([P, KD, EXPERTS]), ALU.mult))
            v.tensor_copy(lg[:, :, :], pos[:, :, 0:8]).then_inc(wrg_ready, 1)
            for n in range(4):
                j, half = n // 2, n % 2
                bank = ready_unit(dve, ("htok", n))
                frees(("htok", n), v.tensor_copy(hacc[:, j, half * BANK:(half + 1) * BANK], bank[:, :]))
            dve.wait_ge(ss_ready, 2)
            v.tensor_scalar(sms[:, :], ss[:, :], 1.0 / D, EPS_RMS, ALU.mult, ALU.add).then_inc(sms_ready, 1)
            dve.wait_ge(srt_ready, 1)
            steps.did(v.reciprocal(srs[:, :], srt[:, :]))
            steps.settle()
            bank = ready_unit(dve, ("logit",))
            v.scalar_tensor_tensor(lg[:, 0, :], bank[:, 0:EXPERTS], srs[:, 0:1], br_bc[:, :], ALU.mult, ALU.add)
            frees(("logit",), v.scalar_tensor_tensor(lg[:, 1, :], bank[:, EXPERTS:2 * EXPERTS], srs[:, 1:2], br_bc[:, :], ALU.mult, ALU.add))
            wait_taken(dve, ("logit",))
            for j in range(2):
                steps.did(v.max(mx[:, j, :], lg[:, j, :]))
            steps.settle()
            v.tensor_tensor(gap[:, :], mx[:, :, 1], mx[:, :, 0], ALU.subtract).then_inc(gap_ready, 1)
            for j in range(2):
                steps.did(v.max_index(mi[:, j, :], mx[:, j, :], lg[:, j, :]))
            steps.settle()
            steps.did(v.tensor_copy(mif[:, :, :], mi[:, :, :]))
            steps.settle()
            for j in range(2):
                steps.did(v.tensor_scalar(oh0[:, j, :], iota_f[:, 0:EXPERTS], mif[:, j, 0:1], None, ALU.is_equal))
                steps.did(v.tensor_scalar(oh1[:, j, :], iota_f[:, 0:EXPERTS], mif[:, j, 1:2], None, ALU.is_equal))
            steps.settle()
            for j in range(2):
                v.tensor_tensor(mask[:, j, 0:EXPERTS], oh0[:, j, :], oh1[:, j, :], ALU.add).then_inc(mask_ready, 1)
            dve.wait_ge(pexp_ready, 1)
            steps.did(v.tensor_scalar(pden[:, :], pexp[:, :], 1.0, None, ALU.add))
            steps.settle()
            steps.did(v.reciprocal(pr0[:, :], pden[:, :]))
            steps.settle()
            steps.did(v.tensor_tensor(pr1[:, :], pexp[:, :], pr0[:, :], ALU.mult))
            for j in range(2):
                steps.did(v.tensor_scalar(comb[:, j, 0:EXPERTS], oh0[:, j, :], pr0[:, j:j + 1], None, ALU.mult))
            steps.settle()
            for j in range(2):
                v.scalar_tensor_tensor(comb[:, j, 0:EXPERTS], oh1[:, j, :], pr1[:, j:j + 1], comb[:, j, 0:EXPERTS], ALU.mult, ALU.add)\
                 .then_inc(comb_ready, 1)
            bank = ready_unit(dve, ("pos",))
            v.tensor_copy(pos[:, :, 0:EXPERTS], bank[:, 0:2 * EXPERTS].rearrange("p (j e) -> p j e", j=2)).then_inc(routed, 1)
            v.tensor_copy(count[:, :], bank[:, 2 * EXPERTS:3 * EXPERTS]).then_inc(routed, 1)
            dve.wait_ge(s_gbc, 16)
            for j in range(2):
                ins = v.scalar_tensor_tensor(xs[:, j, :], hacc[:, j, :], srs[:, j:j + 1], gbc, ALU.mult, ALU.mult)
                if j == 0:
                    ins.then_inc(xs_ready, 1)
            frees(("pos",), ins)
            dve.wait_ge(routed, 2)
            dve.wait_ge(comb_ready, 2)
            assert freed[0] == NU

            def select(e):
                for dst, src in ((psel, mask), (pgat, comb)):
                    for j in range(2):
                        v.tensor_scalar(dst[:, j, :], iota_f[:, :], pos[:, j, bass.ds(e, 1)], src[:, j, bass.ds(e, 1)],
                                        ALU.is_equal, ALU.mult).then_inc(sel_ready, 1)

            select(0)
            v.tensor_copy(lg[:, :, :], pos[:, :, 0:8]).then_inc(e_taken, 1)
            with dve.Fori(0, EXPERTS) as e:
                def unit_ready(u):
                    dve.wait_ge(e_full, e * EU + (u + 1))
                    return psum[u % 4]

                for u in range(4):
                    bank = unit_ready(u)
                    v.tensor_copy(xg[:, 2 * u:2 * u + 2, :], bank[:, :].rearrange("p (d s) -> p d s", d=2)).then_inc(e_taken, 1)
                bank = unit_ready(U_PG)
                v.tensor_copy(pgT[:, :, :], bank[:, :].rearrange("p (s t) -> p s t", s=2)).then_inc(e_taken, 1)
                for f in range(ET):
                    if f % 4 == 0 and f >= 8:
                        dve.wait_ge(e_down_used, e * (FB - 1) + (f // 4 - 1))
                    bank = unit_ready(U_H + f)
                    dve.wait_ge(e_silu, e * ET + (f + 1))
                    v.tensor_tensor(act[:, f // 4 % 2, f % 4, :], bank[:, SLOTS:2 * SLOTS], esilu[:, f % 2, :], ALU.mult).then_inc(e_taken, 1)
                    if f == ET - 8:
                        select(e + 1)
                for u in range(4):
                    bank = unit_ready(U_Y + u)
                    v.tensor_copy(ytok[:, u // 2, u % 2 * BANK:(u % 2 + 1) * BANK], bank[:, :]).then_inc(e_taken, 1)
                for u in range(4):
                    bank = unit_ready(U_O + u)
                    h = hacc[:, u // 2, u % 2 * BANK:(u % 2 + 1) * BANK]
                    v.tensor_tensor(h, bank[:, :], h, ALU.add).then_inc(e_taken, 1)


_INS = ["x", "meta", "norm_mix", "w_in", "b_in", "q_norm", "k_norm", "w_attn_o", "conv_w", "conv_b", "conv_ln_g",
        "conv_ln_b", "w_conv_o", "pool_w", "pool_scale", "w_pool_o", "w_out", "norm_ffn", "w_ff_gate", "w_ff_up",
        "w_ff_down", "w_router", "b_router", "w_e_gate", "w_e_up", "w_e_down"]


def kernel(**inputs):
    import concourse.bacc as bacc
    from concourse.bass_utils import run_bass_kernel_spmd

    nc = bacc.Bacc("TRN2", target_bir_lowering=False, num_devices=1)
    arrays, args = {}, []
    for name in _INS:
        a = np.ascontiguousarray(inputs[name])
        arrays[f"in_{name}"] = a
        args.append(nc.dram_tensor(f"in_{name}", a.shape, mybir.dt.from_np(a.dtype), kind="ExternalInput").ap())
    out = nc.dram_tensor("out_y", inputs["x"].shape, F32, kind="ExternalOutput").ap()
    trunk_program(nc, *args, out)
    r = run_bass_kernel_spmd(nc, [arrays], core_ids=[0])
    return r.results[0]["out_y"]
```

```python
from contextlib import ExitStack

import numpy as np

import concourse.bass as bass
from concourse import mybir

ALU = mybir.AluOpType
ACT = mybir.ActivationFunctionType
F32 = mybir.dt.float32
F32R = mybir.dt.float32r
I32 = mybir.dt.int32
U32 = mybir.dt.uint32
AX_X = mybir.AxisListType.X

P = 128
BANK = 512
BANKS = 8


def trunk_program(nc, x, meta, norm_mix, w_in, b_in, q_norm, k_norm, w_attn_o, conv_w, conv_b, conv_ln_g,
                  conv_ln_b, w_conv_o, pool_w, pool_scale, w_pool_o, w_out, norm_ffn, w_ff_gate, w_ff_up,
                  w_ff_down, w_router, b_router, w_e_gate, w_e_up, w_e_down, out):
    _, SEQ, D = x.shape
    META = meta.shape[0]
    DEPTH, _, IN_W = w_in.shape
    HD = q_norm.shape[1]
    ATT_W = w_attn_o.shape[1]
    HEADS = ATT_W // HD
    TAPS, CONV_W = conv_w.shape[1:]
    GROUPS, GW = pool_w.shape[1:3]
    POOL_W = GROUPS * GW
    D_FF = w_ff_gate.shape[2]
    EXPERTS, D_FE = w_e_gate.shape[1], w_e_gate.shape[3]
    L = META + SEQ
    assert DEPTH == 2 and SEQ == 2 * P and META == 16 and 2 * HD == P and 2 * GW == P

    KD = D // P
    QT = ATT_W // P
    CT = CONV_W // P
    PT_ = POOL_W // P
    GT = 3 * KD
    FT = D_FF // P
    ET = D_FE // P
    COL_F = 3 * ATT_W
    COL_CONV = COL_F + HEADS
    COL_POOL = COL_CONV + 2 * CONV_W
    COL_GATE = COL_POOL + POOL_W
    PAD_C = TAPS - 1
    PAD_P = 16
    EPS_RMS, EPS_LN = 1e-6, 1e-5
    NEG = -1e30
    TOK = [(0, META), (META, P), (META + P, P)]
    S_COL = {2: (0, L), 1: (L, META + P), 0: (L + META + P, META)}
    SW = L + META + P + META
    SLOTS = SEQ

    BW = 4096
    blocks = []
    for l in range(DEPTH):
        def cols(w, c0, n):
            return w[:, c0:c0 + n].rearrange("(k p) n -> p k n", p=P), w.shape[0] // P, n
        blocks.append((("conv", l), *cols(w_in[l], COL_CONV, 2 * CONV_W)))
        blocks.append((("pool", l), *cols(w_in[l], COL_POOL, POOL_W)))
        for i, part in enumerate("qkv"):
            blocks.append(((part, l), *cols(w_in[l], i * ATT_W, ATT_W)))
        for i in range(GT // 4):
            blocks.append((("gate", l, i), *cols(w_in[l], COL_GATE + i * 4 * P, 4 * P)))
        blocks.append((("attn_o", l), *cols(w_attn_o[l], 0, D)))
        blocks.append((("conv_o", l), *cols(w_conv_o[l], 0, D)))
        blocks.append((("pool_o", l), *cols(w_pool_o[l], 0, D)))
        for i in range(2):
            blocks.append((("out", l, i), *cols(w_out[l], i * D // 2, D // 2)))
        if l == 0:
            for i in range(0, FT, 4):
                n = min(4, FT - i) * P
                blocks.append((("ff_gate", i // 4), *cols(w_ff_gate[0], i * P, n)))
                blocks.append((("ff_up", i // 4), *cols(w_ff_up[0], i * P, n)))
            for half in range(2):
                for k in range(0, FT, 8):
                    n = min(8, FT - k)
                    blocks.append((("ff_down", half, k // 8), *cols(w_ff_down[0][k * P:(k + n) * P, :], half * D // 2, D // 2)))
    RING = 5
    index = {b[0]: n for n, b in enumerate(blocks)}
    NB = len(blocks)
    HB = BW // 2
    RAW, SPLIT = 7, 3
    FB = ET // 4
    ESEQ = []
    for i in range(FB):
        ESEQ += [(kind, i, h) for kind in "gu" for h in range(2)]
        ESEQ += [("d", i - 1, h) for h in range(2)] if i else []
    ESEQ += [("d", FB - 1, h) for h in range(2)]
    EB = len(ESEQ)
    epos = {b: n for n, b in enumerate(ESEQ)}
    assert EB % RAW == 0 and EB % SPLIT == 0
    MAX_JOBS = EXPERTS + 2 * SEQ // (P + 1)
    TABLE = MAX_JOBS + 1

    order = []
    GATES_F, GATES_H = 5, GT - 2 * HEADS
    for kt in range(KD):
        order.append(("x", kt))
    for l in range(DEPTH):
        order += [("norm", l)] + ([("param", 0), ("param", 1)] if l == 0 else [])
        order += [("conv", l, i) for i in range(2 * CT)] + [("pool", l, i) for i in range(PT_)]
        order += [("q", l, i) for i in range(QT)] + [("k", l, i) for i in range(QT)]
        order += [("mean", l)] + ([("param", 2), ("param", 3)] if l == 0 else [])
        order += [("v", l, i) for i in range(QT)]
        order += [("var", l)] + [("mix", l, i) for i in range(PT_)]
        order += [("qk_ms", l, i) for i in range(2 * QT)]
        order += [("fg", l)] + [("vtok", l, j) for j in range(3)]
        order += [("gate", l, g) for g in range(GATES_F)]
        order += [("ftok", l), ("frow", l)] + [("gate", l, GATES_F)]
        order += [("fbc", l, h) for h in range(HEADS)]
        order += [("gate", l, g) for g in range(GATES_F + 1, GATES_H)]
        for h in range(HEADS):
            order += [("s", l, h), ("gate", l, GATES_H + 2 * h)]
            order += [("pv", l, h - 1)] if h else []
            order += [("gate", l, GATES_H + 2 * h + 1), ("pt", l, h), ("ptm", l, h)]
        order += [("pv", l, HEADS - 1)]
        for d in range(KD):
            order += [("ya", l, d), ("yc", l, d), ("yp", l, d)]
        order += [("out", l, d) for d in range(KD)]
        if l == 0:
            order += [("norm", "ffn")]
            for f in range(FT):
                order += [("ffg", f), ("ffu", f)]
            order += [("ffd", d) for d in range(KD)]
    order += [("htok", n) for n in range(4)] + [("logit",), ("pos",)]
    unit = {name: n for n, name in enumerate(order)}
    NU = len(order)
    F_PG, F_T, F_O = 2, 3, 3 + FB
    EF = F_O + 4
    U_PG, U_H, U_T, U_O = 2, 3, 4, 3 + 2 * FB
    EU = U_O + 4

    ctx = ExitStack()
    mixers = ExitStack()
    with ctx:
        def sb(name, shape, dt=F32):
            return ctx.enter_context(nc.sbuf_tensor(name, shape, dt))

        def sbm(name, shape, dt=F32):
            return mixers.enter_context(nc.sbuf_tensor(name, shape, dt))

        def sem(name):
            return ctx.enter_context(nc.semaphore(name))

        psum = [ctx.enter_context(nc.psum_tensor(f"bank{i}", [P, BANK], F32)) for i in range(BANKS)]

        ring = sb("ring", [P, RING, BW])
        hT = sb("hT", [P, KD, L])
        vT = sb("vT", [P, QT, L])
        att_buf = sb("att_buf", [P, QT * L + 3 * ATT_W])
        attT = att_buf[:, 0:QT * L].rearrange("p (i t) -> p i t", i=QT)
        vtok_flat = att_buf[:, QT * L:QT * L + 3 * ATT_W]
        vtok = vtok_flat.rearrange("p (j n) -> p j n", j=3)
        WP = PT_ * (PAD_P + L)
        psa = vtok_flat[:, 0:WP].rearrange("p (c t) -> p c t", c=PT_)
        psb = vtok_flat[:, WP:2 * WP].rearrange("p (c t) -> p c t", c=PT_)
        ident = sb("ident", [P, P])
        ones = sb("ones", [P, P])
        mean_ones = sb("mean_ones", [P, P])
        head_ones = sb("head_ones", [P, P])
        tri = sb("tri", [P, 3, L])
        strict = tri[:, 1, META - 1:META - 1 + P]
        iota_f = sb("iota_f", [P, SLOTS])
        rcnt = sb("rcnt", [P, PT_, PAD_P])
        NA = 2 * KD + 3 * QT + 2 * CT + PT_ + GT + 3 * CT + PT_ + 2
        NT = TAPS * CT
        par = sb("par", [P, 2 * DEPTH, P])
        bf_bc = sb("bf_bc", [P, DEPTH, HEADS])
        wf = sb("wf", [P, DEPTH, KD, HEADS])
        pw = sb("pw", [P, DEPTH, PT_, P])
        wr = sb("wr", [P, KD, EXPERTS])
        wrg = sb("wrg", [P, KD, EXPERTS])
        br_bc = sb("br_bc", [P, EXPERTS])
        fg = sb("fg", [P, 3 * HEADS])
        fga = sb("fga", [P, 3 * HEADS])
        fge = sb("fge", [P, 3 * HEADS])
        fgl = sb("fgl", [P, 3 * HEADS])
        ls = sb("ls", [P, 3 * HEADS])
        ftok = sb("ftok", [P, 3 * HEADS])
        frow = sb("frow", [HEADS, L])
        qgain = sb("qgain", [P, 2])
        nmax = sb("nmax", [P, 2, 3])
        rsum = sb("rsum", [P, 2, 3])
        rinv = sb("rinv", [P, 2, 3])


        job_table = sb("job_table", [P, 2, TABLE], I32)
        n_jobs = sb("n_jobs", [P, 2], I32)
        small = {n: sb(n, [P, 2]) for n in ("ss", "sms", "srt", "srs", "gap", "pexp", "pden", "pr0", "pr1")}
        ss, sms, srt, srs, gap, pexp, pden, pr0, pr1 = (small[n] for n in small)
        lg = sb("lg", [P, 2, 8])
        mx = sb("mx", [P, 2, 8])
        mi = sb("mi", [P, 2, 8], U32)
        mif = sb("mif", [P, 2, 8])
        oh0 = sb("oh0", [P, 2, EXPERTS])
        oh1 = sb("oh1", [P, 2, EXPERTS])
        comb = sb("comb", [P, 2, 2 * EXPERTS])
        mask = sb("mask", [P, 2, 2 * EXPERTS])
        pos = sb("pos", [P, 2, 2 * EXPERTS])

        spare = sbm("spare", [P, 2 * BW])
        gates = spare[:, 0:GT * L].rearrange("p (b d t) -> p b d t", b=3, d=KD)
        hidden = spare[:, 0:FT * L].rearrange("p (f t) -> p f t", f=FT)
        xload = spare[:, 0:2 * D].rearrange("p (j n) -> p j n", j=2)
        mload = spare[0:META, 2 * D:3 * D]
        hn = sbm("hn", [P, KD, L])
        qkT = sbm("qkT", [P, 2 * QT, L])
        mT = qkT
        fbm = sbm("fbm", [P, HEADS, SW])
        sq = fbm[:, :, 0:L]
        conv_buf = sbm("conv_buf", [P, 4 * CT, L])
        conv_in = conv_buf[:, 0:2 * CT, :]
        cy = conv_buf[:, 2 * CT:3 * CT, :]
        csq = conv_buf[:, 3 * CT:4 * CT, :]
        upad = sbm("upad", [P, CT, PAD_C + L])
        ppad = sbm("ppad", [P, PT_, PAD_P + L])
        poolo = sbm("poolo", [P, PT_, L])
        sc = sbm("sc", [P, 2, SW])
        pt = sbm("pt", [P, 3 * P])
        ptm = sbm("ptm", [META, L])
        rms = sbm("rms", [P, 2, L])
        rstd = sbm("rstd", [P, 2, L])
        silu = sbm("silu", [P, 2, L])
        silu_flat = silu[:, :, :].rearrange("p a t -> p (a t)")
        iota_i = rms[:, :, :].rearrange("p a t -> p (a t)")[:, 0:SLOTS].bitcast(I32)
        rows = silu_flat[:, 0:2 * DEPTH * P].rearrange("p (r n) -> p r n", n=P)

        def flat(t):
            return t[:, :, :].rearrange("p a t -> p (a t)")

        hacc = att_buf[:, 0:2 * D].rearrange("p (j n) -> p j n", j=2)
        gbc = flat(vT)[:, 0:D]
        raw = flat(ring)[:, 0:RAW * HB].rearrange("p (r n) -> p r n", r=RAW)
        rest = flat(ring)[:, RAW * HB:RING * BW]
        xs = rest[:, 0:2 * D].rearrange("p (j n) -> p j n", j=2)
        hid = rest[:, 2 * D:2 * D + BANK]
        esilu = rest[:, 2 * D + BANK:2 * D + 3 * BANK].rearrange("p (b n) -> p b n", b=2)
        ytok = rest[:, 2 * D + 3 * BANK:3 * D + 3 * BANK]
        psel = rest[:, 3 * D + 3 * BANK:3 * D + 3 * BANK + 2 * P].rearrange("p (j s) -> p j s", j=2)
        pgat = rest[:, 3 * D + 3 * BANK + 2 * P:3 * D + 3 * BANK + 4 * P].rearrange("p (j s) -> p j s", j=2)
        tok_sq = ytok
        pgT = flat(tri)[:, 0:SEQ]
        mixers.close()
        cum = sb("cum", [P, 4, 2 * EXPERTS])
        cmp = sb("cmp", [P, TABLE, EXPERTS])
        jobf = sb("jobf", [P, 2, TABLE])
        w_hi = sb("w_hi", [P, SPLIT, HB], F32R)
        w_lo = sb("w_lo", [P, SPLIT, HB], F32R)
        xg_hi = sb("xg_hi", [P, D], F32R)
        xg_lo = sb("xg_lo", [P, D], F32R)
        act_hi = sb("act_hi", [P, BANK], F32R)
        act_lo = sb("act_lo", [P, BANK], F32R)

        s_x = sem("x_loaded")
        s_par = [sem(f"params_loaded{l}") for l in range(DEPTH)]
        s_out = sem("out_written")
        s_gbc = sem("ffn_gain_loaded")
        slot_full = [sem(f"slot_full{i}") for i in range(RING)]
        landed = [sem(f"expert_block_landed{i}") for i in range(RAW)]
        psum_ready = sem("psum_ready")
        taken = sem("units_taken")
        down_used = sem("down_block_used")
        zeroed = sem("psum_zeroed")
        pw_zeroed = sem("pool_blocks_zeroed")
        rcnt_ready = sem("window_counts_ready")
        consts = sem("consts_built")
        pool_step = sem("pool_step")
        dve_step = sem("dve_step")
        act_step = sem("act_step")
        sq_ready = sem("squares_ready")
        root_ready = sem("root_ready")
        hn_ready = sem("normed_ready")
        glu_gate = sem("glu_gate")
        conv_done = sem("conv_done")
        centred_sq = sem("centred_sq")
        ln_root = sem("ln_root")
        ln_scaled = sem("ln_scaled")
        conv_act = sem("conv_act")
        pool_mix = sem("pool_mix")
        qk_sq = sem("qk_sq")
        qk_root = sem("qk_root")
        qk_ready = sem("qk_ready")
        fg_log = sem("forget_log")
        ls_ready = sem("log_sigmoid_ready")
        fbm_ready = sem("decay_masked")
        max_ready = sem("max_ready")
        exp_ready = sem("exp_ready")
        rinv_ready = sem("rinv_ready")
        probs_ready = sem("probs_ready")
        gate_ready = sem("gate_ready")
        m_ready = sem("mixed_ready")
        silu_ready = sem("silu_ready")
        ss_ready = sem("token_square_ready")
        sms_ready = sem("token_ms_ready")
        srt_ready = sem("token_root_ready")
        xs_ready = sem("tokens_normed")
        wrg_ready = sem("router_ready")
        gap_ready = sem("top_gap_ready")
        pexp_ready = sem("top_exp_ready")
        mask_ready = sem("mask_ready")
        routed = sem("routed")
        comb_ready = sem("combine_ready")
        sel_ready = sem("selection_ready")
        e_full = sem("expert_unit_ready")
        e_taken = sem("expert_units_taken")
        hi_ready = sem("high_part_ready")
        lo_ready = sem("low_part_ready")
        split_used = sem("split_block_used")
        e_scalar = sem("expert_scalar_step")

        N_PAR = [15 + 4, 15 + 4 + 2]

        def tokens_of(l):
            return 0 if l == 0 else META

        def weight_rows(t, b):
            return t[:, b % SPLIT, :].rearrange("p (k n) -> p k n", k=2 if ESEQ[b][0] == "d" else 4)

        def block_ap(name):
            _, _, k, n = blocks[index[name]]
            return ring[:, index[name] % RING, 0:k * n].rearrange("p (k n) -> p k n", k=k)

        C_MIX, C_FFN = 0, KD
        C_Q = 2 * KD
        C_K = C_Q + QT
        C_V = C_K + QT
        C_CONV = C_V + QT
        C_POOL = C_CONV + 2 * CT
        C_GATE = C_POOL + PT_
        C_CB = C_GATE + GT
        C_LG = C_CB + CT
        C_LB = C_LG + CT
        C_PS = C_LB + CT
        C_QN = C_PS + PT_
        C_KN = C_QN + 1
        assert C_KN + 1 == NA <= P and NT <= P

        def pcol(l, c):
            return par[:, 2 * l, c:c + 1]

        def tap(l, t, c):
            return par[:, 2 * l + 1, CT * t + c:CT * t + c + 1]



        last_unit = {}
        down_used_at = {}
        for l in range(DEPTH):
            last_unit["conv", l] = ("conv", l, 2 * CT - 1)
            last_unit["pool", l] = ("pool", l, PT_ - 1)
            for part in "qkv":
                last_unit[part, l] = (part, l, QT - 1)
            for i in range(GT // 4):
                last_unit["gate", l, i] = ("gate", l, 4 * i + 3)
            last_unit["attn_o", l] = ("ya", l, KD - 1)
            last_unit["conv_o", l] = ("yc", l, KD - 1)
            last_unit["pool_o", l] = ("yp", l, KD - 1)
            for i in range(2):
                last_unit["out", l, i] = ("out", l, 4 * i + 3)
        for i in range(0, FT, 4):
            last_unit["ff_gate", i // 4] = ("ffg", min(i + 3, FT - 1))
            last_unit["ff_up", i // 4] = ("ffu", min(i + 3, FT - 1))
        KB = (FT + 7) // 8
        for half in range(2):
            last_unit["ff_down", half, KB - 1] = ("ffd", 4 * half + 3)
            for k in range(KB - 1):
                down_used_at["ff_down", half, k] = half * (KB - 1) + k + 1

        def wait_used(eng, n):
            name = blocks[n][0]
            if name in down_used_at:
                eng.wait_ge(down_used, down_used_at[name])
            else:
                eng.wait_ge(psum_ready, unit[last_unit[name]] + 1)

        last_in_slot = {s: max(n for n in range(NB) if n % RING == s) for s in range(RING)}
        def free_unit(eng, name):
            n = unit[name]
            if n >= BANKS:
                eng.wait_ge(taken, n - BANKS + 1)
            return psum[n % BANKS]

        def ready_unit(eng, name):
            eng.wait_ge(psum_ready, unit[name] + 1)
            return psum[unit[name] % BANKS]

        def wait_taken(eng, name):
            eng.wait_ge(taken, unit[name] + 1)

        def wait_etaken(eng, e, u):
            eng.wait_ge(e_taken, e * EU + (u + 2))

        def wait_split_used(eng, job, b):
            eng.wait_ge(split_used, job * EB + (b + 1 + SPLIT))

        A_X, A_Y = 0, 2 + 2 * FB
        A_SILU = [2] + [2 * i + 1 for i in range(1, FB)]
        A_TURN = [2 * i + 4 for i in range(FB - 1)] + [1 + 2 * FB]
        EA = A_Y + 2

        def wait_scalar(eng, job, n):
            eng.wait_ge(e_scalar, job * EA + (n + 1))

        def residual(n, kt):
            return (("x", kt), ("out", 0, kt), ("ffd", kt), ("out", 1, kt))[n]

        def score_tiles(l):
            return (2, 1, 0) if l == 0 else (2, 1)

        def scored(l, h, n):
            return sum(len(score_tiles(i)) * HEADS for i in range(l)) + len(score_tiles(l)) * h + n

        class Steps:

            def __init__(self, eng, semaphore):
                self.eng, self.semaphore, self.n = eng, semaphore, 0

            def did(self, instruction):
                self.n += 1
                instruction.then_inc(self.semaphore, 1)
                return self.n

            def settle(self, n=None):
                self.eng.wait_ge(self.semaphore, self.n if n is None else n)

        def load_params(eng, l):
            r = rows[:, 2 * l, :]
            for at, src in ((C_MIX, norm_mix[l]), (C_FFN, norm_ffn[l]), (C_Q, b_in[l, 0:COL_F]),
                            (C_CONV, b_in[l, COL_CONV:IN_W]), (C_CB, conv_b[l]), (C_LG, conv_ln_g[l]),
                            (C_LB, conv_ln_b[l]), (C_PS, pool_scale[l])):
                v = src.rearrange("(r p) -> r p", p=P)
                eng.dma_start(r[at:at + v.shape[0], :], v).then_inc(s_par[l], 16)
            for at, src in ((C_QN, q_norm), (C_KN, k_norm)):
                for b in range(2):
                    eng.dma_start(r[at:at + 1, b * HD:(b + 1) * HD], src[l:l + 1, :]).then_inc(s_par[l], 16)
            eng.dma_start(rows[0:NT, 2 * l + 1, :], conv_w[l].rearrange("k (c p) -> (k c) p", p=P)).then_inc(s_par[l], 16)
            eng.dma_start(bf_bc[:, l, :], b_in[l:l + 1, COL_F:COL_CONV].broadcast_to([P, HEADS])).then_inc(s_par[l], 16)
            eng.dma_start(wf[:, l], w_in[l][:, COL_F:COL_CONV].rearrange("(k p) n -> p k n", p=P)).then_inc(s_par[l], 16)
            eng.wait_ge(pw_zeroed, 1)
            for g in range(GROUPS):
                b = GW * (g % 2)
                eng.dma_start(pw[b:b + GW, l, g // 2, b:b + GW], pool_w[l, g]).then_inc(s_par[l], 16)

        block = ctx.enter_context(nc.Block())

        @block.sync
        def _(sp):
            sp.dma_start(xload, x[0].rearrange("(j p) n -> p j n", p=P)).then_inc(s_x, 16)
            sp.dma_start(mload, meta).then_inc(s_x, 16)
            for n, (name, src, k, cols_) in enumerate(blocks):
                if n >= RING:
                    wait_used(sp, n - RING)
                dst = ring[:, n % RING, 0:k * cols_].rearrange("p (k n) -> p k n", k=k)
                sp.dma_start(dst, src).then_inc(slot_full[n % RING], 16)

            def expert_block(e, b):
                kind, i, h = ESEQ[b]
                if kind == "d":
                    r = (2 * i + h) * 2 * P
                    src = w_e_down[0][bass.ds(e, 1), r:r + 2 * P, :].rearrange("a (k p) n -> p (a k) n", p=P)
                else:
                    w, r = (w_e_gate if kind == "g" else w_e_up), h * D // 2
                    src = w[0][bass.ds(e, 1), r:r + D // 2, i * BANK:(i + 1) * BANK].rearrange("a (k p) n -> p (a k) n", p=P)
                dst = raw[:, b % RAW, :].rearrange("p (k n) -> p k n", k=2 if kind == "d" else 4)
                sp.dma_start(dst, src).then_inc(landed[b % RAW], 16)

            for b in range(RAW):
                wait_used(sp, last_in_slot[b // 2])
                expert_block(0, b)
            sp.wait_ge(routed, 3)
            last = sp.value_load(n_jobs[0:1, 1:2], min_val=EXPERTS - 1, max_val=MAX_JOBS - 1)
            with sp.Fori(0, last) as job:
                e_up, e_down = (sp.value_load(job_table[0:1, 0, bass.ds(job, 1)], min_val=0, max_val=EXPERTS - 1) for _ in range(2))
                for b in range(RAW, EB):
                    sp.wait_ge(lo_ready, job * EB + (b - RAW + 1))
                    expert_block(e_down if ESEQ[b][0] == "d" else e_up, b)
                e1 = sp.value_load(job_table[0:1, 0, bass.ds(job + 1, 1)], min_val=0, max_val=EXPERTS - 1)
                for b in range(RAW):
                    sp.wait_ge(lo_ready, job * EB + (b + EB - RAW + 1))
                    expert_block(e1, b)
            for b in range(RAW, EB):
                sp.wait_ge(lo_ready, last * EB + (b - RAW + 1))
                expert_block(EXPERTS - 1, b)
            for n, (j, half) in enumerate((j, half) for j in range(2) for half in range(2)):
                wait_etaken(sp, last, U_O + n)
                sp.dma_start(out[0, j * P:(j + 1) * P, half * BANK:(half + 1) * BANK],
                             hacc[:, j, half * BANK:(half + 1) * BANK]).then_inc(s_out, 16)
            sp.wait_ge(s_out, 4 * 16)

        @block.gpsimd
        def _(pool):
            steps = Steps(pool, pool_step)
            pool.memset(ident[:, :], 0.0).then_inc(consts, 1)
            pool.memset(ones[:, :], 1.0).then_inc(consts, 1)
            pool.memset(mean_ones[:, :], 1.0 / CONV_W).then_inc(consts, 1)
            pool.memset(tri[:, :, :], 1.0).then_inc(consts, 1)
            pool.memset(upad[:, :, 0:PAD_C], 0.0).then_inc(consts, 1)
            pool.memset(ppad[:, :, 0:PAD_P], 0.0).then_inc(consts, 1)
            pool.iota(iota_i, pattern=[[1, SLOTS]], base=0, channel_multiplier=0).then_inc(consts, 1)
            pool.wait_ge(consts, 7)
            pool.affine_select(out=ident[:, :], in_=ident[:, :], compare_op=ALU.not_equal, fill=1.0, base=0,
                               pattern=[[-1, P]], channel_multiplier=1).then_inc(consts, 1)
            for i, (t0, _) in enumerate(TOK):
                pool.affine_select(out=tri[:, i, :], in_=tri[:, i, :], compare_op=ALU.is_ge, fill=0.0, base=-t0,
                                   pattern=[[1, L]], channel_multiplier=-1).then_inc(consts, 1)
            pool.tensor_copy(iota_f[:, :], iota_i).then_inc(consts, 1)

            for l in range(1, DEPTH):
                load_params(pool, l)
            pool.dma_start(wr[:, :, :], w_router[0].rearrange("(k p) n -> p k n", p=P)).then_inc(s_par[1], 16)
            pool.dma_start(br_bc[:, :], b_router.broadcast_to([P, EXPERTS])).then_inc(s_par[1], 16)

            for l in range(DEPTH):
                if l > 0:
                    pool.wait_ge(psum_ready, unit["pv", l - 1, HEADS - 1] + 1)
                steps.did(pool.memset(psa[:, :, 0:PAD_P], 0.0))
                steps.did(pool.memset(psb[:, :, 0:PAD_P], 0.0))
                wait_taken(pool, ("pool", l, PT_ - 1))

                def shifted(dst, src, n, tiles):
                    steps.settle()
                    steps.did(pool.tensor_tensor(dst[:, tiles, PAD_P:], src[:, tiles, PAD_P:],
                                                 src[:, tiles, PAD_P - n:PAD_P + L - n], ALU.add))

                shifted(psa, ppad, 1, slice(0, 2))
                shifted(psb, psa, 2, slice(0, 2))
                shifted(psa, psb, 4, slice(1, 2))
                shifted(psb, psa, 8, slice(1, 2))
                for g in range(GROUPS):
                    b, c, w = GW * (g % 2), g // 2, 2 ** (g + 1)
                    total = (psa, psb)[g % 2]
                    steps.settle()
                    steps.did(pool.tensor_scalar(poolo[b:b + GW, c, PAD_P:], total[b:b + GW, c, 2 * PAD_P:], 1.0 / w, None, ALU.mult))
                    if l == 0 and g == 0:
                        pool.wait_ge(rcnt_ready, 1)
                    steps.did(pool.tensor_tensor(poolo[b:b + GW, c, 0:PAD_P], total[b:b + GW, c, PAD_P:2 * PAD_P],
                                                 rcnt[b:b + GW, c, :], ALU.mult))
                steps.settle()
                for c in range(PT_):
                    pool.tensor_tensor(poolo[:, c, :], poolo[:, c, :], ppad[:, c, PAD_P:], ALU.subtract).then_inc(pool_mix, 1)

                wait_taken(pool, ("fbc", l, HEADS - 1))
                steps.did(pool.tensor_copy(fbm[:, :, S_COL[1][0]:S_COL[1][0] + S_COL[1][1]], fbm[:, :, 0:S_COL[1][1]]))
                steps.settle()
                steps.did(pool.tensor_copy(fbm[0:META, :, S_COL[0][0]:S_COL[0][0] + META], fbm[0:META, :, 0:META]))
                steps.settle()
                for j, n in ((0, META), (1, P), (2, P)):
                    c0 = S_COL[j][0] + S_COL[j][1] - n
                    v = fbm[0:n, :, c0:c0 + n]
                    if j > 0:
                        pool.wait_ge(fbm_ready, 3 * l + j)
                    pool.affine_select(out=v, in_=v, compare_op=ALU.is_ge, fill=-NEG, base=0,
                                       pattern=[[0, HEADS], [-1, n]], channel_multiplier=1).then_inc(fbm_ready, 1)

                t0 = tokens_of(l)
                for d in range(KD):
                    wait_taken(pool, ("yp", l, d))
                    steps.did(pool.tensor_tensor(mT[:, d, t0:], gates[:, 0, d, t0:], gates[:, 1, d, t0:], ALU.add))
                    steps.settle()
                    pool.tensor_tensor(mT[:, d, t0:], mT[:, d, t0:], gates[:, 2, d, t0:], ALU.add).then_inc(m_ready, 1)

            pool.wait_ge(psum_ready, unit["pv", DEPTH - 1, HEADS - 1] + 1)
            pool.dma_start(gbc, norm_ffn[DEPTH - 1:DEPTH, :].broadcast_to([P, D])).then_inc(s_gbc, 16)

        @block.tensor
        def _(pe):
            def need(name):
                n = index[name]
                pe.wait_ge(slot_full[n % RING], 16 * (n // RING + 1))

            def project(name, w, c0, rhs, kts, t0=0, out_rows=P):
                bank = free_unit(pe, name)
                for kt in range(kts):
                    mm = nc.tensor.matmul(bank[0:out_rows, t0:L], w[:, kt, c0:c0 + P], rhs(kt), start=(kt == 0), stop=(kt == kts - 1))
                mm.then_inc(psum_ready, 1)

            def norm_sum(name, k):
                bank = free_unit(pe, name)
                for kt in range(KD):
                    pe.wait_ge(sq_ready, k * KD + kt + 1)
                    mm = nc.tensor.matmul(bank[:, 0:L], ones[:, :], sq[:, kt, :], start=(kt == 0), stop=(kt == KD - 1))
                mm.then_inc(psum_ready, 1)

            pe.wait_ge(consts, 12)
            pe.wait_ge(zeroed, BANKS + 3)
            pe.wait_ge(s_x, 32)
            for kt in range(KD):
                bank = free_unit(pe, ("x", kt))
                c = slice(kt * P, (kt + 1) * P)
                nc.tensor.transpose(bank[:, 0:META], mload[:, c], ident[0:META, 0:META])
                for j in range(2):
                    tr = nc.tensor.transpose(bank[:, TOK[j + 1][0]:TOK[j + 1][0] + P], xload[:, j, c], ident[:, :])
                tr.then_inc(psum_ready, 1)
            def turn_params(l):
                pe.wait_ge(s_par[l], 16 * N_PAR[l])
                for n, height in ((2 * l, NA), (2 * l + 1, NT)):
                    bank = free_unit(pe, ("param", n))
                    nc.tensor.transpose(bank[:, 0:height], rows[0:height, n, :], ident[0:height, 0:height]).then_inc(psum_ready, 1)


            for l in range(DEPTH):
                t0 = tokens_of(l)
                norm_sum(("norm", l), 2 * l)
                if l == 0:
                    turn_params(0)

                def normed(kt, c0=0):
                    return hn[:, kt, c0:]

                def wait_normed(kt):
                    pe.wait_ge(hn_ready, 2 * l * KD + kt + 1)
                    return hn[:, kt, :]

                need(("conv", l))
                w = block_ap(("conv", l))
                for i in range(2 * CT):
                    project(("conv", l, i), w, i * P, wait_normed if i == 0 else normed, KD)
                need(("pool", l))
                w = block_ap(("pool", l))
                for i in range(PT_):
                    project(("pool", l, i), w, i * P, normed, KD)
                for part in "qk":
                    need((part, l))
                    w = block_ap((part, l))
                    for i in range(QT):
                        project((part, l, i), w, i * P, normed, KD)
                bank = free_unit(pe, ("mean", l))
                for c in range(CT):
                    pe.wait_ge(conv_done, l * CT + c + 1)
                    mm = nc.tensor.matmul(bank[:, 0:L], mean_ones[:, :], cy[:, c, :], start=(c == 0), stop=(c == CT - 1))
                mm.then_inc(psum_ready, 1)
                if l == 0:
                    turn_params(1)
                need(("v", l))
                w = block_ap(("v", l))
                for i in range(QT):
                    project(("v", l, i), w, i * P, normed, KD)
                bank = free_unit(pe, ("var", l))
                for c in range(CT):
                    pe.wait_ge(centred_sq, l * CT + c + 1)
                    mm = nc.tensor.matmul(bank[:, 0:L], mean_ones[:, :], csq[:, c, :], start=(c == 0), stop=(c == CT - 1))
                mm.then_inc(psum_ready, 1)
                for c in range(PT_):
                    bank = free_unit(pe, ("mix", l, c))
                    pe.wait_ge(pool_mix, l * PT_ + c + 1)
                    nc.tensor.matmul(bank[:, 0:L], pw[:, l, c, :], poolo[:, c, :], start=True, stop=True).then_inc(psum_ready, 1)
                for i in range(2 * QT):
                    bank = free_unit(pe, ("qk_ms", l, i))
                    pe.wait_ge(qk_sq, l * 2 * QT + i + 1)
                    nc.tensor.matmul(bank[:, 0:L], head_ones[:, :], fbm[:, i, 0:L], start=True, stop=True).then_inc(psum_ready, 1)
                bank = free_unit(pe, ("fg", l))
                for j, (a, n) in enumerate(TOK):
                    for kt in range(KD):
                        mm = nc.tensor.matmul(bank[0:n, j * HEADS:(j + 1) * HEADS], hn[:, kt, a:a + n], wf[:, l, kt, :],
                                              start=(kt == 0), stop=(kt == KD - 1))
                mm.then_inc(psum_ready, 1)
                for j, (a, n) in enumerate(TOK):
                    bank = free_unit(pe, ("vtok", l, j))
                    wait_taken(pe, ("v", l, QT - 1))
                    for i in range(QT):
                        tr = nc.tensor.transpose(bank[0:n, i * P:(i + 1) * P], vT[:, i, a:a + n], ident[:, :])
                    tr.then_inc(psum_ready, 1)
                def gate_tile(g):
                    if g % 4 == 0:
                        need(("gate", l, g // 4))
                    project(("gate", l, g), block_ap(("gate", l, g // 4)), g % 4 * P, lambda kt: hn[:, kt, t0:], KD, t0)

                for g in range(GATES_F):
                    gate_tile(g)
                pe.wait_ge(ls_ready, l + 1)
                bank = free_unit(pe, ("ftok", l))
                for j, (a, n) in enumerate(TOK):
                    for i in range(j + 1):
                        m = TOK[i][1]
                        mm = nc.tensor.matmul(bank[0:n, j * HEADS:(j + 1) * HEADS], tri[0:m, i, a:a + n],
                                              ls[0:m, i * HEADS:(i + 1) * HEADS], start=(i == 0), stop=(i == j))
                mm.then_inc(psum_ready, 1)
                bank = free_unit(pe, ("frow", l))
                for i, (a, n) in enumerate(TOK):
                    mm = nc.tensor.matmul(bank[0:HEADS, 0:L], ls[0:n, i * HEADS:(i + 1) * HEADS], tri[0:n, i, :],
                                          start=(i == 0), stop=(i == 2))
                mm.then_inc(psum_ready, 1)
                gate_tile(GATES_F)
                for h in range(HEADS):
                    bank = free_unit(pe, ("fbc", l, h))
                    if h == 0:
                        wait_taken(pe, ("frow", l))
                    nc.tensor.matmul(bank[:, 0:L], ident[0:HEADS, h:h + 1].broadcast_to([HEADS, P]), frow[:, :],
                                     start=True, stop=True).then_inc(psum_ready, 1)

                for g in range(GATES_F + 1, GATES_H):
                    gate_tile(g)

                def scores(h):
                    b, i = HD * (h % 2), h // 2
                    bank = free_unit(pe, ("s", l, h))
                    if h == 0:
                        pe.wait_ge(qk_ready, (l + 1) * 2 * QT)
                    for j in score_tiles(l):
                        a, n = TOK[j]
                        c0, keys = S_COL[j]
                        mm = nc.tensor.matmul(bank[0:n, c0:c0 + keys], qkT[b:b + HD, i, a:a + n], qkT[b:b + HD, QT + i, 0:keys],
                                              start=True, stop=True)
                    mm.then_inc(psum_ready, 1)

                def turn_probs(h):
                    s = sc[:, h % 2, :]
                    c2, c1, c0 = S_COL[2][0], S_COL[1][0], S_COL[0][0]
                    bank = free_unit(pe, ("pt", l, h))
                    pe.wait_ge(probs_ready, scored(l, h + 1, 0))
                    nc.tensor.transpose(bank[:, 0:P], s[:, c1 + META:c1 + META + P], ident[:, :])
                    nc.tensor.transpose(bank[:, P:2 * P], s[:, c2 + META:c2 + META + P], ident[:, :])
                    nc.tensor.transpose(bank[:, 2 * P:3 * P], s[:, c2 + META + P:c2 + L], ident[:, :]).then_inc(psum_ready, 1)
                    bank = free_unit(pe, ("ptm", l, h))
                    if l == 0:
                        nc.tensor.transpose(bank[0:META, 0:META], s[0:META, c0:c0 + META], ident[0:META, 0:META])
                    nc.tensor.transpose(bank[0:META, META:META + P], s[:, c1:c1 + META], ident[:, :])
                    nc.tensor.transpose(bank[0:META, META + P:L], s[:, c2:c2 + META], ident[:, :]).then_inc(psum_ready, 1)

                def values(h):
                    b, c = HD * (h % 2), slice(h * HD, (h + 1) * HD)
                    bank = free_unit(pe, ("pv", l, h))
                    wait_taken(pe, ("ptm", l, h))
                    nc.tensor.matmul(bank[b:b + HD, t0:L], vtok[0:META, 0, c], ptm[:, t0:L], start=True, stop=False)
                    nc.tensor.matmul(bank[b:b + HD, META:L], vtok[:, 1, c], pt[:, 0:2 * P], start=False, stop=False)
                    nc.tensor.matmul(bank[b:b + HD, META + P:L], vtok[:, 2, c], pt[:, 2 * P:3 * P], start=False,
                                     stop=True).then_inc(psum_ready, 1)

                for h in range(HEADS):
                    scores(h)
                    gate_tile(GATES_H + 2 * h)
                    if h > 0:
                        values(h - 1)
                    gate_tile(GATES_H + 2 * h + 1)
                    turn_probs(h)
                values(HEADS - 1)

                for d in range(KD):
                    if d == 0:
                        need(("attn_o", l))
                        wait_taken(pe, ("pv", l, HEADS - 1))
                    project(("ya", l, d), block_ap(("attn_o", l)), d * P, lambda i: attT[:, i, t0:], QT, t0)
                    if d == 0:
                        need(("conv_o", l))
                        pe.wait_ge(conv_act, (l + 1) * CT)
                    project(("yc", l, d), block_ap(("conv_o", l)), d * P, lambda i: csq[:, i, t0:], CT, t0)
                    if d == 0:
                        need(("pool_o", l))
                    project(("yp", l, d), block_ap(("pool_o", l)), d * P, lambda i: poolo[:, i, t0:], PT_, t0)

                def mixed(kt):
                    pe.wait_ge(m_ready, l * KD + kt + 1)
                    return mT[:, kt, t0:]

                for d in range(KD):
                    if d % 4 == 0:
                        need(("out", l, d // 4))
                    project(("out", l, d), block_ap(("out", l, d // 4)), d % 4 * P,
                            mixed if d == 0 else lambda kt: mT[:, kt, t0:], KD, t0)

                if l == 0:
                    norm_sum(("norm", "ffn"), 1)

                    def ffn_normed(kt):
                        pe.wait_ge(hn_ready, KD + kt + 1)
                        return hn[:, kt, :]

                    for f in range(FT):
                        for part, name in (("ff_gate", "ffg"), ("ff_up", "ffu")):
                            if f % 4 == 0:
                                need((part, f // 4))
                            project((name, f), block_ap((part, f // 4)), f % 4 * P, ffn_normed if f == 0 else normed, KD)
                    for half in range(2):
                        banks = []
                        for k in range(KB):
                            need(("ff_down", half, k))
                            w = block_ap(("ff_down", half, k))
                            ks = min(8, FT - 8 * k)
                            for d in range(4):
                                if k == 0:
                                    banks.append(free_unit(pe, ("ffd", 4 * half + d)))
                                for kt in range(ks):
                                    f = 8 * k + kt
                                    if half == 0 and d == 0:
                                        wait_taken(pe, ("ffu", f))
                                    mm = nc.tensor.matmul(banks[d][:, 0:L], w[:, kt, d * P:(d + 1) * P], hidden[:, f, :],
                                                          start=(f == 0), stop=(f == FT - 1))
                                if k == KB - 1:
                                    mm.then_inc(psum_ready, 1)
                            if k < KB - 1:
                                mm.then_inc(down_used, 1)

            for n in range(4):
                j, half = n // 2, n % 2
                a = TOK[j + 1][0]
                bank = free_unit(pe, ("htok", n))
                for d in range(4):
                    if j == 0:
                        wait_taken(pe, residual(3, 4 * half + d))
                    tr = nc.tensor.transpose(bank[:, d * P:(d + 1) * P], hT[:, 4 * half + d, a:a + P], ident[:, :])
                tr.then_inc(psum_ready, 1)
            bank = free_unit(pe, ("logit",))
            pe.wait_ge(wrg_ready, 1)
            for j in range(2):
                a = TOK[j + 1][0]
                for kt in range(KD):
                    mm = nc.tensor.matmul(bank[:, j * EXPERTS:(j + 1) * EXPERTS], hT[:, kt, a:a + P], wrg[:, kt, :],
                                          start=(kt == 0), stop=(kt == KD - 1))
            mm.then_inc(psum_ready, 1)
            bank = free_unit(pe, ("pos",))
            pe.wait_ge(mask_ready, 2)
            for c, terms in enumerate((((strict, 0),), ((ones[:, :], 0), (strict, 1)), ((ones[:, :], 0), (ones[:, :], 1)))):
                if c == 2:
                    mm.then_inc(split_used, SPLIT)
                for n, (lhs, j) in enumerate(terms):
                    mm = nc.tensor.matmul(bank[:, c * EXPERTS:(c + 1) * EXPERTS], lhs, mask[:, j, 0:EXPERTS],
                                          start=(n == 0), stop=(n == len(terms) - 1))
            mm.then_inc(psum_ready, 1)

            pe.wait_ge(routed, 3)
            pe.wait_ge(xs_ready, 1)
            pe.wait_ge(taken, NU)
            jobs = pe.value_load(n_jobs[0:1, 0:1], min_val=EXPERTS, max_val=MAX_JOBS)

            def split_matmuls(bank, terms, w_h, w_l, first, last):
                n, total = 0, 3 * len(terms)
                for which in range(2):
                    for x_h, x_l, k, c in terms:
                        for lhs in ((x_h, x_l), (x_h,))[which]:
                            w = (w_h, w_l)[which]
                            mm = nc.tensor.matmul(bank[:, :], lhs, w[:, k, c:c + BANK], start=(first and n == 0), stop=(last and n == total - 1))
                            n += 1
                return mm

            with pe.Fori(0, jobs) as job:
                def block_split(b):
                    pe.wait_ge(lo_ready, job * EB + (b + 1))

                pe.wait_ge(sel_ready, job * 4 + 4)
                wait_etaken(pe, job, -1)
                for u in range(2):
                    bank = psum[4 + u]
                    for d in range(4):
                        kt = 4 * u + d
                        for j in range(2):
                            mm = nc.tensor.matmul(bank[:, d * P:(d + 1) * P], xs[:, j, kt * P:(kt + 1) * P],
                                                  psel[:, j, :], start=(j == 0), stop=(j == 1))
                    mm.then_inc(e_full, 1)
                for j in range(2):
                    tr = nc.tensor.transpose(psum[3][:, j * P:(j + 1) * P], pgat[:, j, :], ident[:, :])
                tr.then_inc(e_full, 1)

                def product(kind, i, bank):
                    for h in range(2):
                        b = epos[kind, i, h]
                        block_split(b)
                        terms = [(xg_hi[:, k * P:(k + 1) * P], xg_lo[:, k * P:(k + 1) * P], k - 4 * h, 0) for k in range(4 * h, 4 * h + 4)]
                        split_matmuls(bank, terms, weight_rows(w_hi, b), weight_rows(w_lo, b), h == 0, h == 1).then_inc(split_used, 1)

                def turn(i):
                    wait_etaken(pe, job, U_H + 2 * i)
                    for f in range(4):
                        tr = nc.tensor.transpose(psum[3][:, f * P:(f + 1) * P], hid[:, f * P:(f + 1) * P], ident[:, :])
                    tr.then_inc(e_full, 1)

                def down(i):
                    wait_etaken(pe, job, U_T + 2 * i)
                    for h in range(2):
                        b = epos["d", i, h]
                        block_split(b)
                        for half in range(2):
                            terms = [(act_hi[:, f * P:(f + 1) * P], act_lo[:, f * P:(f + 1) * P], f - 2 * h, half * BANK)
                                     for f in range(2 * h, 2 * h + 2)]
                            mm = split_matmuls(psum[6 + half], terms, weight_rows(w_hi, b), weight_rows(w_lo, b),
                                               i == 0 and h == 0, i == FB - 1 and h == 1)
                        mm.then_inc(split_used, 1)

                wait_etaken(pe, job, 1)
                for i in range(FB):
                    product("g", i, psum[i % 2])
                    if i > 0:
                        turn(i - 1)
                    product("u", i, psum[2])
                    if i > 0:
                        down(i - 1)
                turn(FB - 1)
                down(FB - 1)
                wait_etaken(pe, job, U_PG)
                for u in range(4):
                    j, half = u // 2, u % 2
                    if u < 2:
                        wait_scalar(pe, job, A_Y + half)
                    else:
                        wait_etaken(pe, job, U_O + u - 2)
                    nc.tensor.matmul(psum[4 + u % 2][:, :], pgT[:, j * P:(j + 1) * P], ytok[:, half * BANK:(half + 1) * BANK],
                                     start=True, stop=True).then_inc(e_full, 1)

        @block.scalar
        def _(act_e):
            a_ = nc.scalar.activation
            steps = Steps(act_e, act_step)
            load_params(act_e, 0)

            def root(n):
                wait_taken(act_e, (("norm", 0), ("norm", "ffn"), ("norm", 1))[n])
                a_(rms[:, 0, :], rms[:, 0, :], ACT.Sqrt).then_inc(root_ready, 1)

            def squares(n):
                for kt in range(KD):
                    wait_taken(act_e, residual(n, kt))
                    a_(sq[:, kt, :], hT[:, kt, :], ACT.Square).then_inc(sq_ready, 1)

            for l in range(DEPTH):
                t0 = tokens_of(l)
                squares(2 * l)
                root(2 * l)
                for c in range(CT):
                    wait_taken(act_e, ("conv", l, CT + c))
                    a_(conv_in[:, CT + c, :], conv_in[:, CT + c, :], ACT.Sigmoid).then_inc(glu_gate, 1)
                for i in range(2 * QT):
                    wait_taken(act_e, ("qk"[i // QT], l, i % QT))
                    a_(fbm[:, i, 0:L], qkT[:, i, :], ACT.Square).then_inc(qk_sq, 1)
                wait_taken(act_e, ("mean", l))
                for c in range(CT):
                    a_(csq[:, c, :], cy[:, c, :], ACT.Square).then_inc(centred_sq, 1)
                wait_taken(act_e, ("var", l))
                a_(rms[:, 1, :], rms[:, 1, :], ACT.Sqrt).then_inc(ln_root, 1)
                for c in range(CT):
                    act_e.wait_ge(ln_scaled, l * CT + c + 1)
                    a_(csq[:, c, :], cy[:, c, :], ACT.Silu, bias=pcol(l, C_LB + c)).then_inc(conv_act, 1)
                for i in range(2 * QT):
                    wait_taken(act_e, ("qk_ms", l, i))
                    a_(silu[:, i % 2, :], rms[:, i % 2, :], ACT.Sqrt).then_inc(qk_root, 1)
                wait_taken(act_e, ("fg", l))
                steps.did(a_(fga[:, :], fg[:, :], ACT.Abs))
                steps.settle()
                steps.did(a_(fge[:, :], fga[:, :], ACT.Exp, scale=-1.0))
                steps.settle()
                a_(fgl[:, :], fge[:, :], ACT.Ln, bias=ones[:, 0:1]).then_inc(fg_log, 1)
                for h in range(HEADS):
                    s = sc[:, h % 2, :]
                    for n, j in enumerate(score_tiles(l)):
                        m, (c0, keys) = TOK[j][1], S_COL[j]
                        act_e.wait_ge(max_ready, scored(l, h, n) + 1)
                        a_(s[0:m, c0:c0 + keys], s[0:m, c0:c0 + keys], ACT.Exp, bias=nmax[0:m, h % 2, j:j + 1],
                           accum_out=rsum[0:m, h % 2, j:j + 1]).then_inc(exp_ready, 1)
                    act_e.wait_ge(rinv_ready, l * HEADS + h + 1)
                    for j in score_tiles(l):
                        m, (c0, keys) = TOK[j][1], S_COL[j]
                        a_(s[0:m, c0:c0 + keys], s[0:m, c0:c0 + keys], ACT.Copy,
                           scale=rinv[0:m, h % 2, j:j + 1]).then_inc(probs_ready, 1)
                wait_taken(act_e, ("gate", l, GT - 1))
                for d in range(KD):
                    a_(gates[:, :, d, t0:], gates[:, :, d, t0:], ACT.Sigmoid).then_inc(gate_ready, 1)
                if l == 0:
                    squares(1)
                    root(1)
                    for f in range(FT):
                        bank = ready_unit(act_e, ("ffg", f))
                        if f >= 2:
                            wait_taken(act_e, ("ffu", f - 2))
                        a_(silu[:, f % 2, :], bank[:, 0:L], ACT.Silu).then_inc(silu_ready, 1)

            for j in range(2):
                wait_taken(act_e, ("htok", 2 * j + 1))
                if j > 0:
                    act_e.wait_ge(ss_ready, j)
                a_(tok_sq, hacc[:, j, :], ACT.Square, accum_out=ss[:, j:j + 1]).then_inc(ss_ready, 1)
            act_e.wait_ge(sms_ready, 1)
            a_(srt[:, :], sms[:, :], ACT.Sqrt).then_inc(srt_ready, 1)
            act_e.wait_ge(gap_ready, 1)
            a_(pexp[:, :], gap[:, :], ACT.Exp).then_inc(pexp_ready, 1)

            act_e.wait_ge(routed, 3)
            jobs = act_e.value_load(n_jobs[0:1, 0:1], min_val=EXPERTS, max_val=MAX_JOBS)
            with act_e.Fori(0, jobs) as job:
                split = [0]

                def high_parts(upto):
                    for b in range(split[0], min(upto + 1, EB)):
                        act_e.wait_ge(landed[b % RAW], job * (16 * (EB // RAW)) + 16 * (b // RAW + 1))
                        wait_split_used(act_e, job, b - SPLIT)
                        a_(w_hi[:, b % SPLIT, :], raw[:, b % RAW, :], ACT.Copy).then_inc(hi_ready, 1)
                        split[0] = b + 1

                high_parts(1)
                for u in range(2):
                    act_e.wait_ge(e_full, job * EF + (u + 1))
                    a_(xg_hi[:, u * BANK:(u + 1) * BANK], psum[4 + u][:, :], ACT.Copy).then_inc(e_scalar, 1)
                for i in range(FB + 1):
                    if i < FB:
                        end = epos["g", i, 1]
                        high_parts(end + 2)
                        wait_split_used(act_e, job, end)
                        a_(esilu[:, i % 2, :], psum[i % 2][:, :], ACT.Silu).then_inc(e_scalar, 1)
                    if i == FB:
                        high_parts(EB - 1)
                    if i > 0:
                        act_e.wait_ge(e_full, job * EF + (F_T + i))
                        a_(act_hi[:, :], psum[3][:, :], ACT.Copy).then_inc(e_scalar, 1)
                for half in range(2):
                    wait_split_used(act_e, job, EB - 1)
                    a_(ytok[:, half * BANK:(half + 1) * BANK], psum[6 + half][:, :], ACT.Copy).then_inc(e_scalar, 1)

        @block.vector
        def _(dve):
            v = nc.vector
            steps = Steps(dve, dve_step)
            freed = [0]

            def frees(name, instruction, count=1):
                assert unit[name] == freed[0], (name, freed[0])
                freed[0] += count
                instruction.then_inc(taken, count)

            v.memset(pw[:, :, :, :].rearrange("p l c n -> p (l c n)"), 0.0).then_inc(pw_zeroed, 1)
            for i in range(BANKS):
                v.memset(psum[i][:, :], 0.0).then_inc(zeroed, 1)
            v.memset(fg[:, :], 0.0).then_inc(zeroed, 1)
            steps.did(v.memset(head_ones[:, :], 0.0))
            steps.settle()
            for b in range(2):
                v.memset(head_ones[b * HD:(b + 1) * HD, b * HD:(b + 1) * HD], 1.0).then_inc(zeroed, 1)
            steps.did(v.memset(rsum[:, :, :], 1.0))
            for t in (pos, mask, comb):
                steps.did(v.memset(t[:, :, :], 0.0))
            dve.wait_ge(consts, 12)
            for g in range(GROUPS):
                b = GW * (g % 2)
                steps.did(v.tensor_scalar(rcnt[b:b + GW, g // 2, :], iota_f[b:b + GW, 0:PAD_P], 1.0, 2.0 ** (g + 1), ALU.add, ALU.min))
            steps.settle()
            v.reciprocal(rcnt[:, :, :], rcnt[:, :, :]).then_inc(rcnt_ready, 1)

            for kt in range(KD):
                bank = ready_unit(dve, ("x", kt))
                frees(("x", kt), v.tensor_copy(hT[:, kt, :], bank[:, 0:L]))
            def take_params(l):
                for n in (2 * l, 2 * l + 1):
                    bank = ready_unit(dve, ("param", n))
                    height = (NA, NT)[n % 2]
                    frees(("param", n), v.tensor_copy(par[:, n, 0:height], bank[:, 0:height]))
                wait_taken(dve, ("param", 2 * l + 1))

            def norm(name, n, l, gain):
                bank = ready_unit(dve, name)
                frees(name, v.tensor_scalar(rms[:, 0, :], bank[:, 0:L], 1.0 / D, EPS_RMS, ALU.mult, ALU.add))
                if n == 0:
                    take_params(0)
                dve.wait_ge(root_ready, n + 1)
                steps.did(v.reciprocal(rstd[:, 0, :], rms[:, 0, :]))
                steps.settle()
                for kt in range(KD):
                    v.scalar_tensor_tensor(hn[:, kt, :], hT[:, kt, :], pcol(l, gain + kt), rstd[:, 0, :], ALU.mult, ALU.mult)\
                     .then_inc(hn_ready, 1)

            for l in range(DEPTH):
                t0 = tokens_of(l)
                norm(("norm", l), 2 * l, l, C_MIX)

                for i in range(2 * CT):
                    bank = ready_unit(dve, ("conv", l, i))
                    frees(("conv", l, i), v.tensor_scalar(conv_in[:, i, :], bank[:, 0:L], pcol(l, C_CONV + i), None, ALU.add))
                for i in range(PT_):
                    bank = ready_unit(dve, ("pool", l, i))
                    frees(("pool", l, i), v.tensor_scalar(ppad[:, i, PAD_P:], bank[:, 0:L], pcol(l, C_POOL + i), None, ALU.add))
                last = [0] * CT
                for c in range(CT):
                    dve.wait_ge(glu_gate, l * CT + c + 1)
                    last[c] = steps.did(v.tensor_tensor(upad[:, c, PAD_C:], conv_in[:, c, :], conv_in[:, CT + c, :], ALU.mult))

                def taps(first, count):
                    for t in range(first, min(first + count, TAPS)):
                        for c in range(CT):
                            steps.settle(last[c])
                            if t == 0:
                                last[c] = steps.did(v.tensor_scalar(cy[:, c, :], upad[:, c, 0:L], tap(l, 0, c), pcol(l, C_CB + c),
                                                                    ALU.mult, ALU.add))
                                continue
                            ins = v.scalar_tensor_tensor(cy[:, c, :], upad[:, c, t:t + L], tap(l, t, c), cy[:, c, :], ALU.mult, ALU.add)
                            if t < TAPS - 1:
                                last[c] = steps.did(ins)
                            else:
                                ins.then_inc(conv_done, 1)

                per = -(-TAPS // (2 * QT - 1))
                for i in range(2 * QT):
                    name = ("qk"[i // QT], l, i % QT)
                    bank = ready_unit(dve, name)
                    frees(name, v.tensor_scalar(qkT[:, i, :], bank[:, 0:L], pcol(l, C_Q + i), None, ALU.add))
                    taps(i * per, per)
                bank = ready_unit(dve, ("mean", l))
                dve.wait_ge(conv_done, (l + 1) * CT)
                v.tensor_tensor(cy[:, 0, :], cy[:, 0, :], bank[:, 0:L], ALU.subtract)
                frees(("mean", l), v.tensor_tensor(cy[:, 1, :], cy[:, 1, :], bank[:, 0:L], ALU.subtract))
                if l == 0:
                    take_params(1)
                for i in range(QT):
                    bank = ready_unit(dve, ("v", l, i))
                    frees(("v", l, i), v.tensor_scalar(vT[:, i, :], bank[:, 0:L], pcol(l, C_V + i), None, ALU.add))
                bank = ready_unit(dve, ("var", l))
                frees(("var", l), v.tensor_scalar(rms[:, 1, :], bank[:, 0:L], EPS_LN, None, ALU.add))
                dve.wait_ge(ln_root, l + 1)
                steps.did(v.reciprocal(rstd[:, 1, :], rms[:, 1, :]))
                steps.settle()
                for c in range(CT):
                    v.scalar_tensor_tensor(cy[:, c, :], cy[:, c, :], pcol(l, C_LG + c), rstd[:, 1, :], ALU.mult, ALU.mult).then_inc(ln_scaled, 1)
                for c in range(PT_):
                    bank = ready_unit(dve, ("mix", l, c))
                    frees(("mix", l, c), v.tensor_scalar(poolo[:, c, :], bank[:, 0:L], pcol(l, C_PS + c), None, ALU.mult))

                steps.did(v.tensor_scalar(qgain[:, 0:1], pcol(l, C_QN), float(HD) ** -0.5, None, ALU.mult))
                steps.did(v.tensor_copy(qgain[:, 1:2], pcol(l, C_KN)))
                for i in range(2 * QT):
                    bank = ready_unit(dve, ("qk_ms", l, i))
                    frees(("qk_ms", l, i), v.tensor_scalar(rms[:, i % 2, :], bank[:, 0:L], 1.0 / HD, EPS_RMS, ALU.mult, ALU.add))
                    dve.wait_ge(qk_root, l * 2 * QT + i + 1)
                    steps.did(v.reciprocal(rstd[:, i % 2, :], silu[:, i % 2, :]))
                    steps.settle()
                    v.scalar_tensor_tensor(qkT[:, i, :], qkT[:, i, :], qgain[:, i // QT:i // QT + 1], rstd[:, i % 2, :],
                                           ALU.mult, ALU.mult).then_inc(qk_ready, 1)

                def take_gate(g):
                    bank = ready_unit(dve, ("gate", l, g))
                    frees(("gate", l, g), v.tensor_scalar(gates[:, g // KD, g % KD, t0:], bank[:, t0:L], pcol(l, C_GATE + g), None, ALU.add))

                bank = ready_unit(dve, ("fg", l))
                v.tensor_tensor(fg[0:META, 0:HEADS], bank[0:META, 0:HEADS], bf_bc[0:META, l, :], ALU.add)
                v.tensor_tensor(fg[:, HEADS:2 * HEADS], bank[:, HEADS:2 * HEADS], bf_bc[:, l, :], ALU.add)
                frees(("fg", l), v.tensor_tensor(fg[:, 2 * HEADS:], bank[:, 2 * HEADS:3 * HEADS], bf_bc[:, l, :], ALU.add))
                for j, (_, n) in enumerate(TOK):
                    bank = ready_unit(dve, ("vtok", l, j))
                    if j == 0:
                        dve.wait_ge(pool_mix, (l + 1) * PT_)
                    frees(("vtok", l, j), v.tensor_copy(vtok[0:n, j, :], bank[0:n, 0:ATT_W]))
                dve.wait_ge(fg_log, l + 1)
                v.scalar_tensor_tensor(ls[:, :], fg[:, :], 0.0, fgl[:, :], ALU.min, ALU.subtract).then_inc(ls_ready, 1)
                for g in range(GATES_F):
                    take_gate(g)
                bank = ready_unit(dve, ("ftok", l))
                v.tensor_copy(ftok[0:META, 0:HEADS], bank[0:META, 0:HEADS])
                frees(("ftok", l), v.tensor_copy(ftok[:, HEADS:], bank[:, HEADS:3 * HEADS]))
                bank = ready_unit(dve, ("frow", l))
                frees(("frow", l), v.tensor_copy(frow[:, :], bank[0:HEADS, 0:L]))
                take_gate(GATES_F)
                for h in range(HEADS):
                    bank = ready_unit(dve, ("fbc", l, h))
                    frees(("fbc", l, h), v.tensor_copy(fbm[:, h, 0:L], bank[:, 0:L]))

                def take_values(h):
                    b = HD * (h % 2)
                    bank = ready_unit(dve, ("pv", l, h))
                    frees(("pv", l, h), v.tensor_copy(attT[b:b + HD, h // 2, t0:], bank[b:b + HD, t0:L]))

                for g in range(GATES_F + 1, GATES_H):
                    take_gate(g)
                dve.wait_ge(fbm_ready, (l + 1) * 3)
                for h in range(HEADS):
                    bank = ready_unit(dve, ("s", l, h))
                    tiles = score_tiles(l)
                    for j in tiles:
                        m, (c0, keys) = TOK[j][1], S_COL[j]
                        ins = v.scalar_tensor_tensor(sc[0:m, h % 2, c0:c0 + keys], bank[0:m, c0:c0 + keys],
                                                     ftok[0:m, j * HEADS + h:j * HEADS + h + 1], fbm[0:m, h, c0:c0 + keys],
                                                     ALU.add, ALU.subtract)
                    frees(("s", l, h), ins)
                    wait_taken(dve, ("s", l, h))
                    for j in tiles:
                        m, (c0, keys) = TOK[j][1], S_COL[j]
                        v.tensor_reduce(nmax[0:m, h % 2, j:j + 1], sc[0:m, h % 2, c0:c0 + keys], AX_X, ALU.max, negate=True).then_inc(max_ready, 1)
                    take_gate(GATES_H + 2 * h)
                    dve.wait_ge(exp_ready, scored(l, h + 1, 0))
                    v.reciprocal(rinv[:, h % 2, :], rsum[:, h % 2, :]).then_inc(rinv_ready, 1)
                    if h > 0:
                        take_values(h - 1)
                    take_gate(GATES_H + 2 * h + 1)
                    bank = ready_unit(dve, ("pt", l, h))
                    frees(("pt", l, h), v.tensor_copy(pt[:, :], bank[:, 0:3 * P]))
                    bank = ready_unit(dve, ("ptm", l, h))
                    frees(("ptm", l, h), v.tensor_copy(ptm[:, t0:], bank[0:META, t0:L]))
                take_values(HEADS - 1)

                for d in range(KD):
                    dve.wait_ge(gate_ready, l * KD + d + 1)
                    for b, name in enumerate(("ya", "yc", "yp")):
                        bank = ready_unit(dve, (name, l, d))
                        g = gates[:, b, d, t0:]
                        frees((name, l, d), v.tensor_tensor(g, bank[:, t0:L], g, ALU.mult))
                for d in range(KD):
                    bank = ready_unit(dve, ("out", l, d))
                    frees(("out", l, d), v.tensor_tensor(hT[:, d, t0:], bank[:, t0:L], hT[:, d, t0:], ALU.add))
                if l == 0:
                    norm(("norm", "ffn"), 1, 0, C_FFN)
                    for f in range(FT):
                        dve.wait_ge(silu_ready, f + 1)
                        bank = ready_unit(dve, ("ffu", f))
                        frees(("ffg", f), v.tensor_tensor(hidden[:, f, :], bank[:, 0:L], silu[:, f % 2, :], ALU.mult), 2)
                    for d in range(KD):
                        bank = ready_unit(dve, ("ffd", d))
                        frees(("ffd", d), v.tensor_tensor(hT[:, d, :], bank[:, 0:L], hT[:, d, :], ALU.add))

            steps.did(v.tensor_tensor(wrg[:, :, :], wr[:, :, :],
                                      par[:, 2 * (DEPTH - 1), C_FFN:C_FFN + KD].unsqueeze(2).broadcast_to([P, KD, EXPERTS]), ALU.mult))
            v.tensor_copy(lg[:, :, :], pos[:, :, 0:8]).then_inc(wrg_ready, 1)
            for n in range(4):
                j, half = n // 2, n % 2
                bank = ready_unit(dve, ("htok", n))
                frees(("htok", n), v.tensor_copy(hacc[:, j, half * BANK:(half + 1) * BANK], bank[:, :]))
            for t in (cum, jobf):
                steps.did(v.memset(t[:, :, :], 0.0))
            dve.wait_ge(ss_ready, 2)
            v.tensor_scalar(sms[:, :], ss[:, :], 1.0 / D, EPS_RMS, ALU.mult, ALU.add).then_inc(sms_ready, 1)
            dve.wait_ge(srt_ready, 1)
            steps.did(v.reciprocal(srs[:, :], srt[:, :]))
            steps.settle()
            bank = ready_unit(dve, ("logit",))
            v.scalar_tensor_tensor(lg[:, 0, :], bank[:, 0:EXPERTS], srs[:, 0:1], br_bc[:, :], ALU.mult, ALU.add)
            frees(("logit",), v.scalar_tensor_tensor(lg[:, 1, :], bank[:, EXPERTS:2 * EXPERTS], srs[:, 1:2], br_bc[:, :], ALU.mult, ALU.add))
            wait_taken(dve, ("logit",))
            for j in range(2):
                steps.did(v.max(mx[:, j, :], lg[:, j, :]))
            steps.settle()
            v.tensor_tensor(gap[:, :], mx[:, :, 1], mx[:, :, 0], ALU.subtract).then_inc(gap_ready, 1)
            for j in range(2):
                steps.did(v.max_index(mi[:, j, :], mx[:, j, :], lg[:, j, :]))
            steps.settle()
            steps.did(v.tensor_copy(mif[:, :, :], mi[:, :, :]))
            steps.settle()
            for j in range(2):
                steps.did(v.tensor_scalar(oh0[:, j, :], iota_f[:, 0:EXPERTS], mif[:, j, 0:1], None, ALU.is_equal))
                steps.did(v.tensor_scalar(oh1[:, j, :], iota_f[:, 0:EXPERTS], mif[:, j, 1:2], None, ALU.is_equal))
            steps.settle()
            for j in range(2):
                v.tensor_tensor(mask[:, j, 0:EXPERTS], oh0[:, j, :], oh1[:, j, :], ALU.add).then_inc(mask_ready, 1)
            dve.wait_ge(pexp_ready, 1)
            steps.did(v.tensor_scalar(pden[:, :], pexp[:, :], 1.0, None, ALU.add))
            steps.settle()
            steps.did(v.reciprocal(pr0[:, :], pden[:, :]))
            steps.settle()
            steps.did(v.tensor_tensor(pr1[:, :], pexp[:, :], pr0[:, :], ALU.mult))
            for j in range(2):
                steps.did(v.tensor_scalar(comb[:, j, 0:EXPERTS], oh0[:, j, :], pr0[:, j:j + 1], None, ALU.mult))
            steps.settle()
            for j in range(2):
                v.scalar_tensor_tensor(comb[:, j, 0:EXPERTS], oh1[:, j, :], pr1[:, j:j + 1], comb[:, j, 0:EXPERTS], ALU.mult, ALU.add)\
                 .then_inc(comb_ready, 1)
            bank = ready_unit(dve, ("pos",))
            v.tensor_copy(pos[:, :, 0:EXPERTS], bank[:, 0:2 * EXPERTS].rearrange("p (j e) -> p j e", j=2)).then_inc(routed, 1)
            steps.did(v.tensor_scalar(cum[:, 0, EXPERTS:], bank[:, 2 * EXPERTS:3 * EXPERTS], float(P), 1.0, ALU.is_gt, ALU.add))
            for n in range(3):
                steps.settle()
                steps.did(v.tensor_tensor(cum[:, n + 1, EXPERTS:], cum[:, n, EXPERTS:], cum[:, n, EXPERTS - 2 ** n:2 * EXPERTS - 2 ** n], ALU.add))
            steps.settle()
            v.tensor_copy(n_jobs[:, 0:1], cum[:, 3, 2 * EXPERTS - 1:])
            v.tensor_scalar(n_jobs[:, 1:2], cum[:, 3, 2 * EXPERTS - 1:], -1.0, None, ALU.add).then_inc(routed, 1)
            steps.did(v.tensor_tensor(cmp[:, :, :], iota_f[:, 0:TABLE].unsqueeze(2).broadcast_to([P, TABLE, EXPERTS]),
                                      cum[:, 3, EXPERTS:].unsqueeze(1).broadcast_to([P, TABLE, EXPERTS]), ALU.is_ge))
            steps.settle()
            steps.did(v.tensor_reduce(jobf[:, 0, :], cmp[:, :, :], AX_X, ALU.add))
            steps.settle()
            steps.did(v.tensor_tensor(jobf[:, 1, 1:], jobf[:, 0, 1:], jobf[:, 0, 0:TABLE - 1], ALU.is_equal))
            steps.settle()
            v.tensor_copy(job_table[:, :, :], jobf[:, :, :]).then_inc(routed, 1)
            dve.wait_ge(s_gbc, 16)
            for j in range(2):
                ins = v.scalar_tensor_tensor(xs[:, j, :], hacc[:, j, :], srs[:, j:j + 1], gbc, ALU.mult, ALU.mult)
                if j == 0:
                    ins.then_inc(xs_ready, 1)
            frees(("pos",), ins)
            dve.wait_ge(routed, 3)
            dve.wait_ge(comb_ready, 2)
            assert freed[0] == NU

            def select(e, part):
                for dst, src in ((psel, mask), (pgat, comb)):
                    for j in range(2):
                        v.tensor_scalar(dst[:, j, :], iota_f[:, bass.ds(part * P, P)], pos[:, j, bass.ds(e, 1)], src[:, j, bass.ds(e, 1)],
                                        ALU.is_equal, ALU.mult).then_inc(sel_ready, 1)

            select(0, 0)
            v.tensor_copy(lg[:, :, :], pos[:, :, 0:8]).then_inc(e_taken, 1)
            jobs = dve.value_load(n_jobs[0:1, 0:1], min_val=EXPERTS, max_val=MAX_JOBS)
            with dve.Fori(0, jobs) as job:
                split = [0]

                def low_parts(upto):
                    for b in range(split[0], min(upto + 1, EB)):
                        dve.wait_ge(hi_ready, job * EB + (b + 1))
                        v.tensor_tensor(w_lo[:, b % SPLIT, :], raw[:, b % RAW, :], w_hi[:, b % SPLIT, :].bitcast(F32),
                                        ALU.subtract).then_inc(lo_ready, 1)
                        split[0] = b + 1

                def unit_ready(n):
                    dve.wait_ge(e_full, job * EF + (n + 1))

                low_parts(0)
                for u in range(2):
                    wait_scalar(dve, job, A_X + u)
                    c = slice(u * BANK, (u + 1) * BANK)
                    v.tensor_tensor(xg_lo[:, c], psum[4 + u][:, :], xg_hi[:, c].bitcast(F32), ALU.subtract).then_inc(e_taken, 1)
                unit_ready(F_PG)
                v.tensor_copy(pgT, psum[3][:, 0:SEQ]).then_inc(e_taken, 1)
                for i in range(FB + 1):
                    if i > 0:
                        low_parts(epos["g", i, 1] + 2 if i < FB else EB - 2)
                        wait_scalar(dve, job, A_TURN[i - 1])
                        v.tensor_tensor(act_lo[:, :], psum[3][:, :], act_hi[:, :].bitcast(F32), ALU.subtract).then_inc(e_taken, 1)
                    if i < FB:
                        end = epos["u", i, 1]
                        low_parts(end + 2)
                        wait_split_used(dve, job, end)
                        wait_scalar(dve, job, A_SILU[i])
                        v.tensor_tensor(hid, psum[2][:, :], esilu[:, i % 2, :], ALU.mult).then_inc(e_taken, 1)
                low_parts(EB - 1)
                e = dve.value_load(job_table[0:1, 0, bass.ds(job + 1, 1)], min_val=0, max_val=EXPERTS)
                part = dve.value_load(job_table[0:1, 1, bass.ds(job + 1, 1)], min_val=0, max_val=1)
                select(e, part)
                for u in range(4):
                    unit_ready(F_O + u)
                    h = hacc[:, u // 2, u % 2 * BANK:(u % 2 + 1) * BANK]
                    v.tensor_tensor(h, psum[4 + u % 2][:, :], h, ALU.add).then_inc(e_taken, 1)


_INS = ["x", "meta", "norm_mix", "w_in", "b_in", "q_norm", "k_norm", "w_attn_o", "conv_w", "conv_b", "conv_ln_g",
        "conv_ln_b", "w_conv_o", "pool_w", "pool_scale", "w_pool_o", "w_out", "norm_ffn", "w_ff_gate", "w_ff_up",
        "w_ff_down", "w_router", "b_router", "w_e_gate", "w_e_up", "w_e_down"]


def kernel(**inputs):
    import concourse.bacc as bacc
    from concourse.bass_utils import run_bass_kernel_spmd

    nc = bacc.Bacc("TRN2", target_bir_lowering=False, num_devices=1)
    arrays, args = {}, []
    for name in _INS:
        a = np.ascontiguousarray(inputs[name])
        arrays[f"in_{name}"] = a
        args.append(nc.dram_tensor(f"in_{name}", a.shape, mybir.dt.from_np(a.dtype), kind="ExternalInput").ap())
    out = nc.dram_tensor("out_y", inputs["x"].shape, F32, kind="ExternalOutput").ap()
    trunk_program(nc, *args, out)
    r = run_bass_kernel_spmd(nc, [arrays], core_ids=[0])
    return r.results[0]["out_y"]
```

```python
from contextlib import ExitStack

import numpy as np

import concourse.bass as bass
from concourse import mybir

ALU = mybir.AluOpType
ACT = mybir.ActivationFunctionType
F32 = mybir.dt.float32
F32R = mybir.dt.float32r
I32 = mybir.dt.int32
U32 = mybir.dt.uint32
AX_X = mybir.AxisListType.X

P = 128
BANK = 512
BANKS = 8


def trunk_program(nc, x, meta, norm_mix, w_in, b_in, q_norm, k_norm, w_attn_o, conv_w, conv_b, conv_ln_g,
                  conv_ln_b, w_conv_o, pool_w, pool_scale, w_pool_o, w_out, norm_ffn, w_ff_gate, w_ff_up,
                  w_ff_down, w_router, b_router, w_e_gate, w_e_up, w_e_down, out):
    _, SEQ, D = x.shape
    META = meta.shape[0]
    DEPTH, _, IN_W = w_in.shape
    HD = q_norm.shape[1]
    ATT_W = w_attn_o.shape[1]
    HEADS = ATT_W // HD
    TAPS, CONV_W = conv_w.shape[1:]
    GROUPS, GW = pool_w.shape[1:3]
    POOL_W = GROUPS * GW
    D_FF = w_ff_gate.shape[2]
    EXPERTS, D_FE = w_e_gate.shape[1], w_e_gate.shape[3]
    L = META + SEQ
    assert DEPTH == 2 and SEQ == 2 * P and META == 16 and 2 * HD == P and 2 * GW == P

    KD = D // P
    QT = ATT_W // P
    CT = CONV_W // P
    PT_ = POOL_W // P
    GT = 3 * KD
    FT = D_FF // P
    ET = D_FE // P
    COL_F = 3 * ATT_W
    COL_CONV = COL_F + HEADS
    COL_POOL = COL_CONV + 2 * CONV_W
    COL_GATE = COL_POOL + POOL_W
    PAD_C = TAPS - 1
    PAD_P = 16
    EPS_RMS, EPS_LN = 1e-6, 1e-5
    NEG = -1e30
    TOK = [(0, META), (META, P), (META + P, P)]
    S_COL = {2: (0, L), 1: (L, META + P), 0: (L + META + P, META)}
    SW = L + META + P + META
    SLOTS = SEQ

    HB = 2048
    blocks = []
    for l in range(DEPTH):
        def cols(w, c0, n):
            return w[:, c0:c0 + n].rearrange("(k p) n -> p k n", p=P), w.shape[0] // P, n

        def pairs(part, w, c0, tiles):
            for i in range(tiles // 2):
                blocks.append(((part, l, i), *cols(w, c0 + i * 2 * P, 2 * P)))

        pairs("conv", w_in[l], COL_CONV, 2 * CT)
        pairs("pool", w_in[l], COL_POOL, PT_)
        for i, part in enumerate("qkv"):
            pairs(part, w_in[l], i * ATT_W, QT)
        pairs("gate", w_in[l], COL_GATE, GT)
        blocks.append((("conv_o", l), *cols(w_conv_o[l], 0, D)))
        blocks.append((("pool_o", l), *cols(w_pool_o[l], 0, D)))
        for i in range(2):
            blocks.append((("attn_o", l, i), *cols(w_attn_o[l], i * D // 2, D // 2)))
        pairs("out", w_out[l], 0, KD)
        if l == 0:
            for i in range(FT // 2):
                blocks.append((("ff_gate", i), *cols(w_ff_gate[0], i * 2 * P, 2 * P)))
                blocks.append((("ff_up", i), *cols(w_ff_up[0], i * 2 * P, 2 * P)))
            for half in range(2):
                for k in range(0, FT, 4):
                    n = min(4, FT - k)
                    blocks.append((("ff_down", half, k // 4), *cols(w_ff_down[0][k * P:(k + n) * P, :], half * D // 2, D // 2)))
    assert FT % 2 == 0
    RING = 3
    index = {b[0]: n for n, b in enumerate(blocks)}
    NB = len(blocks)
    RAW, SPLIT = 7, 3
    FB = ET // 4
    ESEQ = []
    for i in range(FB):
        ESEQ += [(kind, i, h) for kind in "gu" for h in range(2)]
        ESEQ += [("d", i - 1, h) for h in range(2)] if i else []
    ESEQ += [("d", FB - 1, h) for h in range(2)]
    EB = len(ESEQ)
    epos = {b: n for n, b in enumerate(ESEQ)}
    assert EB % RAW == 0 and EB % SPLIT == 0
    MAX_JOBS = EXPERTS + 2 * SEQ // (P + 1)
    TABLE = MAX_JOBS + 1

    order = []
    GATES_F, GATES_H = 2, GT - 2 * HEADS
    QK = [i + b for i in range(QT) for b in (0, QT)]
    QK_AFTER = [QK[0:1], QK[1:2], QK[2:3], [], QK[3:4], QK[4:5], QK[5:6], QK[6:8]]
    QK_LATE = 2
    assert 2 * QT == 8 == GATES_H == len(QK_AFTER)
    for kt in range(KD):
        order.append(("x", kt))
    for l in range(DEPTH):
        order += [("norm", l)] + ([("param", 0), ("param", 1)] if l == 0 else [])
        order += [("conv", l, i) for i in range(2 * CT)] + [("pool", l, i) for i in range(PT_)]
        order += [("q", l, i) for i in range(QT)] + [("k", l, i) for i in range(QT)]
        order += [("v", l, 0), ("v", l, 1), ("mean", l)] + ([("param", 2), ("param", 3)] if l == 0 else [])
        order += [("v", l, i) for i in range(2, QT)]
        order += [("var", l)] + [("mix", l, i) for i in range(PT_)]
        order += [("fg", l)] + [("vtok", l, j) for j in range(3)]
        for g in range(GATES_H):
            order += [("gate", l, g)] + [("qk_ms", l, i) for i in QK_AFTER[g]]
            order += [("ftok", l), ("frow", l)] if g == GATES_F else []
            order += [("fbc", l, h) for h in range(HEADS)] if g == GATES_F + 1 else []
        for h in range(HEADS):
            order += [("s", l, h), ("gate", l, GATES_H + 2 * h)]
            order += [("pv", l, h - 1)] if h else []
            order += [("gate", l, GATES_H + 2 * h + 1), ("pt", l, h), ("ptm", l, h)]
        order += [("yc", l, d) for d in range(KD)] + [("pv", l, HEADS - 1)]
        order += [("yp", l, d) for d in range(KD)] + [("ya", l, d) for d in range(KD)]
        order += [("out", l, d) for d in range(KD)]
        if l == 0:
            order += [("norm", "ffn")]
            for f in range(0, FT, 2):
                order += [("ffg", f), ("ffg", f + 1), ("ffu", f), ("ffu", f + 1)]
            order += [("ffd", d) for d in range(KD)]
    order += [("htok", n) for n in range(4)] + [("logit",), ("pos",)]
    unit = {name: n for n, name in enumerate(order)}
    NU = len(order)
    F_PG, F_T = 2, 3
    EF = F_T + FB
    U_PG, U_H, U_T = 2, 3, 4
    EU = 3 + 2 * FB

    ctx = ExitStack()
    with ctx:
        def sb(name, shape, dt=F32):
            return ctx.enter_context(nc.sbuf_tensor(name, shape, dt))

        def sem(name):
            return ctx.enter_context(nc.semaphore(name))

        psum = [ctx.enter_context(nc.psum_tensor(f"bank{i}", [P, BANK], F32)) for i in range(BANKS)]

        w_hi = sb("w_hi", [P, SPLIT, HB], F32R)
        w_lo = sb("w_lo", [P, SPLIT, HB], F32R)
        hT = sb("hT", [P, KD, L])
        ident = sb("ident", [P, P])
        ones = sb("ones", [P, P])
        mean_ones = sb("mean_ones", [P, P])
        head_ones = sb("head_ones", [P, P])
        tri = sb("tri", [P, 3, L])
        strict = tri[:, 1, META - 1:META - 1 + P]
        iota_f = sb("iota_f", [P, SLOTS])
        rcnt = sb("rcnt", [P, PT_, PAD_P])
        NA = 2 * KD + 3 * QT + 2 * CT + PT_ + GT + 3 * CT + PT_ + 2
        NT = TAPS * CT
        par = sb("par", [P, 2 * DEPTH, P])
        bf_bc = sb("bf_bc", [P, DEPTH, HEADS])
        wf = sb("wf", [P, DEPTH, KD, HEADS])
        pw = sb("pw", [P, DEPTH, PT_, P])
        wr = sb("wr", [P, KD, EXPERTS])
        wrg = sb("wrg", [P, KD, EXPERTS])
        br_bc = sb("br_bc", [P, EXPERTS])
        fg = sb("fg", [P, 3 * HEADS])
        fga = sb("fga", [P, 3 * HEADS])
        fge = sb("fge", [P, 3 * HEADS])
        fgl = sb("fgl", [P, 3 * HEADS])
        ls = sb("ls", [P, 3 * HEADS])
        ftok = sb("ftok", [P, 3 * HEADS])
        frow = sb("frow", [HEADS, L])
        qgain = sb("qgain", [P, 2])
        nmax = sb("nmax", [P, 2, 3])
        rsum = sb("rsum", [P, 2, 3])
        rinv = sb("rinv", [P, 2, 3])

        job_table = sb("job_table", [P, 2, TABLE], I32)
        n_jobs = sb("n_jobs", [P, 2], I32)
        small = {n: sb(n, [P, 2]) for n in ("ss", "sms", "srt", "srs", "gap", "pexp", "pden", "pr0", "pr1")}
        ss, sms, srt, srs, gap, pexp, pden, pr0, pr1 = (small[n] for n in small)
        lg = sb("lg", [P, 2, 8])
        mx = sb("mx", [P, 2, 8])
        mi = sb("mi", [P, 2, 8], U32)
        mif = sb("mif", [P, 2, 8])
        oh0 = sb("oh0", [P, 2, EXPERTS])
        oh1 = sb("oh1", [P, 2, EXPERTS])
        comb = sb("comb", [P, 2, 2 * EXPERTS])
        mask = sb("mask", [P, 2, 2 * EXPERTS])
        pos = sb("pos", [P, 2, 2 * EXPERTS])

        base = -(-nc.sbuf_base // 32) * 32
        top = {}

        def at(plan, name, shape, dt=F32, over=None):
            start = top.get(plan, base) if over is None else where[over]
            where[name] = start
            top[plan] = max(top.get(plan, base), -(-(start + 4 * int(np.prod(shape[1:]))) // 32) * 32)
            return nc.alloc_sbuf_tensor_at(name, shape, dt, offset=start)

        where = {}
        raw = at("experts", "raw", [P, RAW, HB])
        top["mixers"] = top["ffn"] = base + 4 * RING * HB
        gates = at("mixers", "gates", [P, 3, KD, L])
        qkT = at("mixers", "qkT", [P, 2 * QT, L])
        fbm = at("mixers", "fbm", [P, HEADS, SW])
        mT = qkT
        hn = at("mixers", "hn", [P, KD, L], over="gates")
        load_at = at("mixers", "loaded", [P, 3 * D], over="fbm")
        xload = load_at[:, 0:2 * D].rearrange("p (j n) -> p j n", j=2)
        qk_squares = gates[:, 2, :, :]
        mload = load_at[0:META, 2 * D:3 * D]
        hid_hi = at("ffn", "hid_hi", [P, FT, L], F32R)
        hid_lo = at("ffn", "hid_lo", [P, FT, L], F32R)
        assert top["ffn"] <= top["mixers"]
        hn_hi = at("mixers", "hn_hi", [P, KD, L], F32R)
        hn_lo = at("mixers", "hn_lo", [P, KD, L], F32R)
        m_hi, m_lo = hn_hi, hn_lo
        vT = at("mixers", "vT", [P, QT, L])
        att_hi = at("mixers", "att_hi", [P, QT, L], F32R, over="vT")
        att_lo = at("mixers", "att_lo", [P, QT, L], F32R)
        vtok = at("mixers", "vtok", [P, 3, ATT_W])
        psa = at("mixers", "psa", [P, PT_, PAD_P + L], over="vtok")
        where["psb"] = where["psa"] + 4 * PT_ * (PAD_P + L)
        psb = at("mixers", "psb", [P, PT_, PAD_P + L], over="psb")
        conv_in = at("mixers", "conv_in", [P, 2 * CT, L])
        conv_hi = at("mixers", "conv_hi", [P, CT, L], F32R, over="conv_in")
        where["conv_lo"] = where["conv_in"] + 4 * CT * L
        conv_lo = at("mixers", "conv_lo", [P, CT, L], F32R, over="conv_lo")
        cy = at("mixers", "cy", [P, CT, L])
        csq = at("mixers", "csq", [P, CT, L])
        poolo = at("mixers", "poolo", [P, PT_, L])
        hid = at("mixers", "hidden", [P, CT, L], over="cy")
        sq = at("mixers", "sq", [P, KD, L], over="conv_in")
        assert KD == 4 * CT
        sc = at("mixers", "sc", [P, 2, SW], over="cy")
        where["pt"] = where["cy"] + 4 * 2 * SW
        pt = at("mixers", "pt", [P, 3 * P], over="pt")
        pool_hi = at("mixers", "pool_hi", [P, PT_, L], F32R)
        pool_lo = at("mixers", "pool_lo", [P, PT_, L], F32R)
        upad = at("mixers", "upad", [P, CT, PAD_C + L])
        ppad = at("mixers", "ppad", [P, PT_, PAD_P + L])
        ptm = at("mixers", "ptm", [META, L])
        rms = at("mixers", "rms", [P, 2, L])
        rstd = at("mixers", "rstd", [P, 2, L])
        silu = at("mixers", "silu", [P, 2, L])
        iota_i = rms[:, :, :].rearrange("p a t -> p (a t)")[:, 0:SLOTS].bitcast(I32)
        rows = silu[:, :, :].rearrange("p a t -> p (a t)")[:, 0:2 * DEPTH * P].rearrange("p (r n) -> p r n", n=P)

        hacc = at("experts", "hacc", [P, 2, D])
        gain_bc = at("experts", "gain_bc", [P, D])
        gbc = gain_bc[:, :]
        xs = at("experts", "xs", [P, 2, D])
        ehid = at("experts", "ehid", [P, BANK])
        esilu = at("experts", "esilu", [P, 2, BANK])
        ytok = at("experts", "ytok", [P, D])
        tok_sq = ytok[:, :]
        psel = at("experts", "psel", [P, 2, P])
        pgat = at("experts", "pgat", [P, 2, P])
        xg_hi = at("experts", "xg_hi", [P, D], F32R)
        xg_lo = at("experts", "xg_lo", [P, D], F32R)
        act_hi = at("experts", "act_hi", [P, 2, BANK], F32R)
        act_lo = at("experts", "act_lo", [P, 2, BANK], F32R)
        cum = at("experts", "cum", [P, 4, 2 * EXPERTS])
        cmp = at("experts", "cmp", [P, TABLE, EXPERTS])
        jobf = at("experts", "jobf", [P, 2, TABLE])
        pgT = tri[:, :, :].rearrange("p a t -> p (a t)")[:, 0:SEQ]
        assert max(top.values()) <= nc.sbuf_usable_end

        s_x = sem("x_loaded")
        s_par = [sem(f"params_loaded{l}") for l in range(DEPTH)]
        s_out = sem("out_written")
        s_gbc = sem("ffn_gain_loaded")
        slot_full = [sem(f"slot_full{i}") for i in range(RING)]
        block_high = sem("block_high_part")
        block_low = sem("block_low_part")
        hn_raw = sem("normed_whole")
        hn_high = sem("normed_high_part")
        conv_split = sem("conv_split")
        pool_split = sem("pool_split")
        att_high = sem("values_high_part")
        m_raw = sem("mixed_whole")
        m_high = sem("mixed_high_part")
        hid_high = sem("hidden_high_part")
        hid_ready = sem("hidden_ready")
        landed = [sem(f"expert_block_landed{i}") for i in range(RAW)]
        psum_ready = sem("psum_ready")
        taken = sem("units_taken")
        down_used = sem("down_block_used")
        zeroed = sem("psum_zeroed")
        pw_zeroed = sem("pool_blocks_zeroed")
        rcnt_ready = sem("window_counts_ready")
        consts = sem("consts_built")
        pool_step = sem("pool_step")
        dve_step = sem("dve_step")
        act_step = sem("act_step")
        sq_ready = sem("squares_ready")
        root_ready = sem("root_ready")
        hn_ready = sem("normed_ready")
        glu_gate = sem("glu_gate")
        conv_done = sem("conv_done")
        centred_sq = sem("centred_sq")
        ln_root = sem("ln_root")
        ln_scaled = sem("ln_scaled")
        conv_act = sem("conv_act")
        pool_mix = sem("pool_mix")
        qk_sq = sem("qk_sq")
        qk_root = sem("qk_root")
        qk_ready = sem("qk_ready")
        fg_log = sem("forget_log")
        ls_ready = sem("log_sigmoid_ready")
        fbm_ready = sem("decay_masked")
        max_ready = sem("max_ready")
        exp_ready = sem("exp_ready")
        rinv_ready = sem("rinv_ready")
        probs_ready = sem("probs_ready")
        gate_ready = sem("gate_ready")
        m_ready = sem("mixed_ready")
        silu_ready = sem("silu_ready")
        ss_ready = sem("token_square_ready")
        sms_ready = sem("token_ms_ready")
        srt_ready = sem("token_root_ready")
        xs_ready = sem("tokens_normed")
        wrg_ready = sem("router_ready")
        gap_ready = sem("top_gap_ready")
        pexp_ready = sem("top_exp_ready")
        mask_ready = sem("mask_ready")
        routed = sem("routed")
        comb_ready = sem("combine_ready")
        sel_ready = sem("selection_ready")
        e_full = sem("expert_unit_ready")
        e_taken = sem("expert_units_taken")
        hi_ready = sem("high_part_ready")
        lo_ready = sem("low_part_ready")
        split_used = sem("split_block_used")
        e_scalar = sem("expert_scalar_step")
        scattered = sem("results_scattered")
        added = sem("results_added")

        N_PAR = [15, 15 + 2]

        def tokens_of(l):
            return 0 if l == 0 else META

        class Splitter:

            def __init__(self, make):
                self.make, self.n = make, 0

            def before(self, name):
                while self.n < NB and splittable(self.n) < (unit[name] if name else NU):
                    self.make(self.n)
                    self.n += 1

        def block_shape(t, slot, n):
            return t[:, slot, 0:blocks[n][2] * blocks[n][3]]

        def weight_rows(t, b):
            return t[:, b % SPLIT, :].rearrange("p (k n) -> p k n", k=2 if ESEQ[b][0] == "d" else 4)

        def block_parts(name):
            n = index[name]
            _, _, k, c = blocks[n]
            return [w[:, n % SPLIT, 0:k * c].rearrange("p (k n) -> p k n", k=k) for w in (w_hi, w_lo)]

        C_MIX, C_FFN = 0, KD
        C_Q = 2 * KD
        C_K = C_Q + QT
        C_V = C_K + QT
        C_CONV = C_V + QT
        C_POOL = C_CONV + 2 * CT
        C_GATE = C_POOL + PT_
        C_CB = C_GATE + GT
        C_LG = C_CB + CT
        C_LB = C_LG + CT
        C_PS = C_LB + CT
        C_QN = C_PS + PT_
        C_KN = C_QN + 1
        assert C_KN + 1 == NA <= P and NT <= P

        def pcol(l, c):
            return par[:, 2 * l, c:c + 1]

        def tap(l, t, c):
            return par[:, 2 * l + 1, CT * t + c:CT * t + c + 1]

        last_unit = {}
        down_used_at = {}
        for l in range(DEPTH):
            for part, tiles in (("conv", 2 * CT), ("pool", PT_), ("q", QT), ("k", QT), ("v", QT), ("gate", GT), ("out", KD)):
                for i in range(tiles // 2):
                    last_unit[part, l, i] = (part, l, 2 * i + 1)
            last_unit["conv_o", l] = ("yc", l, KD - 1)
            last_unit["pool_o", l] = ("yp", l, KD - 1)
            for i in range(2):
                last_unit["attn_o", l, i] = ("ya", l, 4 * i + 3)
        for i in range(FT // 2):
            last_unit["ff_gate", i] = ("ffg", 2 * i + 1)
            last_unit["ff_up", i] = ("ffu", 2 * i + 1)
        KB = (FT + 3) // 4
        for half in range(2):
            last_unit["ff_down", half, KB - 1] = ("ffd", 4 * half + 3)
            for k in range(KB - 1):
                down_used_at["ff_down", half, k] = half * (KB - 1) + k + 1

        def splittable(n):
            if n < SPLIT:
                return (unit["x", KD // 2], unit["x", KD - 1], unit["norm", 0])[n] + 0.5
            name = blocks[n - SPLIT][0]
            if name in down_used_at:
                return unit["ffd", 4 * name[1]] - 1 + (name[2] + 1) / (KB + 1)
            return unit[last_unit[name]]

        def wait_used(eng, n):
            name = blocks[n][0]
            if name in down_used_at:
                eng.wait_ge(down_used, down_used_at[name])
            else:
                eng.wait_ge(psum_ready, unit[last_unit[name]] + 1)

        def free_unit(eng, name):
            n = unit[name]
            if n >= BANKS:
                eng.wait_ge(taken, n - BANKS + 1)
            return psum[n % BANKS]

        def ready_unit(eng, name):
            eng.wait_ge(psum_ready, unit[name] + 1)
            return psum[unit[name] % BANKS]

        def wait_taken(eng, name):
            eng.wait_ge(taken, unit[name] + 1)

        def wait_etaken(eng, e, u):
            eng.wait_ge(e_taken, e * EU + (u + 2))

        def wait_split_used(eng, job, b):
            eng.wait_ge(split_used, job * EB + (b + 1 + SPLIT))

        A_X, A_Y = 0, 2 + 2 * FB
        A_SILU = [2] + [2 * i + 1 for i in range(1, FB)]
        A_TURN = [2 * i + 4 for i in range(FB - 1)] + [1 + 2 * FB]
        EA = A_Y + 2

        def wait_scalar(eng, job, n):
            eng.wait_ge(e_scalar, job * EA + (n + 3))

        def residual(n, kt):
            return (("x", kt), ("out", 0, kt), ("ffd", kt), ("out", 1, kt))[n]

        def score_tiles(l):
            return (2, 1, 0) if l == 0 else (2, 1)

        def scored(l, h, n):
            return sum(len(score_tiles(i)) * HEADS for i in range(l)) + len(score_tiles(l)) * h + n

        class Steps:

            def __init__(self, eng, semaphore):
                self.eng, self.semaphore, self.n = eng, semaphore, 0

            def did(self, instruction):
                self.n += 1
                instruction.then_inc(self.semaphore, 1)
                return self.n

            def settle(self, n=None):
                self.eng.wait_ge(self.semaphore, self.n if n is None else n)

        def load_params(eng, l):
            r = rows[:, 2 * l, :]
            for at, src in ((C_MIX, norm_mix[l]), (C_FFN, norm_ffn[l]), (C_Q, b_in[l, 0:COL_F]),
                            (C_CONV, b_in[l, COL_CONV:IN_W]), (C_CB, conv_b[l]), (C_LG, conv_ln_g[l]),
                            (C_LB, conv_ln_b[l]), (C_PS, pool_scale[l])):
                v = src.rearrange("(r p) -> r p", p=P)
                eng.dma_start(r[at:at + v.shape[0], :], v).then_inc(s_par[l], 16)
            for at, src in ((C_QN, q_norm), (C_KN, k_norm)):
                eng.dma_start(r[at:at + 1, :].rearrange("o (b n) -> o b n", b=2), src[l:l + 1, :].unsqueeze(1).broadcast_to([1, 2, HD])).then_inc(s_par[l], 16)
            eng.dma_start(rows[0:NT, 2 * l + 1, :], conv_w[l].rearrange("k (c p) -> (k c) p", p=P)).then_inc(s_par[l], 16)
            eng.dma_start(bf_bc[:, l, :], b_in[l:l + 1, COL_F:COL_CONV].broadcast_to([P, HEADS])).then_inc(s_par[l], 16)
            eng.dma_start(wf[:, l], w_in[l][:, COL_F:COL_CONV].rearrange("(k p) n -> p k n", p=P)).then_inc(s_par[l], 16)
            eng.wait_ge(pw_zeroed, 1)
            for odd in range(2):
                b = GW * odd
                eng.dma_start(pw[b:b + GW, l, :, b:b + GW], pool_w[l].rearrange("(c h) i j -> h i c j", h=2)[odd]).then_inc(s_par[l], 16)

        block = ctx.enter_context(nc.Block())

        @block.sync
        def _(sp):
            sp.dma_start(xload, x[0].rearrange("(j p) n -> p j n", p=P)).then_inc(s_x, 16)
            sp.dma_start(mload, meta).then_inc(s_x, 16)
            for n, (name, src, k, cols_) in enumerate(blocks):
                if n >= RING:
                    sp.wait_ge(block_low, n - RING + 1)
                dst = block_shape(raw, n % RING, n).rearrange("p (k n) -> p k n", k=k)
                sp.dma_start(dst, src).then_inc(slot_full[n % RING], 16)
                if n == 0:
                    load_params(sp, 0)
                if n == 2 * RING:
                    for l in range(1, DEPTH):
                        load_params(sp, l)
                    sp.dma_start(wr[:, :, :], w_router[0].rearrange("(k p) n -> p k n", p=P)).then_inc(s_par[1], 16)
                    sp.dma_start(br_bc[:, :], b_router.broadcast_to([P, EXPERTS])).then_inc(s_par[1], 16)

            def expert_block(e, b):
                kind, i, h = ESEQ[b]
                if kind == "d":
                    r = (2 * i + h) * 2 * P
                    src = w_e_down[0][bass.ds(e, 1), r:r + 2 * P, :].rearrange("a (k p) n -> p (a k) n", p=P)
                else:
                    w, r = (w_e_gate if kind == "g" else w_e_up), h * D // 2
                    src = w[0][bass.ds(e, 1), r:r + D // 2, i * BANK:(i + 1) * BANK].rearrange("a (k p) n -> p (a k) n", p=P)
                dst = raw[:, b % RAW, :].rearrange("p (k n) -> p k n", k=2 if kind == "d" else 4)
                sp.dma_start(dst, src).then_inc(landed[b % RAW], 16)

            for b in range(RAW):
                if b < RING:
                    sp.wait_ge(block_low, max(n for n in range(NB) if n % RING == b) + 1)
                elif b == RING:
                    sp.wait_ge(psum_ready, unit["out", DEPTH - 1, 0] + 1)
                    sp.dma_start(gbc, norm_ffn[DEPTH - 1:DEPTH, :].broadcast_to([P, D])).then_inc(s_gbc, 16)
                expert_block(0, b)
            sp.wait_ge(routed, 3)
            last = sp.value_load(n_jobs[0:1, 1:2], min_val=EXPERTS - 1, max_val=MAX_JOBS - 1)
            with sp.Fori(0, last) as job:
                e_up, e_down = (sp.value_load(job_table[0:1, 0, bass.ds(job, 1)], min_val=0, max_val=EXPERTS - 1) for _ in range(2))
                for b in range(RAW, EB):
                    sp.wait_ge(lo_ready, job * EB + (b - RAW + 1))
                    expert_block(e_down if ESEQ[b][0] == "d" else e_up, b)
                e1 = sp.value_load(job_table[0:1, 0, bass.ds(job + 1, 1)], min_val=0, max_val=EXPERTS - 1)
                for b in range(RAW):
                    sp.wait_ge(lo_ready, job * EB + (b + EB - RAW + 1))
                    expert_block(e1, b)
            for b in range(RAW, EB):
                sp.wait_ge(lo_ready, last * EB + (b - RAW + 1))
                expert_block(EXPERTS - 1, b)
            for n, (j, half) in enumerate((j, half) for j in range(2) for half in range(2)):
                sp.wait_ge(added, last * 4 + (4 + n + 1))
                sp.dma_start(out[0, j * P:(j + 1) * P, half * BANK:(half + 1) * BANK],
                             hacc[:, j, half * BANK:(half + 1) * BANK]).then_inc(s_out, 16)
            sp.wait_ge(s_out, 4 * 16)

        @block.gpsimd
        def _(pool):
            steps = Steps(pool, pool_step)
            pool.memset(ident[:, :], 0.0).then_inc(consts, 1)
            pool.memset(ones[:, :], 1.0).then_inc(consts, 1)
            pool.memset(mean_ones[:, :], 1.0 / CONV_W).then_inc(consts, 1)
            pool.memset(tri[:, :, :], 1.0).then_inc(consts, 1)
            pool.memset(upad[:, :, 0:PAD_C], 0.0).then_inc(consts, 1)
            pool.memset(ppad[:, :, 0:PAD_P], 0.0).then_inc(consts, 1)
            pool.iota(iota_i, pattern=[[1, SLOTS]], base=0, channel_multiplier=0).then_inc(consts, 1)
            pool.wait_ge(consts, 7)
            pool.affine_select(out=ident[:, :], in_=ident[:, :], compare_op=ALU.not_equal, fill=1.0, base=0,
                               pattern=[[-1, P]], channel_multiplier=1).then_inc(consts, 1)
            for i, (t0, _) in enumerate(TOK):
                pool.affine_select(out=tri[:, i, :], in_=tri[:, i, :], compare_op=ALU.is_ge, fill=0.0, base=-t0,
                                   pattern=[[1, L]], channel_multiplier=-1).then_inc(consts, 1)
            pool.tensor_copy(iota_f[:, :], iota_i).then_inc(consts, 1)

            def low_part(n):
                if n == 0:
                    pool.wait_ge(block_low, 1)
                    return
                pool.wait_ge(block_high, n + 1)
                pool.tensor_tensor(block_shape(w_lo, n % SPLIT, n), block_shape(raw, n % RING, n),
                                   block_shape(w_hi, n % SPLIT, n).bitcast(F32), ALU.subtract).then_inc(block_low, 1)

            split = Splitter(low_part)

            for l in range(DEPTH):
                if l > 0:
                    split.before(("norm", l))
                    pool.wait_ge(psum_ready, unit["norm", l] + 1)
                steps.did(pool.memset(psa[:, :, 0:PAD_P], 0.0))
                steps.did(pool.memset(psb[:, :, 0:PAD_P], 0.0))
                split.before(("pool", l, PT_ - 1))
                wait_taken(pool, ("pool", l, PT_ - 1))

                def shifted(dst, src, n, tiles):
                    steps.settle()
                    steps.did(pool.tensor_tensor(dst[:, tiles, PAD_P:], src[:, tiles, PAD_P:],
                                                 src[:, tiles, PAD_P - n:PAD_P + L - n], ALU.add))

                split.before(("q", l, 0))
                shifted(psa, ppad, 1, slice(0, 2))
                shifted(psb, psa, 2, slice(0, 2))
                split.before(("q", l, 2))
                shifted(psa, psb, 4, slice(1, 2))
                shifted(psb, psa, 8, slice(1, 2))
                split.before(("k", l, 0))
                for g in range(GROUPS):
                    b, c, w = GW * (g % 2), g // 2, 2 ** (g + 1)
                    total = (psa, psb)[g % 2]
                    steps.settle()
                    steps.did(pool.tensor_scalar(poolo[b:b + GW, c, PAD_P:], total[b:b + GW, c, 2 * PAD_P:], 1.0 / w, None, ALU.mult))
                    if l == 0 and g == 0:
                        pool.wait_ge(rcnt_ready, 1)
                    steps.did(pool.tensor_tensor(poolo[b:b + GW, c, 0:PAD_P], total[b:b + GW, c, PAD_P:2 * PAD_P],
                                                 rcnt[b:b + GW, c, :], ALU.mult))
                    if g % 2:
                        steps.settle()
                        split.before((("k", l, 2), ("v", l, 0))[g // 2])
                        pool.wait_ge(block_low, split.n)
                steps.settle()
                for c in range(PT_):
                    pool.tensor_tensor(poolo[:, c, :], poolo[:, c, :], ppad[:, c, PAD_P:], ALU.subtract).then_inc(pool_mix, 1)

                split.before(("fbc", l, HEADS - 1))
                wait_taken(pool, ("fbc", l, HEADS - 1))
                steps.did(pool.tensor_copy(fbm[:, :, S_COL[1][0]:S_COL[1][0] + S_COL[1][1]], fbm[:, :, 0:S_COL[1][1]]))
                steps.settle()
                steps.did(pool.tensor_copy(fbm[0:META, :, S_COL[0][0]:S_COL[0][0] + META], fbm[0:META, :, 0:META]))
                steps.settle()
                for j, n in ((0, META), (1, P), (2, P)):
                    c0 = S_COL[j][0] + S_COL[j][1] - n
                    v = fbm[0:n, :, c0:c0 + n]
                    if j > 0:
                        pool.wait_ge(fbm_ready, 3 * l + j)
                    pool.affine_select(out=v, in_=v, compare_op=ALU.is_ge, fill=-NEG, base=0,
                                       pattern=[[0, HEADS], [-1, n]], channel_multiplier=1).then_inc(fbm_ready, 1)

            split.before(None)

        @block.tensor
        def _(pe):
            def need(name):
                pe.wait_ge(block_low, index[name] + 1)

            def project(name, w, c0, rhs, kts, t0=0):
                bank = free_unit(pe, name)
                for kt in range(kts):
                    x_h, x_l = rhs(kt)
                    for n, (w_part, x) in enumerate(((w[0], x_h), (w[0], x_l), (w[1], x_h))):
                        mm = nc.tensor.matmul(bank[:, t0:L], w_part[:, kt, c0:c0 + P], x, start=(kt == 0 and n == 0), stop=(kt == kts - 1 and n == 2))
                mm.then_inc(psum_ready, 1)

            def projects(part, l, first, last, rhs, t0=0):
                for i in range(first, last):
                    if i % 2 == 0:
                        need((part, l, i // 2))
                    project((part, l, i), block_parts((part, l, i // 2)), i % 2 * P, rhs[0] if i == first else rhs[1], KD, t0)

            def norm_sum(name, k):
                bank = free_unit(pe, name)
                for kt in range(KD):
                    pe.wait_ge(sq_ready, k * KD + kt + 1)
                    mm = nc.tensor.matmul(bank[:, 0:L], ones[:, :], sq[:, kt, :], start=(kt == 0), stop=(kt == KD - 1))
                mm.then_inc(psum_ready, 1)

            pe.wait_ge(consts, 12)
            pe.wait_ge(zeroed, BANKS + 3)
            pe.wait_ge(s_x, 32)
            for kt in range(KD):
                bank = free_unit(pe, ("x", kt))
                c = slice(kt * P, (kt + 1) * P)
                nc.tensor.transpose(bank[:, 0:META], mload[:, c], ident[0:META, 0:META])
                for j in range(2):
                    tr = nc.tensor.transpose(bank[:, TOK[j + 1][0]:TOK[j + 1][0] + P], xload[:, j, c], ident[:, :])
                tr.then_inc(psum_ready, 1)
            def turn_params(l):
                pe.wait_ge(s_par[l], 16 * N_PAR[l])
                for n, height in ((2 * l, NA), (2 * l + 1, NT)):
                    bank = free_unit(pe, ("param", n))
                    nc.tensor.transpose(bank[:, 0:height], rows[0:height, n, :], ident[0:height, 0:height]).then_inc(psum_ready, 1)

            for l in range(DEPTH):
                t0 = tokens_of(l)
                norm_sum(("norm", l), 2 * l)
                if l == 0:
                    turn_params(0)

                def normed(kt):
                    return hn_hi[:, kt, :], hn_lo[:, kt, :]

                def wait_normed(kt):
                    pe.wait_ge(hn_ready, 2 * l * KD + kt + 1)
                    return normed(kt)

                projects("conv", l, 0, 2 * CT, (wait_normed, normed))
                projects("pool", l, 0, PT_, (normed, normed))
                for part in "qk":
                    projects(part, l, 0, QT, (normed, normed))
                projects("v", l, 0, 2, (normed, normed))
                bank = free_unit(pe, ("mean", l))
                for c in range(CT):
                    pe.wait_ge(conv_done, l * CT + c + 1)
                    mm = nc.tensor.matmul(bank[:, 0:L], mean_ones[:, :], cy[:, c, :], start=(c == 0), stop=(c == CT - 1))
                mm.then_inc(psum_ready, 1)
                if l == 0:
                    turn_params(1)
                projects("v", l, 2, QT, (normed, normed))
                bank = free_unit(pe, ("var", l))
                for c in range(CT):
                    pe.wait_ge(centred_sq, l * CT + c + 1)
                    mm = nc.tensor.matmul(bank[:, 0:L], mean_ones[:, :], csq[:, c, :], start=(c == 0), stop=(c == CT - 1))
                mm.then_inc(psum_ready, 1)
                for c in range(PT_):
                    bank = free_unit(pe, ("mix", l, c))
                    pe.wait_ge(pool_mix, l * PT_ + c + 1)
                    nc.tensor.matmul(bank[:, 0:L], pw[:, l, c, :], poolo[:, c, :], start=True, stop=True).then_inc(psum_ready, 1)
                bank = free_unit(pe, ("fg", l))
                for j, (a, n) in enumerate(TOK):
                    for kt in range(KD):
                        mm = nc.tensor.matmul(bank[0:n, j * HEADS:(j + 1) * HEADS], hn[:, kt, a:a + n], wf[:, l, kt, :],
                                              start=(kt == 0), stop=(kt == KD - 1))
                mm.then_inc(psum_ready, 1)
                for j, (a, n) in enumerate(TOK):
                    bank = free_unit(pe, ("vtok", l, j))
                    wait_taken(pe, ("v", l, QT - 1))
                    for i in range(QT):
                        tr = nc.tensor.transpose(bank[0:n, i * P:(i + 1) * P], vT[:, i, a:a + n], ident[:, :])
                    tr.then_inc(psum_ready, 1)

                def gate_tile(g):
                    rhs = lambda kt: (hn_hi[:, kt, t0:], hn_lo[:, kt, t0:])
                    projects("gate", l, g, g + 1, (rhs, rhs), t0)

                for g in range(GATES_H):
                    gate_tile(g)
                    for i in QK_AFTER[g]:
                        bank = free_unit(pe, ("qk_ms", l, i))
                        pe.wait_ge(qk_sq, l * 2 * QT + i + 1)
                        nc.tensor.matmul(bank[:, 0:L], head_ones[:, :], qk_squares[:, i, :], start=True, stop=True).then_inc(psum_ready, 1)
                    if g == GATES_F:
                        pe.wait_ge(ls_ready, l + 1)
                        bank = free_unit(pe, ("ftok", l))
                        for j, (a, n) in enumerate(TOK):
                            for i in range(j + 1):
                                m = TOK[i][1]
                                mm = nc.tensor.matmul(bank[0:n, j * HEADS:(j + 1) * HEADS], tri[0:m, i, a:a + n],
                                                      ls[0:m, i * HEADS:(i + 1) * HEADS], start=(i == 0), stop=(i == j))
                        mm.then_inc(psum_ready, 1)
                        bank = free_unit(pe, ("frow", l))
                        for i, (a, n) in enumerate(TOK):
                            mm = nc.tensor.matmul(bank[0:HEADS, 0:L], ls[0:n, i * HEADS:(i + 1) * HEADS], tri[0:n, i, :],
                                                  start=(i == 0), stop=(i == 2))
                        mm.then_inc(psum_ready, 1)
                    if g == GATES_F + 1:
                        for h in range(HEADS):
                            bank = free_unit(pe, ("fbc", l, h))
                            if h == 0:
                                wait_taken(pe, ("frow", l))
                            nc.tensor.matmul(bank[:, 0:L], ident[0:HEADS, h:h + 1].broadcast_to([HEADS, P]), frow[:, :],
                                             start=True, stop=True).then_inc(psum_ready, 1)

                def scores(h):
                    b, i = HD * (h % 2), h // 2
                    bank = free_unit(pe, ("s", l, h))
                    pe.wait_ge(qk_ready, l * 2 * QT + 2 * (h // 2 + 1))
                    for j in score_tiles(l):
                        a, n = TOK[j]
                        c0, keys = S_COL[j]
                        mm = nc.tensor.matmul(bank[0:n, c0:c0 + keys], qkT[b:b + HD, i, a:a + n], qkT[b:b + HD, QT + i, 0:keys],
                                              start=True, stop=True)
                    mm.then_inc(psum_ready, 1)

                def turn_probs(h):
                    s = sc[:, h % 2, :]
                    c2, c1, c0 = S_COL[2][0], S_COL[1][0], S_COL[0][0]
                    bank = free_unit(pe, ("pt", l, h))
                    pe.wait_ge(probs_ready, scored(l, h + 1, 0))
                    nc.tensor.transpose(bank[:, 0:P], s[:, c1 + META:c1 + META + P], ident[:, :])
                    nc.tensor.transpose(bank[:, P:2 * P], s[:, c2 + META:c2 + META + P], ident[:, :])
                    nc.tensor.transpose(bank[:, 2 * P:3 * P], s[:, c2 + META + P:c2 + L], ident[:, :]).then_inc(psum_ready, 1)
                    bank = free_unit(pe, ("ptm", l, h))
                    if l == 0:
                        nc.tensor.transpose(bank[0:META, 0:META], s[0:META, c0:c0 + META], ident[0:META, 0:META])
                    nc.tensor.transpose(bank[0:META, META:META + P], s[:, c1:c1 + META], ident[:, :])
                    nc.tensor.transpose(bank[0:META, META + P:L], s[:, c2:c2 + META], ident[:, :]).then_inc(psum_ready, 1)

                def values(h):
                    b, c = HD * (h % 2), slice(h * HD, (h + 1) * HD)
                    bank = free_unit(pe, ("pv", l, h))
                    wait_taken(pe, ("ptm", l, h))
                    nc.tensor.matmul(bank[b:b + HD, t0:L], vtok[0:META, 0, c], ptm[:, t0:L], start=True, stop=False)
                    nc.tensor.matmul(bank[b:b + HD, META:L], vtok[:, 1, c], pt[:, 0:2 * P], start=False, stop=False)
                    nc.tensor.matmul(bank[b:b + HD, META + P:L], vtok[:, 2, c], pt[:, 2 * P:3 * P], start=False,
                                     stop=True).then_inc(psum_ready, 1)

                for h in range(HEADS):
                    scores(h)
                    gate_tile(GATES_H + 2 * h)
                    if h > 0:
                        values(h - 1)
                    gate_tile(GATES_H + 2 * h + 1)
                    turn_probs(h)

                need(("conv_o", l))
                pe.wait_ge(conv_split, (l + 1) * CT)
                for d in range(KD):
                    project(("yc", l, d), block_parts(("conv_o", l)), d * P, lambda i: (conv_hi[:, i, t0:], conv_lo[:, i, t0:]), CT, t0)
                values(HEADS - 1)
                need(("pool_o", l))
                pe.wait_ge(pool_split, (l + 1) * PT_)
                for d in range(KD):
                    project(("yp", l, d), block_parts(("pool_o", l)), d * P, lambda i: (pool_hi[:, i, t0:], pool_lo[:, i, t0:]), PT_, t0)
                for d in range(KD):
                    if d % 4 == 0:
                        need(("attn_o", l, d // 4))
                    if d == 0:
                        wait_taken(pe, ("pv", l, HEADS - 1))
                    project(("ya", l, d), block_parts(("attn_o", l, d // 4)), d % 4 * P, lambda i: (att_hi[:, i, t0:], att_lo[:, i, t0:]), QT, t0)

                def mixed(kt):
                    return m_hi[:, kt, t0:], m_lo[:, kt, t0:]

                def wait_mixed(kt):
                    pe.wait_ge(m_ready, l * KD + kt + 1)
                    return mixed(kt)

                projects("out", l, 0, KD, (wait_mixed, mixed), t0)

                if l == 0:
                    norm_sum(("norm", "ffn"), 1)

                    def ffn_normed(kt):
                        pe.wait_ge(hn_ready, KD + kt + 1)
                        return normed(kt)

                    for i in range(FT // 2):
                        for part, name in (("ff_gate", "ffg"), ("ff_up", "ffu")):
                            need((part, i))
                            for f in (2 * i, 2 * i + 1):
                                project((name, f), block_parts((part, i)), f % 2 * P, ffn_normed if (name, f) == ("ffg", 0) else normed, KD)
                    for half in range(2):
                        banks = []
                        for k in range(KB):
                            need(("ff_down", half, k))
                            w = block_parts(("ff_down", half, k))
                            ks = min(4, FT - 4 * k)
                            for d in range(4):
                                if k == 0:
                                    banks.append(free_unit(pe, ("ffd", 4 * half + d)))
                                for kt in range(ks):
                                    f = 4 * k + kt
                                    if half == 0 and d == 0:
                                        pe.wait_ge(hid_ready, f + 1)
                                    for n, (w_part, x) in enumerate(((w[0], hid_hi), (w[0], hid_lo), (w[1], hid_hi))):
                                        mm = nc.tensor.matmul(banks[d][:, 0:L], w_part[:, kt, d * P:(d + 1) * P], x[:, f, :],
                                                              start=(f == 0 and n == 0), stop=(f == FT - 1 and n == 2))
                                if k == KB - 1:
                                    mm.then_inc(psum_ready, 1)
                            if k < KB - 1:
                                mm.then_inc(down_used, 1)

            for n in range(4):
                j, half = n // 2, n % 2
                a = TOK[j + 1][0]
                bank = free_unit(pe, ("htok", n))
                for d in range(4):
                    if j == 0:
                        wait_taken(pe, residual(3, 4 * half + d))
                    tr = nc.tensor.transpose(bank[:, d * P:(d + 1) * P], hT[:, 4 * half + d, a:a + P], ident[:, :])
                tr.then_inc(psum_ready, 1)
            bank = free_unit(pe, ("logit",))
            pe.wait_ge(wrg_ready, 1)
            for j in range(2):
                a = TOK[j + 1][0]
                for kt in range(KD):
                    mm = nc.tensor.matmul(bank[:, j * EXPERTS:(j + 1) * EXPERTS], hT[:, kt, a:a + P], wrg[:, kt, :],
                                          start=(kt == 0), stop=(kt == KD - 1))
            mm.then_inc(psum_ready, 1)
            bank = free_unit(pe, ("pos",))
            pe.wait_ge(mask_ready, 2)
            for c, terms in enumerate((((strict, 0),), ((ones[:, :], 0), (strict, 1)), ((ones[:, :], 0), (ones[:, :], 1)))):
                if c == 2:
                    mm.then_inc(split_used, SPLIT)
                for n, (lhs, j) in enumerate(terms):
                    mm = nc.tensor.matmul(bank[:, c * EXPERTS:(c + 1) * EXPERTS], lhs, mask[:, j, 0:EXPERTS],
                                          start=(n == 0), stop=(n == len(terms) - 1))
            mm.then_inc(psum_ready, 1)

            pe.wait_ge(routed, 3)
            pe.wait_ge(xs_ready, 2)
            pe.wait_ge(taken, NU)
            jobs = pe.value_load(n_jobs[0:1, 0:1], min_val=EXPERTS, max_val=MAX_JOBS)

            def split_matmuls(bank, terms, w_h, w_l, first, last):
                n, total = 0, 3 * len(terms)
                for which in range(2):
                    for x_h, x_l, k, c in terms:
                        for lhs in ((x_h, x_l), (x_h,))[which]:
                            w = (w_h, w_l)[which]
                            mm = nc.tensor.matmul(bank[:, :], lhs, w[:, k, c:c + BANK], start=(first and n == 0), stop=(last and n == total - 1))
                            n += 1
                return mm

            def scatter(job):
                for u in range(4):
                    j, half = u // 2, u % 2
                    wait_scalar(pe, job, half - 2)
                    nc.tensor.matmul(psum[4 + u][:, :], pgT[:, j * P:(j + 1) * P], ytok[:, half * BANK:(half + 1) * BANK],
                                     start=True, stop=True).then_inc(scattered, 1)

            with pe.Fori(0, jobs) as job:
                def block_split(b):
                    pe.wait_ge(lo_ready, job * EB + (b + 1))

                pe.wait_ge(sel_ready, job * 4 + 4)
                for u in range(2):
                    bank = psum[1 + u]
                    for d in range(4):
                        kt = 4 * u + d
                        for j in range(2):
                            mm = nc.tensor.matmul(bank[:, d * P:(d + 1) * P], xs[:, j, kt * P:(kt + 1) * P],
                                                  psel[:, j, :], start=(j == 0), stop=(j == 1))
                    mm.then_inc(e_full, 1)
                scatter(job)
                for j in range(2):
                    tr = nc.tensor.transpose(psum[3][:, j * P:(j + 1) * P], pgat[:, j, :], ident[:, :])
                tr.then_inc(e_full, 1)

                def product(kind, i, bank):
                    for h in range(2):
                        b = epos[kind, i, h]
                        block_split(b)
                        terms = [(xg_hi[:, k * P:(k + 1) * P], xg_lo[:, k * P:(k + 1) * P], k - 4 * h, 0) for k in range(4 * h, 4 * h + 4)]
                        split_matmuls(bank, terms, weight_rows(w_hi, b), weight_rows(w_lo, b), h == 0, h == 1).then_inc(split_used, 1)

                def turn(i):
                    wait_etaken(pe, job, U_H + 2 * i)
                    for f in range(4):
                        tr = nc.tensor.transpose(psum[3][:, f * P:(f + 1) * P], ehid[:, f * P:(f + 1) * P], ident[:, :])
                    tr.then_inc(e_full, 1)

                def down(i):
                    wait_etaken(pe, job, U_T + 2 * i)
                    if i == 0:
                        pe.wait_ge(added, job * 4 + 4)
                    for h in range(2):
                        b = epos["d", i, h]
                        if i == FB - 2 and h == 1:
                            turn(FB - 1)
                        block_split(b)
                        for half in range(2):
                            terms = [(act_hi[:, i % 2, f * P:(f + 1) * P], act_lo[:, i % 2, f * P:(f + 1) * P], f - 2 * h, half * BANK)
                                     for f in range(2 * h, 2 * h + 2)]
                            mm = split_matmuls(psum[6 + half], terms, weight_rows(w_hi, b), weight_rows(w_lo, b),
                                               i == 0 and h == 0, i == FB - 1 and h == 1)
                        mm.then_inc(split_used, 1)

                wait_etaken(pe, job, 1)
                for i in range(FB):
                    product("g", i, psum[i % 2])
                    if i > 0:
                        turn(i - 1)
                    product("u", i, psum[2])
                    if i > 0:
                        down(i - 1)
                down(FB - 1)
            scatter(jobs)

        @block.scalar
        def _(act_e):
            a_ = nc.scalar.activation
            steps = Steps(act_e, act_step)

            def high_part(n):
                act_e.wait_ge(slot_full[n % RING], 16 * (n // RING + 1))
                if n >= SPLIT:
                    wait_used(act_e, n - SPLIT)
                a_(block_shape(w_hi, n % SPLIT, n), block_shape(raw, n % RING, n), ACT.Copy).then_inc(block_high, 1)

            split = Splitter(high_part)

            def high_normed(n):
                for kt in range(KD):
                    act_e.wait_ge(hn_raw, n * KD + kt + 1)
                    a_(hn_hi[:, kt, :], hn[:, kt, :], ACT.Copy).then_inc(hn_high, 1)

            def root(n):
                split.before((("norm", 0), ("norm", "ffn"), ("norm", 1))[n])
                wait_taken(act_e, (("norm", 0), ("norm", "ffn"), ("norm", 1))[n])
                a_(rms[:, 0, :], rms[:, 0, :], ACT.Sqrt).then_inc(root_ready, 1)

            def squares(n):
                for kt in range(KD):
                    split.before(residual(n, kt))
                    wait_taken(act_e, residual(n, kt))
                    a_(sq[:, kt, :], hT[:, kt, :], ACT.Square).then_inc(sq_ready, 1)

            for l in range(DEPTH):
                t0 = tokens_of(l)
                squares(2 * l)
                root(2 * l)
                high_normed(2 * l)
                for c in range(CT):
                    split.before(("conv", l, CT + c))
                    wait_taken(act_e, ("conv", l, CT + c))
                    a_(conv_in[:, CT + c, :], conv_in[:, CT + c, :], ACT.Sigmoid).then_inc(glu_gate, 1)
                for i in range(2 * QT):
                    split.before(("qk"[i // QT], l, i % QT))
                    wait_taken(act_e, ("qk"[i // QT], l, i % QT))
                    a_(qk_squares[:, i, :], qkT[:, i, :], ACT.Square).then_inc(qk_sq, 1)
                split.before(("mean", l))
                wait_taken(act_e, ("mean", l))
                for c in range(CT):
                    a_(csq[:, c, :], cy[:, c, :], ACT.Square).then_inc(centred_sq, 1)
                split.before(("var", l))
                wait_taken(act_e, ("var", l))
                a_(rms[:, 1, :], rms[:, 1, :], ACT.Sqrt).then_inc(ln_root, 1)
                for c in range(CT):
                    act_e.wait_ge(ln_scaled, l * CT + c + 1)
                    for dst in (conv_hi, csq):
                        a_(dst[:, c, :], cy[:, c, :], ACT.Silu, bias=pcol(l, C_LB + c)).then_inc(conv_act, 1)
                split.before(("fg", l))
                wait_taken(act_e, ("fg", l))
                steps.did(a_(fga[:, :], fg[:, :], ACT.Abs))
                steps.settle()
                steps.did(a_(fge[:, :], fga[:, :], ACT.Exp, scale=-1.0))
                steps.settle()
                a_(fgl[:, :], fge[:, :], ACT.Ln, bias=ones[:, 0:1]).then_inc(fg_log, 1)
                for n, i in enumerate(QK):
                    split.before(("qk_ms", l, i))
                    wait_taken(act_e, ("qk_ms", l, i))
                    a_(silu[:, n % 2, :], rms[:, n % 2, :], ACT.Sqrt).then_inc(qk_root, 1)

                def high_values(h):
                    b = HD * (h % 2)
                    split.before(("pv", l, h))
                    bank = ready_unit(act_e, ("pv", l, h))
                    a_(att_hi[b:b + HD, h // 2, t0:], bank[b:b + HD, t0:L], ACT.Copy).then_inc(att_high, 1)

                for h in range(HEADS):
                    s = sc[:, h % 2, :]
                    split.before(("s", l, h))
                    for n, j in enumerate(score_tiles(l)):
                        m, (c0, keys) = TOK[j][1], S_COL[j]
                        act_e.wait_ge(max_ready, scored(l, h, n) + 1)
                        a_(s[0:m, c0:c0 + keys], s[0:m, c0:c0 + keys], ACT.Exp, bias=nmax[0:m, h % 2, j:j + 1],
                           accum_out=rsum[0:m, h % 2, j:j + 1]).then_inc(exp_ready, 1)
                    act_e.wait_ge(rinv_ready, l * HEADS + h + 1)
                    for j in score_tiles(l):
                        m, (c0, keys) = TOK[j][1], S_COL[j]
                        a_(s[0:m, c0:c0 + keys], s[0:m, c0:c0 + keys], ACT.Copy,
                           scale=rinv[0:m, h % 2, j:j + 1]).then_inc(probs_ready, 1)
                    if h > 0:
                        high_values(h - 1)
                split.before(("gate", l, GT - 1))
                wait_taken(act_e, ("gate", l, GT - 1))
                for b in (1, 2, 0):
                    for d in range(0, KD, 4):
                        g = gates[:, b, d:d + 4, t0:]
                        a_(g, g, ACT.Sigmoid).then_inc(gate_ready, 1)
                high_values(HEADS - 1)
                for d in range(KD):
                    split.before(("ya", l, d))
                    act_e.wait_ge(m_raw, l * KD + d + 1)
                    a_(m_hi[:, d, t0:], mT[:, d, t0:], ACT.Copy).then_inc(m_high, 1)
                if l == 0:
                    squares(1)
                    root(1)
                    high_normed(1)
                    for i in range(FT // 2):
                        for f in (2 * i, 2 * i + 1):
                            split.before(("ffg", f))
                            bank = ready_unit(act_e, ("ffg", f))
                            if f >= 2:
                                wait_taken(act_e, ("ffu", f - 2))
                            a_(silu[:, f % 2, :], bank[:, 0:L], ACT.Silu).then_inc(silu_ready, 1)
                        for f in (2 * i, 2 * i + 1):
                            split.before(("ffu", f))
                            wait_taken(act_e, ("ffu", f))
                            a_(hid_hi[:, f, :], hid[:, f % 2, :], ACT.Copy).then_inc(hid_high, 1)

            split.before(None)
            for j in range(2):
                wait_taken(act_e, ("htok", 2 * j + 1))
                if j > 0:
                    act_e.wait_ge(ss_ready, j)
                a_(tok_sq, hacc[:, j, :], ACT.Square, accum_out=ss[:, j:j + 1]).then_inc(ss_ready, 1)
            act_e.wait_ge(sms_ready, 1)
            a_(srt[:, :], sms[:, :], ACT.Sqrt).then_inc(srt_ready, 1)
            act_e.wait_ge(gap_ready, 1)
            a_(pexp[:, :], gap[:, :], ACT.Exp).then_inc(pexp_ready, 1)

            act_e.wait_ge(routed, 3)
            jobs = act_e.value_load(n_jobs[0:1, 0:1], min_val=EXPERTS, max_val=MAX_JOBS)
            with act_e.Fori(0, jobs) as job:
                split = [0]

                def high_parts(upto):
                    for b in range(split[0], min(upto + 1, EB)):
                        act_e.wait_ge(landed[b % RAW], job * (16 * (EB // RAW)) + 16 * (b // RAW + 1))
                        wait_split_used(act_e, job, b - SPLIT)
                        a_(w_hi[:, b % SPLIT, :], raw[:, b % RAW, :], ACT.Copy).then_inc(hi_ready, 1)
                        split[0] = b + 1

                high_parts(1)
                for u in range(2):
                    act_e.wait_ge(e_full, job * EF + (u + 1))
                    a_(xg_hi[:, u * BANK:(u + 1) * BANK], psum[1 + u][:, :], ACT.Copy).then_inc(e_scalar, 1)
                for i in range(FB + 1):
                    if i < FB:
                        end = epos["g", i, 1]
                        high_parts(end + 2)
                        wait_split_used(act_e, job, end)
                        a_(esilu[:, i % 2, :], psum[i % 2][:, :], ACT.Silu).then_inc(e_scalar, 1)
                    if i == FB:
                        high_parts(EB - 1)
                    if i > 0:
                        act_e.wait_ge(e_full, job * EF + (F_T + i))
                        a_(act_hi[:, (i - 1) % 2, :], psum[3][:, :], ACT.Copy).then_inc(e_scalar, 1)
                for half in range(2):
                    wait_split_used(act_e, job, EB - 1)
                    a_(ytok[:, half * BANK:(half + 1) * BANK], psum[6 + half][:, :], ACT.Copy).then_inc(e_scalar, 1)

        @block.vector
        def _(dve):
            v = nc.vector
            steps = Steps(dve, dve_step)
            freed = [0]

            def frees(name, instruction, count=1):
                assert unit[name] == freed[0], (name, freed[0])
                freed[0] += count
                instruction.then_inc(taken, count)

            v.memset(pw[:, :, :, :].rearrange("p l c n -> p (l c n)"), 0.0).then_inc(pw_zeroed, 1)
            for i in range(BANKS):
                v.memset(psum[i][:, :], 0.0).then_inc(zeroed, 1)
            v.memset(fg[:, :], 0.0).then_inc(zeroed, 1)
            steps.did(v.memset(head_ones[:, :], 0.0))
            steps.settle()
            for b in range(2):
                v.memset(head_ones[b * HD:(b + 1) * HD, b * HD:(b + 1) * HD], 1.0).then_inc(zeroed, 1)
            steps.did(v.memset(rsum[:, :, :], 1.0))
            for t in (pos, mask, comb):
                steps.did(v.memset(t[:, :, :], 0.0))
            dve.wait_ge(consts, 12)
            for g in range(GROUPS):
                b = GW * (g % 2)
                steps.did(v.tensor_scalar(rcnt[b:b + GW, g // 2, :], iota_f[b:b + GW, 0:PAD_P], 1.0, 2.0 ** (g + 1), ALU.add, ALU.min))
            steps.settle()
            v.reciprocal(rcnt[:, :, :], rcnt[:, :, :]).then_inc(rcnt_ready, 1)

            for kt in range(KD):
                bank = ready_unit(dve, ("x", kt))
                frees(("x", kt), v.tensor_copy(hT[:, kt, :], bank[:, 0:L]))
            dve.wait_ge(block_high, 1)
            v.tensor_tensor(block_shape(w_lo, 0, 0), block_shape(raw, 0, 0), block_shape(w_hi, 0, 0).bitcast(F32), ALU.subtract)\
             .then_inc(block_low, 1)

            def take_params(l):
                for n in (2 * l, 2 * l + 1):
                    bank = ready_unit(dve, ("param", n))
                    height = (NA, NT)[n % 2]
                    frees(("param", n), v.tensor_copy(par[:, n, 0:height], bank[:, 0:height]))
                wait_taken(dve, ("param", 2 * l + 1))

            def norm(name, n, l, gain):
                bank = ready_unit(dve, name)
                frees(name, v.tensor_scalar(rms[:, 0, :], bank[:, 0:L], 1.0 / D, EPS_RMS, ALU.mult, ALU.add))
                if n == 0:
                    take_params(0)
                dve.wait_ge(root_ready, n + 1)
                steps.did(v.reciprocal(rstd[:, 0, :], rms[:, 0, :]))
                steps.settle()
                for kt in range(KD + 1):
                    if kt < KD:
                        v.scalar_tensor_tensor(hn[:, kt, :], hT[:, kt, :], pcol(l, gain + kt), rstd[:, 0, :], ALU.mult, ALU.mult)\
                         .then_inc(hn_raw, 1)
                    if kt > 0:
                        dve.wait_ge(hn_high, n * KD + kt)
                        v.tensor_tensor(hn_lo[:, kt - 1, :], hn[:, kt - 1, :], hn_hi[:, kt - 1, :].bitcast(F32), ALU.subtract)\
                         .then_inc(hn_ready, 1)

            for l in range(DEPTH):
                t0 = tokens_of(l)
                norm(("norm", l), 2 * l, l, C_MIX)

                for i in range(2 * CT):
                    bank = ready_unit(dve, ("conv", l, i))
                    frees(("conv", l, i), v.tensor_scalar(conv_in[:, i, :], bank[:, 0:L], pcol(l, C_CONV + i), None, ALU.add))
                for i in range(PT_):
                    bank = ready_unit(dve, ("pool", l, i))
                    frees(("pool", l, i), v.tensor_scalar(ppad[:, i, PAD_P:], bank[:, 0:L], pcol(l, C_POOL + i), None, ALU.add))
                last = [0] * CT
                for c in range(CT):
                    dve.wait_ge(glu_gate, l * CT + c + 1)
                    last[c] = steps.did(v.tensor_tensor(upad[:, c, PAD_C:], conv_in[:, c, :], conv_in[:, CT + c, :], ALU.mult))

                def taps(first, count):
                    for t in range(first, min(first + count, TAPS)):
                        for c in range(CT):
                            steps.settle(last[c])
                            if t == 0:
                                last[c] = steps.did(v.tensor_scalar(cy[:, c, :], upad[:, c, 0:L], tap(l, 0, c), pcol(l, C_CB + c),
                                                                    ALU.mult, ALU.add))
                                continue
                            ins = v.scalar_tensor_tensor(cy[:, c, :], upad[:, c, t:t + L], tap(l, t, c), cy[:, c, :], ALU.mult, ALU.add)
                            if t < TAPS - 1:
                                last[c] = steps.did(ins)
                            else:
                                ins.then_inc(conv_done, 1)

                per = -(-TAPS // (2 * QT - 1))
                for i in range(2 * QT):
                    name = ("qk"[i // QT], l, i % QT)
                    bank = ready_unit(dve, name)
                    frees(name, v.tensor_scalar(qkT[:, i, :], bank[:, 0:L], pcol(l, C_Q + i), None, ALU.add))
                    taps(i * per, per)
                def take_v(i):
                    bank = ready_unit(dve, ("v", l, i))
                    frees(("v", l, i), v.tensor_scalar(vT[:, i, :], bank[:, 0:L], pcol(l, C_V + i), None, ALU.add))

                for i in range(2):
                    take_v(i)
                bank = ready_unit(dve, ("mean", l))
                dve.wait_ge(conv_done, (l + 1) * CT)
                v.tensor_tensor(cy[:, 0, :], cy[:, 0, :], bank[:, 0:L], ALU.subtract)
                frees(("mean", l), v.tensor_tensor(cy[:, 1, :], cy[:, 1, :], bank[:, 0:L], ALU.subtract))
                if l == 0:
                    take_params(1)
                for i in range(2, QT):
                    take_v(i)
                bank = ready_unit(dve, ("var", l))
                frees(("var", l), v.tensor_scalar(rms[:, 1, :], bank[:, 0:L], EPS_LN, None, ALU.add))
                dve.wait_ge(ln_root, l + 1)
                steps.did(v.reciprocal(rstd[:, 1, :], rms[:, 1, :]))
                steps.settle()
                for c in range(CT):
                    v.scalar_tensor_tensor(cy[:, c, :], cy[:, c, :], pcol(l, C_LG + c), rstd[:, 1, :], ALU.mult, ALU.mult).then_inc(ln_scaled, 1)
                for c in range(PT_):
                    bank = ready_unit(dve, ("mix", l, c))
                    steps.did(v.tensor_scalar(pool_hi[:, c, :], bank[:, 0:L], pcol(l, C_PS + c), None, ALU.mult))
                    frees(("mix", l, c), v.tensor_scalar(poolo[:, c, :], bank[:, 0:L], pcol(l, C_PS + c), None, ALU.mult))
                wait_taken(dve, ("mix", l, PT_ - 1))
                for c in range(PT_):
                    v.tensor_tensor(pool_lo[:, c, :], poolo[:, c, :], pool_hi[:, c, :].bitcast(F32), ALU.subtract).then_inc(pool_split, 1)
                for c in range(CT):
                    dve.wait_ge(conv_act, 2 * (l * CT + c + 1))
                    v.tensor_tensor(conv_lo[:, c, :], csq[:, c, :], conv_hi[:, c, :].bitcast(F32), ALU.subtract).then_inc(conv_split, 1)

                steps.did(v.tensor_scalar(qgain[:, 0:1], pcol(l, C_QN), float(HD) ** -0.5, None, ALU.mult))
                steps.did(v.tensor_copy(qgain[:, 1:2], pcol(l, C_KN)))

                def mean_square(n):
                    bank = ready_unit(dve, ("qk_ms", l, QK[n]))
                    frees(("qk_ms", l, QK[n]), v.tensor_scalar(rms[:, n % 2, :], bank[:, 0:L], 1.0 / HD, EPS_RMS, ALU.mult, ALU.add))

                def norm_qk(n):
                    i = QK[n]
                    dve.wait_ge(qk_root, l * 2 * QT + n + 1)
                    steps.did(v.reciprocal(rstd[:, n % 2, :], silu[:, n % 2, :]))
                    steps.settle()
                    v.scalar_tensor_tensor(qkT[:, i, :], qkT[:, i, :], qgain[:, i // QT:i // QT + 1], rstd[:, n % 2, :],
                                           ALU.mult, ALU.mult).then_inc(qk_ready, 1)

                def take_gate(g):
                    bank = ready_unit(dve, ("gate", l, g))
                    frees(("gate", l, g), v.tensor_scalar(gates[:, g // KD, g % KD, t0:], bank[:, t0:L], pcol(l, C_GATE + g), None, ALU.add))

                bank = ready_unit(dve, ("fg", l))
                v.tensor_tensor(fg[0:META, 0:HEADS], bank[0:META, 0:HEADS], bf_bc[0:META, l, :], ALU.add)
                v.tensor_tensor(fg[:, HEADS:2 * HEADS], bank[:, HEADS:2 * HEADS], bf_bc[:, l, :], ALU.add)
                frees(("fg", l), v.tensor_tensor(fg[:, 2 * HEADS:], bank[:, 2 * HEADS:3 * HEADS], bf_bc[:, l, :], ALU.add))
                for j, (_, n) in enumerate(TOK):
                    bank = ready_unit(dve, ("vtok", l, j))
                    if j == 0:
                        dve.wait_ge(pool_mix, (l + 1) * PT_)
                    frees(("vtok", l, j), v.tensor_copy(vtok[0:n, j, :], bank[0:n, 0:ATT_W]))
                dve.wait_ge(fg_log, l + 1)
                v.scalar_tensor_tensor(ls[:, :], fg[:, :], 0.0, fgl[:, :], ALU.min, ALU.subtract).then_inc(ls_ready, 1)
                def take_values(h):
                    b = HD * (h % 2)
                    bank = ready_unit(dve, ("pv", l, h))
                    dve.wait_ge(att_high, l * HEADS + h + 1)
                    frees(("pv", l, h), v.tensor_tensor(att_lo[b:b + HD, h // 2, t0:], bank[b:b + HD, t0:L],
                                                        att_hi[b:b + HD, h // 2, t0:].bitcast(F32), ALU.subtract))

                for g in range(GATES_H):
                    take_gate(g)
                    for i in QK_AFTER[g]:
                        mean_square(QK.index(i))
                        if QK.index(i) < 2 * QT - QK_LATE:
                            norm_qk(QK.index(i))
                    if g == GATES_F:
                        bank = ready_unit(dve, ("ftok", l))
                        v.tensor_copy(ftok[0:META, 0:HEADS], bank[0:META, 0:HEADS])
                        frees(("ftok", l), v.tensor_copy(ftok[:, HEADS:], bank[:, HEADS:3 * HEADS]))
                        bank = ready_unit(dve, ("frow", l))
                        frees(("frow", l), v.tensor_copy(frow[:, :], bank[0:HEADS, 0:L]))
                    if g == GATES_F + 1:
                        for h in range(HEADS):
                            bank = ready_unit(dve, ("fbc", l, h))
                            frees(("fbc", l, h), v.tensor_copy(fbm[:, h, 0:L], bank[:, 0:L]))
                dve.wait_ge(fbm_ready, (l + 1) * 3)
                dve.wait_ge(conv_split, (l + 1) * CT)
                dve.wait_ge(pool_split, (l + 1) * PT_)
                for h in range(HEADS):
                    bank = ready_unit(dve, ("s", l, h))
                    tiles = score_tiles(l)
                    for j in tiles:
                        m, (c0, keys) = TOK[j][1], S_COL[j]
                        ins = v.scalar_tensor_tensor(sc[0:m, h % 2, c0:c0 + keys], bank[0:m, c0:c0 + keys],
                                                     ftok[0:m, j * HEADS + h:j * HEADS + h + 1], fbm[0:m, h, c0:c0 + keys],
                                                     ALU.add, ALU.subtract)
                    frees(("s", l, h), ins)
                    wait_taken(dve, ("s", l, h))
                    for j in tiles:
                        m, (c0, keys) = TOK[j][1], S_COL[j]
                        v.tensor_reduce(nmax[0:m, h % 2, j:j + 1], sc[0:m, h % 2, c0:c0 + keys], AX_X, ALU.max, negate=True).then_inc(max_ready, 1)
                    take_gate(GATES_H + 2 * h)
                    if h < QK_LATE:
                        norm_qk(2 * QT - QK_LATE + h)
                    dve.wait_ge(exp_ready, scored(l, h + 1, 0))
                    v.reciprocal(rinv[:, h % 2, :], rsum[:, h % 2, :]).then_inc(rinv_ready, 1)
                    if h > 0:
                        take_values(h - 1)
                    take_gate(GATES_H + 2 * h + 1)
                    bank = ready_unit(dve, ("pt", l, h))
                    frees(("pt", l, h), v.tensor_copy(pt[:, :], bank[:, 0:3 * P]))
                    bank = ready_unit(dve, ("ptm", l, h))
                    frees(("ptm", l, h), v.tensor_copy(ptm[:, t0:], bank[0:META, t0:L]))

                def gated(name, b, group, d):
                    dve.wait_ge(gate_ready, l * 6 + 2 * group + d // 4 + 1)
                    bank = ready_unit(dve, (name, l, d))
                    g = gates[:, b, d, t0:]
                    frees((name, l, d), v.tensor_tensor(g, bank[:, t0:L], g, ALU.mult))

                for d in range(KD):
                    gated("yc", 1, 0, d)
                take_values(HEADS - 1)
                for d in range(KD):
                    gated("yp", 2, 1, d)
                    wait_taken(dve, ("yp", l, d))
                    steps.did(v.tensor_tensor(gates[:, 1, d, t0:], gates[:, 1, d, t0:], gates[:, 2, d, t0:], ALU.add))

                def low_mixed(d):
                    dve.wait_ge(m_high, l * KD + d + 1)
                    v.tensor_tensor(m_lo[:, d, t0:], mT[:, d, t0:], m_hi[:, d, t0:].bitcast(F32), ALU.subtract).then_inc(m_ready, 1)

                steps.settle()
                for d in range(KD):
                    gated("ya", 0, 2, d)
                    wait_taken(dve, ("ya", l, d))
                    v.tensor_tensor(mT[:, d, t0:], gates[:, 0, d, t0:], gates[:, 1, d, t0:], ALU.add).then_inc(m_raw, 1)
                    if d > 0:
                        low_mixed(d - 1)
                low_mixed(KD - 1)
                for d in range(KD):
                    bank = ready_unit(dve, ("out", l, d))
                    frees(("out", l, d), v.tensor_tensor(hT[:, d, t0:], bank[:, t0:L], hT[:, d, t0:], ALU.add))
                if l == 0:
                    norm(("norm", "ffn"), 1, 0, C_FFN)

                    def low_hidden(f):
                        dve.wait_ge(hid_high, f + 1)
                        v.tensor_tensor(hid_lo[:, f, :], hid[:, f % 2, :], hid_hi[:, f, :].bitcast(F32), ALU.subtract).then_inc(hid_ready, 1)

                    for f in range(FT):
                        dve.wait_ge(silu_ready, (f // 2 + 1) * 2)
                        bank = ready_unit(dve, ("ffu", f))
                        if f > 0:
                            low_hidden(f - 1)
                        if f > 1:
                            dve.wait_ge(hid_ready, f - 1)
                        frees(("ffg", f) if f % 2 == 0 else ("ffu", f),
                              v.tensor_tensor(hid[:, f % 2, :], bank[:, 0:L], silu[:, f % 2, :], ALU.mult), 3 if f % 2 == 0 else 1)
                    low_hidden(FT - 1)
                    for d in range(KD):
                        bank = ready_unit(dve, ("ffd", d))
                        frees(("ffd", d), v.tensor_tensor(hT[:, d, :], bank[:, 0:L], hT[:, d, :], ALU.add))

            steps.did(v.tensor_tensor(wrg[:, :, :], wr[:, :, :],
                                      par[:, 2 * (DEPTH - 1), C_FFN:C_FFN + KD].unsqueeze(2).broadcast_to([P, KD, EXPERTS]), ALU.mult))
            v.tensor_copy(lg[:, :, :], pos[:, :, 0:8]).then_inc(wrg_ready, 1)
            for n in range(4):
                j, half = n // 2, n % 2
                bank = ready_unit(dve, ("htok", n))
                frees(("htok", n), v.tensor_copy(hacc[:, j, half * BANK:(half + 1) * BANK], bank[:, :]))
            for t in (cum, jobf):
                steps.did(v.memset(t[:, :, :], 0.0))
            dve.wait_ge(ss_ready, 2)
            v.tensor_scalar(sms[:, :], ss[:, :], 1.0 / D, EPS_RMS, ALU.mult, ALU.add).then_inc(sms_ready, 1)
            v.memset(ytok[:, :], 0.0).then_inc(e_scalar, 2)
            dve.wait_ge(srt_ready, 1)
            steps.did(v.reciprocal(srs[:, :], srt[:, :]))
            steps.settle()
            bank = ready_unit(dve, ("logit",))
            v.scalar_tensor_tensor(lg[:, 0, :], bank[:, 0:EXPERTS], srs[:, 0:1], br_bc[:, :], ALU.mult, ALU.add)
            frees(("logit",), v.scalar_tensor_tensor(lg[:, 1, :], bank[:, EXPERTS:2 * EXPERTS], srs[:, 1:2], br_bc[:, :], ALU.mult, ALU.add))
            wait_taken(dve, ("logit",))
            for j in range(2):
                steps.did(v.max(mx[:, j, :], lg[:, j, :]))
            steps.settle()
            v.tensor_tensor(gap[:, :], mx[:, :, 1], mx[:, :, 0], ALU.subtract).then_inc(gap_ready, 1)
            for j in range(2):
                steps.did(v.max_index(mi[:, j, :], mx[:, j, :], lg[:, j, :]))
            steps.settle()
            steps.did(v.tensor_copy(mif[:, :, :], mi[:, :, :]))
            steps.settle()
            for j in range(2):
                steps.did(v.tensor_scalar(oh0[:, j, :], iota_f[:, 0:EXPERTS], mif[:, j, 0:1], None, ALU.is_equal))
                steps.did(v.tensor_scalar(oh1[:, j, :], iota_f[:, 0:EXPERTS], mif[:, j, 1:2], None, ALU.is_equal))
            steps.settle()
            for j in range(2):
                v.tensor_tensor(mask[:, j, 0:EXPERTS], oh0[:, j, :], oh1[:, j, :], ALU.add).then_inc(mask_ready, 1)
            dve.wait_ge(pexp_ready, 1)
            steps.did(v.tensor_scalar(pden[:, :], pexp[:, :], 1.0, None, ALU.add))
            steps.settle()
            steps.did(v.reciprocal(pr0[:, :], pden[:, :]))
            steps.settle()
            steps.did(v.tensor_tensor(pr1[:, :], pexp[:, :], pr0[:, :], ALU.mult))
            for j in range(2):
                steps.did(v.tensor_scalar(comb[:, j, 0:EXPERTS], oh0[:, j, :], pr0[:, j:j + 1], None, ALU.mult))
            steps.settle()
            for j in range(2):
                v.scalar_tensor_tensor(comb[:, j, 0:EXPERTS], oh1[:, j, :], pr1[:, j:j + 1], comb[:, j, 0:EXPERTS], ALU.mult, ALU.add)\
                 .then_inc(comb_ready, 1)
            dve.wait_ge(s_gbc, 16)
            v.scalar_tensor_tensor(xs[:, 0, :], hacc[:, 0, :], srs[:, 0:1], gbc, ALU.mult, ALU.mult).then_inc(xs_ready, 1)
            bank = ready_unit(dve, ("pos",))
            v.tensor_copy(pos[:, :, 0:EXPERTS], bank[:, 0:2 * EXPERTS].rearrange("p (j e) -> p j e", j=2)).then_inc(routed, 1)
            steps.did(v.tensor_scalar(cum[:, 0, EXPERTS:], bank[:, 2 * EXPERTS:3 * EXPERTS], float(P), 1.0, ALU.is_gt, ALU.add))
            for n in range(3):
                steps.settle()
                steps.did(v.tensor_tensor(cum[:, n + 1, EXPERTS:], cum[:, n, EXPERTS:], cum[:, n, EXPERTS - 2 ** n:2 * EXPERTS - 2 ** n], ALU.add))
            steps.settle()
            v.tensor_copy(n_jobs[:, 0:1], cum[:, 3, 2 * EXPERTS - 1:])
            v.tensor_scalar(n_jobs[:, 1:2], cum[:, 3, 2 * EXPERTS - 1:], -1.0, None, ALU.add).then_inc(routed, 1)
            steps.did(v.tensor_tensor(cmp[:, :, :], iota_f[:, 0:TABLE].unsqueeze(2).broadcast_to([P, TABLE, EXPERTS]),
                                      cum[:, 3, EXPERTS:].unsqueeze(1).broadcast_to([P, TABLE, EXPERTS]), ALU.is_ge))
            steps.settle()
            steps.did(v.tensor_reduce(jobf[:, 0, :], cmp[:, :, :], AX_X, ALU.add))
            steps.settle()
            steps.did(v.tensor_tensor(jobf[:, 1, 1:], jobf[:, 0, 1:], jobf[:, 0, 0:TABLE - 1], ALU.is_equal))
            steps.settle()
            v.tensor_copy(job_table[:, :, :], jobf[:, :, :]).then_inc(routed, 1)
            v.scalar_tensor_tensor(xs[:, 1, :], hacc[:, 1, :], srs[:, 1:2], gbc, ALU.mult, ALU.mult).then_inc(xs_ready, 1)
            frees(("pos",), v.memset(pgT, 0.0))
            dve.wait_ge(routed, 3)
            dve.wait_ge(comb_ready, 2)
            assert freed[0] == NU

            def select(e, part):
                for dst, src in ((psel, mask), (pgat, comb)):
                    for j in range(2):
                        v.tensor_scalar(dst[:, j, :], iota_f[:, bass.ds(part * P, P)], pos[:, j, bass.ds(e, 1)], src[:, j, bass.ds(e, 1)],
                                        ALU.is_equal, ALU.mult).then_inc(sel_ready, 1)

            select(0, 0)
            v.tensor_copy(lg[:, :, :], pos[:, :, 0:8]).then_inc(e_taken, 1)
            jobs = dve.value_load(n_jobs[0:1, 0:1], min_val=EXPERTS, max_val=MAX_JOBS)

            def add_results(job):
                for u in range(4):
                    dve.wait_ge(scattered, job * 4 + (u + 1))
                    h = hacc[:, u // 2, u % 2 * BANK:(u % 2 + 1) * BANK]
                    v.tensor_tensor(h, psum[4 + u][:, :], h, ALU.add).then_inc(added, 1)

            with dve.Fori(0, jobs) as job:
                split = [0]

                def low_parts(upto):
                    for b in range(split[0], min(upto + 1, EB)):
                        dve.wait_ge(hi_ready, job * EB + (b + 1))
                        v.tensor_tensor(w_lo[:, b % SPLIT, :], raw[:, b % RAW, :], w_hi[:, b % SPLIT, :].bitcast(F32),
                                        ALU.subtract).then_inc(lo_ready, 1)
                        split[0] = b + 1

                def unit_ready(n):
                    dve.wait_ge(e_full, job * EF + (n + 1))

                low_parts(0)
                for u in range(2):
                    wait_scalar(dve, job, A_X + u)
                    c = slice(u * BANK, (u + 1) * BANK)
                    v.tensor_tensor(xg_lo[:, c], psum[1 + u][:, :], xg_hi[:, c].bitcast(F32), ALU.subtract).then_inc(e_taken, 1)
                low_parts(3)
                add_results(job)
                unit_ready(F_PG)
                v.tensor_copy(pgT, psum[3][:, 0:SEQ]).then_inc(e_taken, 1)
                for i in range(FB + 1):
                    if i > 0:
                        low_parts(epos["g", i, 1] + 2 if i < FB else EB - 2)
                        wait_scalar(dve, job, A_TURN[i - 1])
                        v.tensor_tensor(act_lo[:, (i - 1) % 2, :], psum[3][:, :], act_hi[:, (i - 1) % 2, :].bitcast(F32), ALU.subtract).then_inc(e_taken, 1)
                    if i < FB:
                        end = epos["u", i, 1]
                        low_parts(end + 2)
                        wait_split_used(dve, job, end)
                        wait_scalar(dve, job, A_SILU[i])
                        v.tensor_tensor(ehid[:, :], psum[2][:, :], esilu[:, i % 2, :], ALU.mult).then_inc(e_taken, 1)
                low_parts(EB - 1)
                e = dve.value_load(job_table[0:1, 0, bass.ds(job + 1, 1)], min_val=0, max_val=EXPERTS)
                part = dve.value_load(job_table[0:1, 1, bass.ds(job + 1, 1)], min_val=0, max_val=1)
                select(e, part)
            add_results(jobs)


_INS = ["x", "meta", "norm_mix", "w_in", "b_in", "q_norm", "k_norm", "w_attn_o", "conv_w", "conv_b", "conv_ln_g",
        "conv_ln_b", "w_conv_o", "pool_w", "pool_scale", "w_pool_o", "w_out", "norm_ffn", "w_ff_gate", "w_ff_up",
        "w_ff_down", "w_router", "b_router", "w_e_gate", "w_e_up", "w_e_down"]


def kernel(**inputs):
    import concourse.bacc as bacc
    from concourse.bass_utils import run_bass_kernel_spmd

    nc = bacc.Bacc("TRN2", target_bir_lowering=False, num_devices=1)
    arrays, args = {}, []
    for name in _INS:
        a = np.ascontiguousarray(inputs[name])
        arrays[f"in_{name}"] = a
        args.append(nc.dram_tensor(f"in_{name}", a.shape, mybir.dt.from_np(a.dtype), kind="ExternalInput").ap())
    out = nc.dram_tensor("out_y", inputs["x"].shape, F32, kind="ExternalOutput").ap()
    trunk_program(nc, *args, out)
    r = run_bass_kernel_spmd(nc, [arrays], core_ids=[0])
    return r.results[0]["out_y"]
```
